# Optimizing a Trainium2 kernel written in Bass

```python
import math
import jax, jax.numpy as jnp
from jax import lax
import numpy as np

'''One inference step of a YOCO-style hybrid decoder: N_A Hawk/Griffin RG-LRU layers (self-decoder)
followed by N_B sliding-window GQA layers with per-head attention sinks and ALiBi (cross-decoder),
all of which read ONE shared K/V computed from the residual stream after the last RG-LRU layer.
Every layer is macaron: x += 1/2 SwiGLU(rms(x)); x += mixer(rms(x)); x += 1/2 SwiGLU(rms(x)).

Inputs:
  x_prompt       (BATCH, SEQ, D_MODEL)        new sequences, positions 0..SEQ-1
  x_sample       (DEC_BATCH, DEC_SEQ, D_MODEL) new tokens at positions PAST_LEN..PAST_LEN+DEC_SEQ-1
  state_rg_h     (N_A, DEC_BATCH, D_RNN)       RG-LRU hidden state per recurrent layer
  state_rg_conv  (N_A, DEC_BATCH, CONV_W-1, D_RNN) last CONV_W-1 conv inputs per recurrent layer
  cache_k/cache_v (DEC_BATCH, WIN_BUF, N_KV, HEAD_DIM) shared window K/V, WIN_BUF = min(WINDOW, PAST_LEN),
                 row i holds position PAST_LEN - WIN_BUF + i
  then all weights.
Returns (y_prompt (BATCH,SEQ,D_MODEL), y_sample (DEC_BATCH,DEC_SEQ,D_MODEL),
  prompt_rg_h (N_A,BATCH,D_RNN), prompt_rg_conv (N_A,BATCH,CONV_W-1,D_RNN),
  prompt_k, prompt_v (BATCH,min(WINDOW,SEQ),N_KV,HEAD_DIM),
  sample_rg_h (N_A,DEC_BATCH,D_RNN), sample_rg_conv (N_A,DEC_BATCH,CONV_W-1,D_RNN),
  sample_k, sample_v (DEC_BATCH,WIN_BUF,N_KV,HEAD_DIM)).
'''

D_MODEL = 1024
BATCH = 1
SEQ = 512
DEPTH = 2
DEC_BATCH = 8
DEC_SEQ = 8
PAST_LEN = 1024
PAGE_SIZE = 128

N_A = DEPTH // 2
N_B = DEPTH - N_A
D_RNN = D_MODEL
LRU_BW = 256
LRU_BLOCKS = D_RNN // LRU_BW
CONV_W = 4
LRU_C = 8.0
HEAD_DIM = 64
N_HEADS = D_MODEL // HEAD_DIM
N_KV = max(1, N_HEADS // 8)
GROUP = N_HEADS // N_KV
WINDOW = 128
D_FF = ((8 * D_MODEL // 3 + 127) // 128) * 128
EPS = 1e-6
NEG = -1e30

kernel_name = 'yoco_hawk_swa_sink_alibi_decoder'

def rms_norm(x, g):
    xf = x.astype(jnp.float32)
    y = xf * lax.rsqrt(jnp.mean(xf * xf, axis=-1, keepdims=True) + EPS)
    return (y * g.astype(jnp.float32)).astype(x.dtype)

def swiglu(x, w_gu, w_down):
    gu = x @ w_gu
    return (jax.nn.silu(gu[..., :D_FF]) * gu[..., D_FF:]) @ w_down

def alibi_slopes():
    return jnp.exp2(-8.0 * jnp.arange(1, N_HEADS + 1, dtype=jnp.float32) / N_HEADS)

def causal_conv(x, prefix, w, b):
    xe = jnp.concatenate([prefix.astype(x.dtype), x], axis=1)
    t = x.shape[1]
    y = b + sum(xe[:, k:k + t] * w[k] for k in range(CONV_W))
    return y, xe[:, xe.shape[1] - (CONV_W - 1):]

def block_diag(x, w, b):
    xb = x.reshape(x.shape[:-1] + (LRU_BLOCKS, LRU_BW))
    y = jnp.einsum('btnc,ncd->btnd', xb, w.astype(jnp.float32))
    return y.reshape(x.shape) + b.astype(jnp.float32)

def rg_lru(x, h0, w_a, b_a, w_x, b_x, lam):
    xf = x.astype(jnp.float32)
    r = jax.nn.sigmoid(block_diag(xf, w_a, b_a))
    i = jax.nn.sigmoid(block_diag(xf, w_x, b_x))
    log_a = -LRU_C * r * jax.nn.softplus(-lam.astype(jnp.float32))
    a = jnp.exp(log_a)
    u = jnp.sqrt(-jnp.expm1(2.0 * log_a)) * (i * xf)
    u = u.at[:, 0].add(a[:, 0] * h0.astype(jnp.float32))

    def combine(left, right):
        al, bl = left
        ar, br = right
        return al * ar, ar * bl + br

    _, h = lax.associative_scan(combine, (a, u), axis=1)
    return h, h[:, -1]

def recurrent_block(x, h0, buf0, w_in, conv_w, conv_b, w_a, b_a, w_x, b_x, lam, w_out):
    proj = x @ w_in
    gate, xr = proj[..., :D_RNN], proj[..., D_RNN:]
    xc, buf = causal_conv(xr, buf0, conv_w, conv_b)
    h, h_last = rg_lru(xc, h0, w_a, b_a, w_x, b_x, lam)
    y = (h.astype(x.dtype) * jax.nn.gelu(gate)) @ w_out
    return y, h_last.astype(x.dtype), buf

def window_attention(q, k, v, q_pos, k_pos, sinks):
    b, n, tq = q.shape[:3]
    qg = q.reshape(b, n, tq, N_KV, GROUP, HEAD_DIM)
    s = jnp.einsum('bnqkgd,bnskd->bnkgqs', qg, k).astype(jnp.float32) * (HEAD_DIM ** -0.5)
    diff = q_pos[:, :, None] - k_pos[:, None, :]
    valid = (diff >= 0) & (diff < WINDOW) & (k_pos[:, None, :] >= 0)
    slopes = alibi_slopes().reshape(N_KV, GROUP)
    bias = -slopes[None, :, :, None, None] * diff.astype(jnp.float32)[:, None, None]
    s = jnp.where(valid[:, None, None], s + bias, NEG)
    sink = sinks.astype(jnp.float32).reshape(N_KV, GROUP)[:, :, None, None]
    m = jnp.maximum(jnp.max(s, axis=-1, keepdims=True), sink)
    p = jnp.exp(s - m)
    p = p / (jnp.sum(p, axis=-1, keepdims=True) + jnp.exp(sink - m))
    o = jnp.einsum('bnkgqs,bnskd->bnqkgd', p.astype(v.dtype), v)
    return o.reshape(b, n, tq, N_HEADS * HEAD_DIM)

def prompt_window_attention(q, k, v, sinks):
    b, t = q.shape[:2]
    nb = t // WINDOW
    qb = q.reshape(b, nb, WINDOW, N_HEADS, HEAD_DIM)

    def band(z):
        zb = z.reshape(b, nb, WINDOW, N_KV, HEAD_DIM)
        prev = jnp.concatenate([jnp.zeros_like(zb[:, :1]), zb[:, :-1]], axis=1)
        return jnp.concatenate([prev, zb], axis=2)

    start = jnp.arange(nb, dtype=jnp.int32)[:, None] * WINDOW
    q_pos = start + jnp.arange(WINDOW, dtype=jnp.int32)[None]
    k_pos = start - WINDOW + jnp.arange(2 * WINDOW, dtype=jnp.int32)[None]
    o = window_attention(qb, band(k), band(v), q_pos, k_pos, sinks)
    return o.reshape(b, t, N_HEADS * HEAD_DIM)

def sample_window_attention(q, k_all, v_all, sinks):
    b, tq = q.shape[:2]
    tk = k_all.shape[1]
    q_pos = PAST_LEN + jnp.arange(tq, dtype=jnp.int32)
    k_pos = PAST_LEN + tq - tk + jnp.arange(tk, dtype=jnp.int32)
    o = window_attention(q.reshape(b, 1, tq, N_HEADS, HEAD_DIM), k_all[:, None], v_all[:, None],
                         q_pos[None], k_pos[None], sinks)
    return o.reshape(b, tq, N_HEADS * HEAD_DIM)

def trunk(x, rg_h0, rg_buf0, cache_k, cache_v, p):
    rg_h, rg_buf = [], []
    k_att = v_att = new_k = new_v = None
    for l in range(DEPTH):
        x = x + 0.5 * swiglu(rms_norm(x, p['ffn1_norm'][l]), p['ffn1_w_gu'][l], p['ffn1_w_down'][l])
        hn = rms_norm(x, p['mix_norm'][l])
        if l < N_A:
            y, hl, bl = recurrent_block(hn, rg_h0[l], rg_buf0[l], p['rg_w_in'][l], p['rg_conv_w'][l],
                                        p['rg_conv_b'][l], p['rg_w_a'][l], p['rg_b_a'][l], p['rg_w_x'][l],
                                        p['rg_b_x'][l], p['rg_lambda'][l], p['rg_w_out'][l])
            rg_h.append(hl)
            rg_buf.append(bl)
        else:
            j = l - N_A
            q = hn @ p['attn_w_q'][j]
            if cache_k is None:
                o = prompt_window_attention(q, k_att, v_att, p['attn_sinks'][j])
            else:
                o = sample_window_attention(q, k_att, v_att, p['attn_sinks'][j])
            y = o @ p['attn_w_o'][j]
        x = x + y
        x = x + 0.5 * swiglu(rms_norm(x, p['ffn2_norm'][l]), p['ffn2_w_gu'][l], p['ffn2_w_down'][l])
        if l == N_A - 1:
            b, t = x.shape[:2]
            kv = rms_norm(x, p['kv_norm']) @ p['w_kv']
            k = kv[..., :N_KV * HEAD_DIM].reshape(b, t, N_KV, HEAD_DIM)
            v = kv[..., N_KV * HEAD_DIM:].reshape(b, t, N_KV, HEAD_DIM)
            if cache_k is None:
                wb = min(WINDOW, t)
                k_att, v_att = k, v
            else:
                wb = cache_k.shape[1]
                k_att = jnp.concatenate([cache_k.astype(k.dtype), k], axis=1)
                v_att = jnp.concatenate([cache_v.astype(v.dtype), v], axis=1)
            new_k = k_att[:, k_att.shape[1] - wb:]
            new_v = v_att[:, v_att.shape[1] - wb:]
    y = rms_norm(x, p['final_norm'])
    return y, jnp.stack(rg_h), jnp.stack(rg_buf), new_k, new_v

def setup_inputs(seed: int = 0) -> dict:
    key = jax.random.key(seed)
    ks = iter(jax.random.split(key, 40))
    f32 = jnp.float32

    def nrm(shape, scale):
        return jax.random.normal(next(ks), shape, f32) * scale

    win_buf = min(WINDOW, PAST_LEN)
    a0 = jax.random.uniform(next(ks), (N_A, D_RNN), f32, 0.9, 0.999)
    s0 = a0 ** (1.0 / LRU_C)
    lam = jnp.log(s0) - jnp.log1p(-s0)
    return {
        'x_prompt': nrm((BATCH, SEQ, D_MODEL), 1.0),
        'x_sample': nrm((DEC_BATCH, DEC_SEQ, D_MODEL), 1.0),
        'state_rg_h': nrm((N_A, DEC_BATCH, D_RNN), 0.5),
        'state_rg_conv': nrm((N_A, DEC_BATCH, CONV_W - 1, D_RNN), 1.0),
        'cache_k': nrm((DEC_BATCH, win_buf, N_KV, HEAD_DIM), 1.0),
        'cache_v': nrm((DEC_BATCH, win_buf, N_KV, HEAD_DIM), 1.0),
        'ffn1_norm': 1.0 + nrm((DEPTH, D_MODEL), 0.01),
        'ffn1_w_gu': nrm((DEPTH, D_MODEL, 2 * D_FF), D_MODEL ** -0.5),
        'ffn1_w_down': nrm((DEPTH, D_FF, D_MODEL), D_FF ** -0.5),
        'mix_norm': 1.0 + nrm((DEPTH, D_MODEL), 0.01),
        'ffn2_norm': 1.0 + nrm((DEPTH, D_MODEL), 0.01),
        'ffn2_w_gu': nrm((DEPTH, D_MODEL, 2 * D_FF), D_MODEL ** -0.5),
        'ffn2_w_down': nrm((DEPTH, D_FF, D_MODEL), D_FF ** -0.5),
        'rg_w_in': nrm((N_A, D_MODEL, 2 * D_RNN), D_MODEL ** -0.5),
        'rg_conv_w': nrm((N_A, CONV_W, D_RNN), CONV_W ** -0.5),
        'rg_conv_b': nrm((N_A, D_RNN), 0.01),
        'rg_w_a': nrm((N_A, LRU_BLOCKS, LRU_BW, LRU_BW), LRU_BW ** -0.5),
        'rg_b_a': nrm((N_A, D_RNN), 0.01),
        'rg_w_x': nrm((N_A, LRU_BLOCKS, LRU_BW, LRU_BW), LRU_BW ** -0.5),
        'rg_b_x': nrm((N_A, D_RNN), 0.01),
        'rg_lambda': lam,
        'rg_w_out': nrm((N_A, D_RNN, D_MODEL), D_RNN ** -0.5),
        'kv_norm': 1.0 + nrm((D_MODEL,), 0.01),
        'w_kv': nrm((D_MODEL, 2 * N_KV * HEAD_DIM), D_MODEL ** -0.5),
        'attn_w_q': nrm((N_B, D_MODEL, N_HEADS * HEAD_DIM), D_MODEL ** -0.5),
        'attn_sinks': nrm((N_B, N_HEADS), 1.0),
        'attn_w_o': nrm((N_B, N_HEADS * HEAD_DIM, D_MODEL), (N_HEADS * HEAD_DIM) ** -0.5),
        'final_norm': 1.0 + nrm((D_MODEL,), 0.01),
    }

def reference(x_prompt, x_sample, state_rg_h, state_rg_conv, cache_k, cache_v,
              ffn1_norm, ffn1_w_gu, ffn1_w_down, mix_norm, ffn2_norm, ffn2_w_gu, ffn2_w_down,
              rg_w_in, rg_conv_w, rg_conv_b, rg_w_a, rg_b_a, rg_w_x, rg_b_x, rg_lambda, rg_w_out,
              kv_norm, w_kv, attn_w_q, attn_sinks, attn_w_o, final_norm):
    p = dict(ffn1_norm=ffn1_norm, ffn1_w_gu=ffn1_w_gu, ffn1_w_down=ffn1_w_down, mix_norm=mix_norm,
             ffn2_norm=ffn2_norm, ffn2_w_gu=ffn2_w_gu, ffn2_w_down=ffn2_w_down,
             rg_w_in=rg_w_in, rg_conv_w=rg_conv_w, rg_conv_b=rg_conv_b, rg_w_a=rg_w_a, rg_b_a=rg_b_a,
             rg_w_x=rg_w_x, rg_b_x=rg_b_x, rg_lambda=rg_lambda, rg_w_out=rg_w_out,
             kv_norm=kv_norm, w_kv=w_kv, attn_w_q=attn_w_q, attn_sinks=attn_sinks, attn_w_o=attn_w_o,
             final_norm=final_norm)
    b = x_prompt.shape[0]
    h0 = jnp.zeros((N_A, b, D_RNN), x_prompt.dtype)
    buf0 = jnp.zeros((N_A, b, CONV_W - 1, D_RNN), x_prompt.dtype)
    y_prompt, p_h, p_conv, p_k, p_v = trunk(x_prompt, h0, buf0, None, None, p)
    y_sample, s_h, s_conv, s_k, s_v = trunk(x_sample, state_rg_h, state_rg_conv, cache_k, cache_v, p)
    return (y_prompt, y_sample, p_h, p_conv, p_k, p_v, s_h, s_conv, s_k, s_v)


_drawn_inputs = setup_inputs


def setup_inputs(seed=0):
    import zlib

    import numpy as np

    out = dict(_drawn_inputs(seed))
    spreads = {}
    factors = {'ffn1_norm': 8.0,
     'mix_norm': 16.37,
     'ffn2_norm': 27.992,
     'rg_b_a': 40.622,
     'rg_b_x': 35.471,
     'kv_norm': 127.086,
     'final_norm': 200.0,
     'rg_conv_b': 4.651,
     'attn_sinks': 64.0}
    for name, (base, spread) in spreads.items():
        noise = np.random.default_rng([zlib.crc32(name.encode()), seed]).standard_normal(out[name].shape)
        drawn = base * np.exp(spread * noise) if base else spread * noise
        out[name] = __import__('jax').numpy.asarray(drawn.astype(out[name].dtype))
    for name, factor in factors.items():
        out[name] = (out[name] * factor).astype(out[name].dtype)
    return out
```

```python
from contextlib import ExitStack

import concourse.bass as bass
from concourse import mybir

F32 = mybir.dt.float32
F32R = mybir.dt.float32r
ALU = mybir.AluOpType
ACT = mybir.ActivationFunctionType
AX_X = mybir.AxisListType.X

P = 128
D_MODEL, SEQ, DEC_BATCH, DEC_SEQ = 1024, 512, 8, 8
NS = DEC_BATCH * DEC_SEQ
NT = SEQ + NS
KD = D_MODEL // P
FT = 22
HF = FT // 2
CONV_W = 4
HEAD_DIM, N_HEADS, N_KV = 64, 16, 2
WINDOW = 128
NBLK = SEQ // WINDOW
NKEY = WINDOW + NS
EPS = 1e-6

PRE = CONV_W - 1
SEG = PRE + DEC_SEQ
NE = PRE + SEQ + DEC_BATCH * SEG
NP = NE - PRE
S0 = SEQ + PRE
NSTATE = 1 + PRE + DEC_BATCH * (1 + PRE)

(V_F1A, V_F1B, V_MA, V_MB, V_F2A, V_F2B, V_KV, V_FIN,
 V_CW, V_CB, V_BA, V_BX, V_LAM, N_VEC) = (0, 1, 2, 3, 4, 5, 6, 7, 8, 12, 13, 14, 15, 16)

GU_JOBS, DN_JOBS = 2 * HF, KD
N_FFN = 2 * (GU_JOBS + DN_JOBS)


def plan():
    kt, act, base = [], [], {}

    def ffn(f):
        for half in range(2):
            base["gu", f, half] = len(kt)
            kt.extend([KD] * GU_JOBS)
            base["dn", f, half] = len(kt)
            kt.extend([HF] * DN_JOBS)

    ffn(0)
    base["rec"] = len(kt)
    for n in range(KD // 2):
        kt.extend([KD] * 4)
        act.extend(range(len(kt), len(kt) + 4))
        kt.extend([2] * 4)
    base["wout"] = len(kt)
    kt.extend([KD] * KD)
    ffn(1)
    base["kv"] = len(kt)
    kt.extend([KD] * 2)
    ffn(2)
    base["q"] = len(kt)
    kt.extend([KD] * KD)
    base["wo"] = len(kt)
    kt.extend([KD] * KD)
    ffn(3)
    return base, kt, act


def build(nc, A):
    base, KT, ACT_JOBS = plan()
    NJ = len(KT)
    act_jobs = set(ACT_JOBS)
    CH = HF * P

    with ExitStack() as ctx:
        def sb(name, shape, dt=F32):
            return ctx.enter_context(nc.sbuf_tensor(name, shape, dt))

        def sem(name):
            return ctx.enter_context(nc.semaphore(name))

        x = sb("x", [P, KD, NT])
        xs_hi = sb("xs_hi", [P, KD, NT], F32R)
        xs_lo = sb("xs_lo", [P, KD, NT], F32R)
        act_hi = sb("act_hi", [P, HF * NT], F32R)
        act_lo = sb("act_lo", [P, HF * NT], F32R)
        raw = sb("raw", [P, 4, CH])
        w_hi = sb("w_hi", [P, 2, CH], F32R)
        w_lo = sb("w_lo", [P, 2, CH], F32R)
        rstd = sb("rstd", [P, NT])
        ssum = sb("ssum", [P, NT])
        sq = sb("sq", [P, 2, NT])
        std = sq[:, 0, :]
        params = sb("params_sb", [P, N_VEC, KD])
        ones = sb("ones_sb", [P, P])
        ident = sb("ident_sb", [P, P])
        eps = sb("eps_sb", [P, 1])
        sinks = sb("sinks_sb", [P, N_HEADS + 1])
        AR = 12300
        arena = sb("arena", [P, AR])
        ps = ctx.enter_context(nc.psum_tensor("ps", [P, 8, 512], F32))

        at = [0]

        def take(n):
            v = arena[:, at[0]:at[0] + n]
            at[0] += n
            assert at[0] <= AR, at[0]
            return v

        gate_t = take(2 * NT).rearrange("p (a n) -> p a n", a=2)
        silu_t = take(2 * NT).rearrange("p (a n) -> p a n", a=2)
        up_t = take(2 * NT).rearrange("p (a n) -> p a n", a=2)
        hid = take(2 * NT).rearrange("p (a n) -> p a n", a=2)
        at[0] = 0
        xe = take(2 * NE).rearrange("p (a n) -> p a n", a=2)
        xc = take(2 * NP).rearrange("p (a n) -> p a n", a=2)
        rr = take(2 * NP).rearrange("p (a n) -> p a n", a=2)
        ii = take(2 * NP).rearrange("p (a n) -> p a n", a=2)
        tt = take(2 * NP).rearrange("p (a n) -> p a n", a=2)
        tmp = take(2 * NP).rearrange("p (a n) -> p a n", a=2)
        hh = take(2 * NP).rearrange("p (a n) -> p a n", a=2)
        gate = take(4 * NT).rearrange("p (a n) -> p a n", a=4)
        st_in = take(KD * DEC_BATCH * (1 + PRE)).rearrange("p (m s) -> p m s", m=KD)
        st_out = take(KD * NSTATE).rearrange("p (m s) -> p m s", m=KD)
        lam = take(8 * KD).rearrange("p (a m) -> p a m", a=8)
        decay = lam[:, 6, :]
        ndecay = lam[:, 7, :]
        at[0] = 8 * NT
        kdup = take(N_KV * NT).rearrange("p (g n) -> p g n", g=N_KV)
        v_tok = take((NBLK + 1) * P).rearrange("p (b n) -> p b n", b=NBLK + 1)
        v_t = take(NT)
        vkeep = at[0]
        at[0] = 0
        q_p = take(KD * SEQ).rearrange("p (m n) -> p m n", m=KD)
        q_s = take(8 * NS).rearrange("p (b n) -> p b n", b=DEC_BATCH)
        assert at[0] <= 8 * NT
        at[0] = vkeep - NT
        dist = take(2 * WINDOW)
        bias_c = take(WINDOW)
        bias_n = take(DEC_BATCH * NS).rearrange("p (b n) -> p b n", b=DEC_BATCH)
        kc = take(DEC_BATCH * WINDOW).rearrange("p (b n) -> p b n", b=DEC_BATCH)
        vc = take(DEC_BATCH * P).rearrange("p (b n) -> p b n", b=DEC_BATCH)
        small = take(64)
        prob_at = at[0]
        prob = take(4 * 256)
        pt_s = take(7 * P)
        pt = [pt_s, pt_s]
        s_s = q_p[:, 0:3, :].rearrange("p m n -> p (m n)").rearrange("p (b n) -> p b n", b=DEC_BATCH)
        ptc = q_p[:, 3:5, :].rearrange("p m n -> p (m n)").rearrange("p (b n) -> p b n", b=DEC_BATCH)
        ptn = q_p[:, 5:7, :].rearrange("p m n -> p (m n)").rearrange("p (b n) -> p b n", b=DEC_BATCH)
        neg_max, row_sum, sink_exp, inv_den = (small[:, 8 * i:8 * i + 8] for i in range(4))

        x_loaded = [sem(f"x_loaded{m}") for m in range(KD)]
        consts_loaded = sem("consts_loaded")
        misc_loaded = sem("misc_loaded")
        state_loaded = sem("state_loaded")
        att_loaded = sem("att_loaded")
        raw_landed = [sem(f"raw_landed{i}") for i in range(4)]
        stored = sem("stored")
        side_stored = sem("side_stored")
        hi_made = sem("hi_made")
        lo_made = sem("lo_made")
        job_done = sem("job_done")
        dve_evac = sem("dve_evac")
        act_evac = sem("act_evac")
        xs_hi_made = sem("xs_hi_made")
        xs_ready = sem("xs_ready")
        sq_made = sem("sq_made")
        ss_added = sem("ss_added")
        stat_sum = sem("stat_sum")
        std_made = sem("std_made")
        rstd_made = sem("rstd_made")
        silu_made = sem("silu_made")
        hid_made = sem("hid_made")
        hid_hi_made = sem("hid_hi_made")
        hid_ready = sem("hid_ready")
        dve_chain = sem("dve_chain")
        pool_chain = sem("pool_chain")
        lam_exp = sem("lam_exp")
        lam_abs = sem("lam_abs")
        xc_made = sem("xc_made")
        xc_hi_made = sem("xc_hi_made")
        xc_ready = sem("xc_ready")
        conv_saved = sem("conv_saved")
        gate_out = sem("gate_out")
        ix_made = sem("ix_made")
        decay_ready = sem("decay_ready")
        tanh_made = sem("tanh_made")
        a_made = sem("a_made")
        m2_made = sem("m2_made")
        mult_made = sem("mult_made")
        h_made = sem("h_made")
        h_saved = sem("h_saved")
        y_made = sem("y_made")
        y_hi_made = sem("y_hi_made")
        y_ready = sem("y_ready")
        v_turned = sem("v_turned")
        v_tok_made = sem("v_tok_made")
        scores_done = sem("scores_done")
        max_made = sem("max_made")
        exp_made = sem("exp_made")
        inv_made = sem("inv_made")
        prob_ready = sem("prob_ready")
        prob_turned = sem("prob_turned")
        pt_ready = sem("pt_ready")
        pv_done = sem("pv_done")
        o_hi_made = sem("o_hi_made")
        att_ready = sem("att_ready")
        y_out = sem("y_out")

        GAIN = [V_F1A, V_MA, V_F2A, V_KV, V_F1B, V_MB, V_F2B]
        FFN_INPUT = [0, 2, 4, 6]
        dve_done = [0]
        for j in range(NJ):
            dve_done.append(dve_done[-1] + (j not in act_jobs))

        def evac(j):
            return dve_done[j + 1]

        def slot_free(pe, j):
            if j < 2:
                return
            if j - 2 in act_jobs:
                pe.wait_ge(act_evac, j - 1 - dve_done[j - 1])
            else:
                pe.wait_ge(dve_evac, dve_done[j - 1])

        def wv(s, r, k):
            return s[:, r, k * P:(k + 1) * P]

        def act_tile(a, k):
            return a[:, k * NT:(k + 1) * NT]

        def halves(ap, at_, w):
            return ap[:, at_:at_ + w]

        EVEN = ((0, 288), (288, 288))
        BLOCKS = ((0, 256), (256, 320))
        PADDED = ((0, NP // 2), (NP // 2, NP // 2))

        def ps2(slot, n=288):
            return ps[:, 2 * slot:2 * slot + 2, 0:n]

        def two(ap, n=2):
            return ap.rearrange("p (a n) -> p a n", a=n)

        def seg(ap, first, n):
            return ap[:, S0:S0 + DEC_BATCH * SEG].rearrange(
                "p (b s) -> p b s", b=DEC_BATCH)[:, :, first:first + n]

        block = ctx.enter_context(nc.Block())

        def load(sp, slot, src, kt):
            sp.dma_start(raw[:, slot, 0:kt * P], src).then_inc(raw_landed[slot], 16)

        @block.sync
        def _(sp):
            for m in range(KD):
                sp.dma_start(x[:, m, :], A["xT"][m]).then_inc(x_loaded[m], 16)
                if m == 0:
                    sp.dma_start(params[:, :, :], A["params"]).then_inc(consts_loaded, 16)
                    sp.dma_start(ones[:, :], A["ones"]).then_inc(consts_loaded, 16)
                    sp.dma_start(eps[:, :], A["eps"]).then_inc(consts_loaded, 16)
                    load(sp, 0, A["w_gu"][0], KD)

            def free(c):
                sp.wait_ge(lo_made, c - 3)

            def stream(first, src, n, kt, row0):
                lead = 0
                while first + lead < 4:
                    if first + lead > 0:
                        load(sp, (first + lead) % 4, src[row0 + lead], kt)
                    lead += 1
                turns = (n - lead) // 4
                if turns:
                    with sp.Fori(0, turns) as i:
                        for k in range(4):
                            c = lead + 4 * i + k
                            sp.wait_ge(lo_made, first + c - 3)
                            load(sp, (first + lead + k) % 4,
                                 src[bass.ds(row0 + c, 1)].rearrange("a p n -> p (a n)"), kt)
                for c in range(lead + 4 * turns, n):
                    free(first + c)
                    load(sp, (first + c) % 4, src[row0 + c], kt)

            def ffn(f):
                for half in range(2):
                    stream(base["gu", f, half], A["w_gu"], GU_JOBS, KD, (2 * f + half) * GU_JOBS)
                    stream(base["dn", f, half], A["w_dn"], DN_JOBS, HF, (2 * f + half) * DN_JOBS)

            ffn(0)
            for n in range(KD // 2):
                stream(base["rec"] + 8 * n, A["w_in"], 4, KD, 4 * n)
                stream(base["rec"] + 8 * n + 4, A["w_ax"], 4, 2, 4 * n)
            stream(base["wout"], A["w_out"], KD, KD, 0)
            ffn(1)
            stream(base["kv"], A["w_kv"], 2, KD, 0)
            ffn(2)
            stream(base["q"], A["w_q"], KD, KD, 0)
            stream(base["wo"], A["w_o"], KD, KD, 0)
            ffn(3)
            for m in range(KD):
                sp.wait_ge(y_out, m + 1)
                sp.dma_start(A["yT"][m], x[:, m, :]).then_inc(stored, 16)
            sp.wait_ge(stored, 16 * KD)
            sp.wait_ge(side_stored, 16 * 6)

        @block.tensor
        def _(pe):
            def mm_k(slot, w, k, hi, lo, cut, first, last, kw=None):
                kw = k if kw is None else kw
                passes = ((w_hi, hi), (w_hi, lo), (w_lo, hi))
                for n, (a, b) in enumerate(passes):
                    for c, (o, width) in enumerate(cut):
                        ins = nc.tensor.matmul(ps[:, 2 * slot + c, 0:width], wv(a, w, kw), halves(b, o, width),
                                               start=first and n == 0, stop=last and n == 2)
                return ins

            def job(j, par, kt, operand, cut=EVEN, ready=None):
                pe.wait_ge(lo_made, j + 1)
                for k in range(kt):
                    if ready:
                        pe.wait_ge(*ready(k))
                    hi, lo = operand(k)
                    ins = mm_k(par, par, k, hi, lo, cut, k == 0, k == kt - 1)
                ins.then_inc(job_done, 1)

            def xs_tile(k):
                return xs_hi[:, k, :], xs_lo[:, k, :]

            def hid_tile(k):
                return act_tile(act_hi, k), act_tile(act_lo, k)

            def stats(s):
                pe.wait_ge(ss_added, (KD - 1) * (s + 1))
                if s == 0:
                    pe.wait_ge(consts_loaded, 48)
                for c, (o, width) in enumerate(EVEN):
                    ins = nc.tensor.matmul(ps[:, 4 + c, 0:width], ones[:, :], ssum[:, o:o + width],
                                           start=True, stop=True)
                ins.then_inc(stat_sum, 1)

            def ffn(f, stat):
                s = FFN_INPUT[f]
                for half in range(2):
                    j0 = base["gu", f, half]
                    for j in (j0, j0 + 1):
                        slot_free(pe, j)
                        job(j, j % 2, KD, xs_tile,
                            ready=(lambda k: (xs_ready, KD * s + k + 1)) if j == j0 and half == 0 else None)
                        if j == j0 and half == 0 and stat is not None:
                            stats(stat)
                    with pe.Fori(0, (GU_JOBS - 2) // 4) as i:
                        for k in range(4):
                            j = 4 * i + (j0 + 2 + k)
                            pe.wait_ge(dve_evac, 4 * i + dve_done[j0 + 1 + k])
                            job(j, (j0 + k) % 2, KD, xs_tile)
                    j0 = base["dn", f, half]
                    u0 = FT * f + HF * half
                    with pe.Fori(0, DN_JOBS // 2) as i:
                        for k in range(2):
                            j = 2 * i + (j0 + k)
                            pe.wait_ge(dve_evac, 2 * i + dve_done[j0 + k - 1])
                            job(j, (j0 + k) % 2, HF, hid_tile,
                                ready=(lambda t: (hid_ready, u0 + t + 1)) if k == 0 else None)

            def recurrent():
                def conv_tile(k):
                    o = KD * NT
                    return act_hi[:, o + k * NP:o + (k + 1) * NP], act_lo[:, o + k * NP:o + (k + 1) * NP]

                for n in range(KD // 2):
                    for r in range(4):
                        j = base["rec"] + 8 * n + r
                        slot_free(pe, j)
                        job(j, j % 2, KD, xs_tile, cut=BLOCKS if r < 2 else EVEN,
                            ready=(lambda k: (xs_ready, KD + k + 1)) if n == r == 0 else None)
                        if n == r == 0:
                            stats(1)
                    for r in range(4):
                        j = base["rec"] + 8 * n + 4 + r
                        slot_free(pe, j)
                        pe.wait_ge(xc_ready, 2 * n + 2)
                        job(j, j % 2, 2, conv_tile, cut=PADDED)

            def out_product(j0, ready):
                for m in range(KD):
                    slot_free(pe, j0 + m)
                    job(j0 + m, (j0 + m) % 2, KD, hid_tile, ready=ready if m == 0 else None)

            def key_value():
                j = base["kv"]
                slot_free(pe, j)
                job(j, j % 2, KD, xs_tile, ready=lambda k: (xs_ready, 3 * KD + k + 1))
                stats(3)
                slot_free(pe, j + 1)
                job(j + 1, (j + 1) % 2, KD, xs_tile)

            def turn_values():
                pe.wait_ge(dve_evac, evac(base["kv"] + 1))
                pe.wait_ge(misc_loaded, 32)
                for b in range(NBLK):
                    nc.tensor.transpose(ps[:, 6, b * P:(b + 1) * P], v_t[:, b * P:(b + 1) * P], ident[:, :])
                nc.tensor.transpose(ps[0:NS, 7, 0:P], v_t[:, SEQ:NT], ident[:, :]).then_inc(v_turned, 1)

            def attention():
                j0 = base["q"]
                for m in range(KD):
                    slot_free(pe, j0 + m)
                    job(j0 + m, (j0 + m) % 2, KD, xs_tile, cut=BLOCKS,
                        ready=(lambda k: (xs_ready, 5 * KD + k + 1)) if m == 0 else None)
                    if m == 0:
                        stats(4)

                def scores(h):
                    m, p, g = h // 2, 64 * (h % 2), h // 8
                    b0 = 4 if h % 2 == 0 else 0
                    if h >= 2:
                        pe.wait_ge(exp_made, h - 1)
                    for b in range(NBLK):
                        q = q_p[p:p + 64, m, b * P:(b + 1) * P]
                        lo, hi = (b - 1) * P, (b + 1) * P
                        if b == 0:
                            lo = 0
                        c = (b % 2) * 256 + (0 if b else P)
                        ins = nc.tensor.matmul(ps[:, b0 + b // 2, c:c + hi - lo], q, kdup[p:p + 64, g, lo:hi],
                                               start=True, stop=True)
                    ins.then_inc(scores_done, 1)

                def turn(h):
                    pe.wait_ge(prob_ready, h + 1)
                    if h >= 1:
                        pe.wait_ge(pt_ready, h)
                    for t in range(7):
                        ins = nc.tensor.transpose(ps[:, 6 + t // 4, (t % 4) * P:(t % 4 + 1) * P],
                                                  prob[:, (t + 1) * P:(t + 2) * P], ident[:, :])
                    ins.then_inc(prob_turned, 1)

                def values(h):
                    m, p, g = h // 2, 64 * (h % 2), h // 8
                    pe.wait_ge(pt_ready, h + 1)
                    if h % 2 == 0 and m >= 2:
                        pe.wait_ge(att_ready, m - 1)
                    for b in range(NBLK):
                        for t in ([0] if b == 0 else [2 * b - 1, 2 * b]):
                            kb = b if t == 2 * b else b - 1
                            ins = nc.tensor.matmul(ps[p:p + 64, 2 + m % 2, b * P:(b + 1) * P],
                                                   v_tok[:, kb, 64 * g:64 * g + 64],
                                                   pt[h % 2][:, t * P:(t + 1) * P],
                                                   start=t in (0, 2 * b - 1), stop=t == 2 * b)
                    ins.then_inc(pv_done, 1)

                pe.wait_ge(dve_evac, dve_done[j0 + KD])
                pe.wait_ge(std_made, 5)
                pe.wait_ge(v_tok_made, 1)
                scores(0)
                scores(1)
                for h in range(N_HEADS + 1):
                    if h < N_HEADS:
                        turn(h)
                    if h >= 1:
                        values(h - 1)
                    if h + 2 < N_HEADS:
                        scores(h + 2)

                pe.wait_ge(exp_made, N_HEADS)
                pe.wait_ge(pt_ready, N_HEADS)
                pe.wait_ge(att_ready, KD)
                pe.wait_ge(att_loaded, 16 * 5)
                for g in range(N_KV):
                    r = slice(64 * g, 64 * g + 64)
                    for b in range(DEC_BATCH):
                        bank, c = (4 - 4 * g) + b // 2, (b % 2) * NKEY
                        q = q_s[r, b, :]
                        nc.tensor.matmul(ps[r, bank, c:c + WINDOW], q, kc[r, b, :], start=True, stop=True)
                        ins = nc.tensor.matmul(ps[r, bank, c + WINDOW:c + NKEY], q, kdup[r, g, SEQ:NT],
                                               start=True, stop=True)
                ins.then_inc(scores_done, 1)
                pe.wait_ge(prob_ready, N_HEADS + 1)
                for b in range(DEC_BATCH):
                    c = (b % 4) * P
                    nc.tensor.transpose(ps[:, 4 + b // 4, c:c + P], s_s[:, b, 0:WINDOW], ident[:, :])
                    ins = nc.tensor.transpose(ps[0:NS, 6 + b // 4, c:c + P], s_s[:, b, WINDOW:NKEY], ident[:, :])
                ins.then_inc(prob_turned, 1)
                pe.wait_ge(pt_ready, N_HEADS + 1)
                for b in range(DEC_BATCH):
                    for h2 in range(2):
                        for g in range(N_KV):
                            out = ps[64 * h2:64 * h2 + 64, 0, 64 * b + 32 * g:64 * b + 32 * g + 32]
                            rows = lambda a: a[:, b, 64 * g:64 * g + 64].rearrange(
                                "p (m h t) -> p h m t", m=4, h=2)[:, h2]
                            nc.tensor.matmul(out, vc[:, b, 64 * g:64 * g + 64], rows(ptc), start=True, stop=False)
                            ins = nc.tensor.matmul(out, v_tok[0:NS, NBLK, 64 * g:64 * g + 64], rows(ptn[0:NS]),
                                                   start=False, stop=True)
                ins.then_inc(pv_done, 1)

            ffn(0, 0)
            recurrent()
            out_product(base["wout"], lambda k: (y_ready, k + 1))
            ffn(1, 2)
            key_value()
            turn_values()
            ffn(2, None)
            attention()
            pe.wait_ge(att_ready, KD + 1)
            out_product(base["wo"], None)
            ffn(3, 5)
            stats(6)

        @block.scalar
        def _(act):
            def prep(c, slot, par, kt, landed, used=None):
                act.wait_ge(raw_landed[slot], landed)
                if used is not None:
                    act.wait_ge(job_done, used)
                nc.scalar.activation(w_hi[:, par, 0:kt * P], raw[:, slot, 0:kt * P],
                                     ACT.Copy).then_inc(hi_made, 1)

            def prep_next(j):
                c = j + 2
                if c < NJ:
                    prep(c, c % 4, c % 2, KT[c], 16 * (c // 4 + 1), used=j + 1)

            def split_x(s, m, stat, x_job):
                if x_job is None:
                    act.wait_ge(x_loaded[m], 16)
                else:
                    act.wait_ge(dve_evac, evac(x_job))
                if s is not None:
                    nc.scalar.activation(xs_hi[:, m, :], x[:, m, :], ACT.Copy,
                                         scale=params[:, GAIN[s], m:m + 1]).then_inc(xs_hi_made, 1)
                if stat is not None:
                    if m >= 3:
                        act.wait_ge(ss_added, (KD - 1) * stat + m - 2)
                    nc.scalar.activation(ssum[:, :] if m == 0 else sq[:, m % 2, :], x[:, m, :],
                                         ACT.Square).then_inc(sq_made, 1)

            def root(stat):
                act.wait_ge(stat_sum, stat + 1)
                nc.scalar.activation(two(std), ps[:, 4:6, 0:288], ACT.Sqrt, bias=eps[:, 0:1],
                                     scale=1.0 / D_MODEL).then_inc(std_made, 1)

            def down(j0, s, stat):
                for m in range(KD):
                    prep_next(j0 + m)
                    if s is not None or stat is not None:
                        split_x(s, m, stat, j0 + m)

            def ffn(f, s, stat):
                for half in range(2):
                    j0 = base["gu", f, half]
                    u0 = FT * f + HF * half
                    turns = (GU_JOBS - 2) // 4

                    def unit(k, i, prep_a, prep_b):
                        u = 2 * i + (u0 + k)
                        par = k % 2
                        prep_a()
                        act.wait_ge(dve_evac, 4 * i + evac(j0 + 2 * k))
                        nc.scalar.activation(silu_t[:, par, :], gate_t[:, par, :], ACT.Silu).then_inc(silu_made, 1)
                        prep_b()
                        act.wait_ge(hid_made, u + 1)
                        nc.scalar.activation(act_hi[:, bass.ds((2 * i + k) * NT, NT)], hid[:, par, :],
                                             ACT.Copy).then_inc(hid_hi_made, 1)

                    with act.Fori(0, turns) as i:
                        def look(k):
                            c = j0 + k + 2
                            return lambda: prep(4 * i + c, c % 4, c % 2, KD, 64 * 0 + 16 * i + 16 * (c // 4 + 1),
                                                used=4 * i + (j0 + k + 1))
                        for k in range(2):
                            unit(k, i, look(2 * k), look(2 * k + 1))
                    for v in range(2 * turns, HF):
                        unit_static(j0 + 2 * v, u0 + v, v)
                    down(base["dn", f, half], s if half else None, stat if half else None)

            def unit_static(j, u, v):
                par = v % 2
                prep_next(j)
                act.wait_ge(dve_evac, evac(j))
                nc.scalar.activation(silu_t[:, par, :], gate_t[:, par, :], ACT.Silu).then_inc(silu_made, 1)
                prep_next(j + 1)
                act.wait_ge(hid_made, u + 1)
                nc.scalar.activation(act_hi[:, v * NT:(v + 1) * NT], hid[:, par, :],
                                     ACT.Copy).then_inc(hid_hi_made, 1)

            def recurrent():
                act.wait_ge(lam_abs, 1)
                nc.scalar.activation(lam[:, 1, :], lam[:, 0, :], ACT.Exp, scale=-1.0).then_inc(lam_exp, 1)
                j0 = base["rec"]
                o = KD * NT

                def round_conv(m):
                    act.wait_ge(xc_made, m + 1)
                    nc.scalar.activation(act_hi[:, o + (m % 2) * NP:o + (m % 2 + 1) * NP], xc[:, m % 2, :],
                                         ACT.Copy).then_inc(xc_hi_made, 1)

                def multiplier(m):
                    act.wait_ge(m2_made, m + 1)
                    nc.scalar.activation(tt[:, m % 2, :], tt[:, m % 2, :], ACT.Sqrt).then_inc(mult_made, 1)

                def gelu(m):
                    act.wait_ge(dve_evac, evac(j0 + 8 * (m // 2) + 2 + m % 2))
                    nc.scalar.activation(gate[:, m % 4, :], gate[:, m % 4, :], ACT.Gelu_apprx_tanh).then_inc(gate_out, 1)

                def round_y(m):
                    act.wait_ge(y_made, m + 1)
                    nc.scalar.activation(act_tile(act_hi, m), tmp[:, m % 2, 0:NT], ACT.Copy).then_inc(y_hi_made, 1)

                for n in range(KD // 2 + 1):
                    j = j0 + 8 * n
                    more = n < KD // 2
                    if more:
                        prep_next(j)
                    if n:
                        multiplier(2 * n - 2)
                        multiplier(2 * n - 1)
                    if more:
                        round_conv(2 * n)
                        prep_next(j + 1)
                        round_conv(2 * n + 1)
                    if n:
                        gelu(2 * n - 2)
                        gelu(2 * n - 1)
                    if more:
                        prep_next(j + 2)
                    if n:
                        round_y(2 * n - 2)
                    if more:
                        prep_next(j + 3)
                    if n:
                        round_y(2 * n - 1)
                    if more:
                        for t in range(2):
                            m = 2 * n + t
                            for q, (dst, vec) in enumerate(((rr, V_BA), (ii, V_BX))):
                                jj = j + 4 + 2 * t + q
                                prep_next(jj)
                                act.wait_ge(job_done, jj + 1)
                                if m >= 2:
                                    act.wait_ge(h_made, m - 1)
                                nc.scalar.activation(two(dst[:, m % 2, :]), ps2(jj % 2, NP // 2), ACT.Sigmoid,
                                                     bias=params[:, vec, m:m + 1]).then_inc(act_evac, 1)
                        act.wait_ge(decay_ready, 1)
                        act.wait_ge(act_evac, 4 * n + 4)
                        for m in (2 * n, 2 * n + 1):
                            nc.scalar.activation(tt[:, m % 2, :], rr[:, m % 2, :], ACT.Tanh,
                                                 scale=ndecay[:, m:m + 1]).then_inc(tanh_made, 1)
                        act.wait_ge(tanh_made, 2 * n + 2)
                        for m in (2 * n, 2 * n + 1):
                            nc.scalar.activation(rr[:, m % 2, :], rr[:, m % 2, :], ACT.Exp,
                                                 scale=decay[:, m:m + 1]).then_inc(a_made, 1)

            def attention():
                act.wait_ge(misc_loaded, 32)
                for h in range(N_HEADS + 1):
                    if h < N_HEADS:
                        b0 = 4 if h % 2 == 0 else 0
                        o = 4 * (h % 2)
                        sp_ = ps[:, b0:b0 + 2, :].rearrange("p a n -> p (a n)")
                        act.wait_ge(max_made, h + 1)
                        nc.scalar.activation(sink_exp[:, o:o + 4], neg_max[:, o:o + 4], ACT.Exp,
                                             bias=sinks[:, h:h + 1])
                        if h >= 1:
                            act.wait_ge(prob_turned, h)
                        for b in range(NBLK):
                            lo = 256 * b + (0 if b else P)
                            hi = 256 * (b + 1)
                            ins = nc.scalar.activation(prob[:, lo:hi], sp_[:, lo:hi], ACT.Exp,
                                                       bias=neg_max[:, o + b:o + b + 1],
                                                       accum_out=row_sum[:, o + b:o + b + 1])
                        ins.then_inc(exp_made, 1)
                    if h >= 1:
                        q = h - 1
                        act.wait_ge(prob_turned, q + 1)
                        if q >= 1:
                            act.wait_ge(pv_done, q)
                        nc.scalar.activation(pt[q % 2][:, 0:512], ps[:, 6, :], ACT.Copy)
                        nc.scalar.activation(pt[q % 2][:, 512:7 * P], ps[:, 7, 0:3 * P], ACT.Copy).then_inc(pt_ready, 1)
                    if h >= 3 and h % 2 == 1:
                        round_o((h - 3) // 2)
                round_o(KD - 1)
                act.wait_ge(max_made, N_HEADS + 1)
                nc.scalar.activation(sink_exp[:, 0:8], neg_max[:, 0:8], ACT.Exp, bias=sinks[:, N_HEADS:N_HEADS + 1])
                for b in range(DEC_BATCH):
                    ins = nc.scalar.activation(s_s[:, b, :], s_s[:, b, :], ACT.Exp, bias=neg_max[:, b:b + 1],
                                               accum_out=row_sum[:, b:b + 1])
                ins.then_inc(exp_made, 1)
                act.wait_ge(prob_turned, N_HEADS + 1)
                nc.scalar.activation(ptc[:, :, :].rearrange("p (a b) n -> p a (b n)", a=2), ps[:, 4:6, :], ACT.Copy)
                nc.scalar.activation(ptn[0:NS, :, :].rearrange("p (a b) n -> p a (b n)", a=2), ps[0:NS, 6:8, :],
                                     ACT.Copy).then_inc(pt_ready, 1)
                act.wait_ge(pv_done, N_HEADS + 1)
                for m in range(KD):
                    ins = nc.scalar.activation(
                        act_hi[:, m * NT + SEQ:(m + 1) * NT].rearrange("p (b t) -> p b t", t=DEC_SEQ),
                        ps[:, 0, :].rearrange("p (b m t) -> p m b t", b=DEC_BATCH, m=KD)[:, m], ACT.Copy)
                ins.then_inc(o_hi_made, 1)

            def round_o(m):
                act.wait_ge(pv_done, 2 * m + 2)
                nc.scalar.activation(act_hi[:, m * NT:m * NT + SEQ], ps[:, 2 + m % 2, :], ACT.Copy).then_inc(o_hi_made, 1)

            prep(0, 0, 0, KT[0], 16)
            act.wait_ge(consts_loaded, 48)
            for m in range(KD):
                split_x(0, m, 0, None)
            prep(1, 1, 1, KT[1], 16)
            root(0)
            ffn(0, 1, 1)
            root(1)
            recurrent()
            down(base["wout"], 2, 2)
            root(2)
            ffn(1, 3, 3)
            root(3)
            j = base["kv"]
            prep_next(j)
            prep_next(j + 1)
            for m in range(KD):
                split_x(4, m, None, j - 1)
            ffn(2, 5, 4)
            root(4)
            for m in range(KD):
                prep_next(base["q"] + m)
            attention()
            down(base["wo"], 6, 5)
            root(5)
            ffn(3, None, 6)
            root(6)

        @block.vector
        def _(dve):
            chain = [0]

            def own(ins):
                chain[0] += 1
                ins.then_inc(dve_chain, 1)
                dve.wait_ge(dve_chain, chain[0])

            def prep(c, slot, par, kt):
                dve.wait_ge(hi_made, c + 1)
                nc.vector.tensor_tensor(w_lo[:, par, 0:kt * P], raw[:, slot, 0:kt * P],
                                        w_hi[:, par, 0:kt * P].bitcast(F32), ALU.subtract).then_inc(lo_made, 1)

            def prep_next(j):
                c = j + 2
                if c < NJ:
                    prep(c, c % 4, c % 2, KT[c])

            def split_x(s, m, stat):
                if s is not None:
                    dve.wait_ge(xs_hi_made, KD * s + m + 1)
                    nc.vector.scalar_tensor_tensor(xs_lo[:, m, :], x[:, m, :], params[:, GAIN[s], m:m + 1],
                                                   xs_hi[:, m, :].bitcast(F32), ALU.mult,
                                                   ALU.subtract).then_inc(xs_ready, 1)
                if stat is not None:
                    dve.wait_ge(sq_made, KD * stat + m + 1)
                    if m >= 2:
                        dve.wait_ge(ss_added, (KD - 1) * stat + m - 1)
                    if m >= 1:
                        nc.vector.tensor_tensor(ssum[:, :], ssum[:, :], sq[:, m % 2, :], ALU.add).then_inc(ss_added, 1)

            def invert(stat):
                dve.wait_ge(std_made, stat + 1)
                nc.vector.reciprocal(rstd[:, :], std).then_inc(rstd_made, 1)
                dve.wait_ge(rstd_made, stat + 1)

            def down(j0, s, stat, factor):
                for m in range(KD):
                    dve.wait_ge(job_done, j0 + m + 1)
                    dve.wait_ge(dve_evac, evac(j0 + m - 1))
                    nc.vector.scalar_tensor_tensor(two(x[:, m, :]), ps2((j0 + m) % 2), factor, two(x[:, m, :]),
                                                   ALU.mult, ALU.add).then_inc(dve_evac, 1)
                    prep_next(j0 + m)
                    split_x(s, m, stat)

            def ffn(f, s, stat):
                for half in range(2):
                    j0 = base["gu", f, half]
                    u0 = FT * f + HF * half
                    turns = (GU_JOBS - 2) // 4

                    def unit(j, u, up_evac, par, slot, tile_at, prep_a, prep_b):
                        dve.wait_ge(job_done, j + 1)
                        nc.vector.tensor_tensor(two(gate_t[:, par, :]), ps2(slot), two(rstd[:, :]),
                                                ALU.mult).then_inc(dve_evac, 1)
                        prep_a()
                        dve.wait_ge(job_done, j + 2)
                        nc.vector.tensor_tensor(two(up_t[:, par, :]), ps2(1 - slot), two(rstd[:, :]),
                                                ALU.mult).then_inc(dve_evac, 1)
                        dve.wait_ge(dve_evac, up_evac)
                        dve.wait_ge(silu_made, u + 1)
                        nc.vector.tensor_tensor(hid[:, par, :], up_t[:, par, :], silu_t[:, par, :],
                                                ALU.mult).then_inc(hid_made, 1)
                        prep_b()
                        dve.wait_ge(hid_hi_made, u + 1)
                        nc.vector.tensor_tensor(act_lo[:, tile_at], hid[:, par, :], act_hi[:, tile_at].bitcast(F32),
                                                ALU.subtract).then_inc(hid_ready, 1)

                    with dve.Fori(0, turns) as i:
                        for k in range(2):
                            ca, cb = j0 + 2 * k + 2, j0 + 2 * k + 3
                            unit(4 * i + (j0 + 2 * k), 2 * i + (u0 + k), 4 * i + evac(j0 + 2 * k + 1), k, j0 % 2,
                                 bass.ds((2 * i + k) * NT, NT),
                                 lambda: prep(4 * i + ca, ca % 4, ca % 2, KD),
                                 lambda: prep(4 * i + cb, cb % 4, cb % 2, KD))
                    for v in range(2 * turns, HF):
                        j = j0 + 2 * v
                        unit(j, u0 + v, evac(j + 1), v % 2, j0 % 2, slice(v * NT, (v + 1) * NT),
                             lambda: prep_next(j), lambda: prep_next(j + 1))
                    down(base["dn", f, half], s if half else None, stat if half else None, 0.5)

            def lru_constants():
                v = params[:, V_LAM, :]
                nc.vector.scalar_tensor_tensor(lam[:, 0, :], v, -1.0, v, ALU.mult, ALU.max).then_inc(lam_abs, 1)
                dve.wait_ge(lam_exp, 1)
                own(nc.vector.tensor_scalar(lam[:, 2, :], lam[:, 1, :], 2.0, None, ALU.add))
                own(nc.vector.reciprocal(lam[:, 3, :], lam[:, 2, :]))
                own(nc.vector.tensor_tensor(lam[:, 2, :], lam[:, 1, :], lam[:, 3, :], ALU.mult))
                own(nc.vector.tensor_tensor(lam[:, 3, :], lam[:, 2, :], lam[:, 2, :], ALU.mult))
                own(nc.vector.tensor_scalar(lam[:, 4, :], lam[:, 3, :], 1.0 / 17, None, ALU.mult))
                for k in range(7, 0, -1):
                    own(nc.vector.scalar_tensor_tensor(lam[:, 4, :], lam[:, 4, :], 1.0 / (2 * k + 1), lam[:, 3, :],
                                                       ALU.add, ALU.mult))
                own(nc.vector.scalar_tensor_tensor(lam[:, 5, :], lam[:, 4, :], 1.0, lam[:, 2, :], ALU.add, ALU.mult))
                own(nc.vector.tensor_scalar(lam[:, 4, :], v, -1.0, 0.0, ALU.mult, ALU.max))
                own(nc.vector.scalar_tensor_tensor(lam[:, 3, :], lam[:, 5, :], 2.0, lam[:, 4, :], ALU.mult, ALU.add))
                nc.vector.tensor_scalar(decay, lam[:, 3, :], -8.0, None, ALU.mult)
                nc.vector.tensor_scalar(ndecay, lam[:, 3, :], 8.0, None, ALU.mult).then_inc(decay_ready, 1)

            def recurrent():
                j0 = base["rec"]
                o = KD * NT
                nc.vector.memset(xe[:, :, 0:PRE], 0.0)
                dve.wait_ge(state_loaded, 16)

                def evacuate_x(m, j):
                    r = m % 2
                    dve.wait_ge(job_done, j + 1)
                    if m >= 2:
                        dve.wait_ge(conv_saved, m - 1)
                    nc.vector.tensor_copy(seg(xe[:, r, :], 0, PRE),
                                          st_in[:, m, DEC_BATCH:].rearrange("p (b k) -> p b k", b=DEC_BATCH))
                    nc.vector.tensor_tensor(xe[:, r, PRE:S0].rearrange("p (a n) -> p a n", a=2),
                                            ps2(j % 2, 256), rstd[:, 0:SEQ].rearrange("p (a n) -> p a n", a=2),
                                            ALU.mult)
                    nc.vector.tensor_tensor(seg(xe[:, r, :], PRE, DEC_SEQ),
                                            ps[:, 2 * (j % 2) + 1, 256:256 + NS].rearrange("p (b t) -> p b t", b=DEC_BATCH),
                                            rstd[:, SEQ:NT].rearrange("p (b t) -> p b t", b=DEC_BATCH),
                                            ALU.mult).then_inc(dve_evac, 1)

                def conv(m):
                    r = m % 2
                    dve.wait_ge(dve_evac, evac(j0 + 8 * (m // 2) + r))
                    if m >= 2:
                        dve.wait_ge(ix_made, m - 1)
                    own(nc.vector.tensor_scalar(xc[:, r, :], xe[:, r, 0:NP], params[:, V_CW, m:m + 1],
                                                params[:, V_CB, m:m + 1], ALU.mult, ALU.add))
                    for k in range(1, CONV_W):
                        ins = nc.vector.scalar_tensor_tensor(xc[:, r, :], xe[:, r, k:k + NP],
                                                             params[:, V_CW + k, m:m + 1], xc[:, r, :],
                                                             ALU.mult, ALU.add)
                        if k < CONV_W - 1:
                            own(ins)
                    ins.then_inc(xc_made, 1)

                def rest_conv(m):
                    r = m % 2
                    dve.wait_ge(xc_hi_made, m + 1)
                    t = slice(o + r * NP, o + (r + 1) * NP)
                    nc.vector.tensor_tensor(act_lo[:, t], xc[:, r, :], act_hi[:, t].bitcast(F32),
                                            ALU.subtract).then_inc(xc_ready, 1)

                def evacuate_gate(m, j):
                    dve.wait_ge(job_done, j + 1)
                    nc.vector.tensor_tensor(two(gate[:, m % 4, :]), ps2(j % 2), two(rstd[:, :]),
                                            ALU.mult).then_inc(dve_evac, 1)

                def square_of_multiplier(m):
                    r = m % 2
                    dve.wait_ge(tanh_made, m + 1)
                    own(nc.vector.tensor_scalar(tmp[:, r, :], tt[:, r, :], 1.0, None, ALU.add))
                    own(nc.vector.reciprocal(tmp[:, r, :], tmp[:, r, :]))
                    nc.vector.scalar_tensor_tensor(tt[:, r, :], tt[:, r, :], 2.0, tmp[:, r, :], ALU.mult,
                                                   ALU.mult).then_inc(m2_made, 1)

                def scan(m):
                    r = m % 2
                    dve.wait_ge(mult_made, m + 1)
                    dve.wait_ge(ix_made, m + 1)
                    dve.wait_ge(a_made, m + 1)
                    own(nc.vector.tensor_tensor(ii[:, r, :], ii[:, r, :], tt[:, r, :], ALU.mult))
                    before = slice(S0 - 1, S0 - 1 + SEG * (DEC_BATCH - 1) + 1, SEG)
                    nc.vector.memset(rr[:, r, before], 0.0)
                    own(nc.vector.tensor_copy(ii[:, r, before], st_in[:, m, 0:DEC_BATCH]))
                    if m >= 2:
                        dve.wait_ge(h_saved, m - 1)
                    nc.vector.tensor_tensor_scan(hh[:, r, :], rr[:, r, :], ii[:, r, :], 0.0, ALU.mult,
                                                 ALU.add).then_inc(h_made, 1)
                    dve.wait_ge(h_made, m + 1)
                    dve.wait_ge(gate_out, m + 1)
                    nc.vector.tensor_tensor(tmp[:, r, 0:SEQ], hh[:, r, 0:SEQ], gate[:, m % 4, 0:SEQ], ALU.mult)
                    nc.vector.tensor_tensor(tmp[:, r, SEQ:NT].rearrange("p (b t) -> p b t", b=DEC_BATCH),
                                            hseg(hh[:, r, :]),
                                            gate[:, m % 4, SEQ:NT].rearrange("p (b t) -> p b t", b=DEC_BATCH),
                                            ALU.mult).then_inc(y_made, 1)

                def rest_y(m):
                    dve.wait_ge(y_hi_made, m + 1)
                    nc.vector.tensor_tensor(act_tile(act_lo, m), tmp[:, m % 2, 0:NT],
                                            act_tile(act_hi, m).bitcast(F32), ALU.subtract).then_inc(y_ready, 1)

                for n in range(KD // 2 + 1):
                    j = j0 + 8 * n
                    more = n < KD // 2
                    a, b = 2 * n, 2 * n + 1
                    if more:
                        evacuate_x(a, j)
                        prep_next(j)
                    if n:
                        square_of_multiplier(a - 2)
                        square_of_multiplier(b - 2)
                    if more:
                        conv(a)
                        evacuate_x(b, j + 1)
                        rest_conv(a)
                        prep_next(j + 1)
                        conv(b)
                        evacuate_gate(a, j + 2)
                        rest_conv(b)
                        prep_next(j + 2)
                    if n:
                        scan(a - 2)
                    if more:
                        evacuate_gate(b, j + 3)
                        prep_next(j + 3)
                    if n:
                        rest_y(a - 2)
                        scan(b - 2)
                    if more:
                        prep_next(j + 4)
                    if n:
                        rest_y(b - 2)
                    if more:
                        for k in range(5, 8):
                            prep_next(j + k)

            def hseg(v):
                return v[:, S0 - PRE:NP].rearrange("p (b s) -> p b s", b=DEC_BATCH)[:, :, PRE:SEG]

            def key_value():
                j = base["kv"]
                dve.wait_ge(job_done, j + 1)
                for g in range(N_KV):
                    for p in range(2):
                        ins = nc.vector.tensor_tensor(
                            two(kdup[64 * p:64 * p + 64, g, :]), ps[64 * g:64 * g + 64, 2 * (j % 2):2 * (j % 2) + 2, 0:288],
                            two(rstd[64 * p:64 * p + 64, :]), ALU.mult)
                ins.then_inc(dve_evac, 1)
                prep_next(j)
                dve.wait_ge(job_done, j + 2)
                nc.vector.tensor_tensor(two(v_t), ps2((j + 1) % 2), two(rstd[:, :]), ALU.mult).then_inc(dve_evac, 1)
                prep_next(j + 1)
                for m in range(KD):
                    split_x(4, m, None)
                dve.wait_ge(v_turned, 1)
                nc.vector.tensor_copy(v_tok[:, 0:NBLK, :].rearrange("p b n -> p (b n)"), ps[:, 6, :])
                nc.vector.tensor_copy(v_tok[0:NS, NBLK, :], ps[0:NS, 7, 0:P]).then_inc(v_tok_made, 1)

            def attention():
                j0 = base["q"]
                scale = HEAD_DIM ** -0.5
                for m in range(KD):
                    j = j0 + m
                    g = m // 4
                    dve.wait_ge(job_done, j + 1)
                    nc.vector.scalar_tensor_tensor(q_p[:, m, :].rearrange("p (a n) -> p a n", a=2), ps2(j % 2, 256), scale,
                                                   rstd[:, 0:SEQ].rearrange("p (a n) -> p a n", a=2),
                                                   ALU.mult, ALU.mult)
                    for p in range(2):
                        hh_ = (2 * (m % 4) + p) * DEC_SEQ
                        by_seq = lambda v: v.rearrange("p (b t) -> p b t", b=DEC_BATCH)
                        ins = nc.vector.scalar_tensor_tensor(
                            q_s[64 * g:64 * g + 64, :, hh_:hh_ + DEC_SEQ],
                            by_seq(ps[64 * p:64 * p + 64, 2 * (j % 2) + 1, 256:256 + NS]), scale,
                            by_seq(rstd[64 * g:64 * g + 64, SEQ:NT]), ALU.mult, ALU.mult)
                    ins.then_inc(dve_evac, 1)
                    prep_next(j)

                dve.wait_ge(att_loaded, 16 * 5)
                dve.wait_ge(misc_loaded, 32)
                for h in range(N_HEADS + 1):
                    if h < N_HEADS:
                        slope = 2.0 ** (-8.0 * (h + 1) / N_HEADS)
                        o = 4 * (h % 2)
                        b0 = 4 if h % 2 == 0 else 0
                        s0 = ps[:, b0, P:2 * P]
                        s3 = ps[:, b0:b0 + 2, :].rearrange("p a n -> p (a n)")[:, 256:1024].rearrange(
                            "p (b n) -> p b n", b=3)
                        dve.wait_ge(scores_done, h + 1)
                        nc.vector.scalar_tensor_tensor(s0, dist[:, P:2 * P], slope, s0, ALU.mult, ALU.add)
                        own(nc.vector.scalar_tensor_tensor(s3, dist.unsqueeze(1).broadcast_to([P, 3, 256]), slope, s3,
                                                           ALU.mult, ALU.add))
                        nc.vector.tensor_reduce(neg_max[:, o:o + 1], s0, AX_X, ALU.max)
                        own(nc.vector.tensor_reduce(neg_max[:, o + 1:o + 4], s3, AX_X, ALU.max))
                        nc.vector.tensor_scalar(neg_max[:, o:o + 4], neg_max[:, o:o + 4], sinks[:, h:h + 1], -1.0,
                                                ALU.max, ALU.mult).then_inc(max_made, 1)
                    if h >= 1:
                        q = h - 1
                        o = 4 * (q % 2)
                        dve.wait_ge(exp_made, q + 1)
                        own(nc.vector.tensor_tensor(inv_den[:, o:o + 4], row_sum[:, o:o + 4], sink_exp[:, o:o + 4], ALU.add))
                        nc.vector.reciprocal(inv_den[:, o:o + 4], inv_den[:, o:o + 4]).then_inc(inv_made, 1)
                    if h >= 4 and h % 2 == 0:
                        rest_o((h - 4) // 2)
                rest_o(KD - 1)
                dve.wait_ge(scores_done, N_HEADS + 1)
                for g in range(N_KV):
                    r = slice(64 * g, 64 * g + 64)
                    b0 = 4 - 4 * g
                    for b in range(0, DEC_BATCH, 2):
                        src = ps[r, b0 + b // 2, 0:2 * NKEY].rearrange("p (a n) -> p a n", a=2)
                        nc.vector.tensor_tensor(s_s[r, b:b + 2, 0:WINDOW], src[:, :, 0:WINDOW],
                                                bias_c[r, :].unsqueeze(1).broadcast_to([64, 2, WINDOW]), ALU.add)
                        ins = nc.vector.tensor_tensor(s_s[r, b:b + 2, WINDOW:NKEY], src[:, :, WINDOW:NKEY],
                                                      bias_n[r, b:b + 2, :], ALU.add)
                own(ins)
                own(nc.vector.tensor_reduce(neg_max[:, 0:8], s_s, AX_X, ALU.max))
                nc.vector.tensor_scalar(neg_max[:, 0:8], neg_max[:, 0:8], sinks[:, N_HEADS:N_HEADS + 1], -1.0,
                                        ALU.max, ALU.mult).then_inc(max_made, 1)
                dve.wait_ge(exp_made, N_HEADS + 1)
                own(nc.vector.tensor_tensor(inv_den[:, 0:8], row_sum[:, 0:8], sink_exp[:, 0:8], ALU.add))
                own(nc.vector.reciprocal(inv_den[:, 0:8], inv_den[:, 0:8]))
                nc.vector.tensor_tensor(s_s, s_s, inv_den[:, 0:8].unsqueeze(2).broadcast_to([P, DEC_BATCH, NKEY]),
                                        ALU.mult).then_inc(prob_ready, 1)
                dve.wait_ge(o_hi_made, KD + 1)
                for m in range(KD):
                    t = slice(m * NT + SEQ, (m + 1) * NT)
                    ins = nc.vector.tensor_tensor(
                        act_lo[:, t].rearrange("p (b t) -> p b t", t=DEC_SEQ),
                        ps[:, 0, :].rearrange("p (b m t) -> p m b t", b=DEC_BATCH, m=KD)[:, m],
                        act_hi[:, t].bitcast(F32).rearrange("p (b t) -> p b t", t=DEC_SEQ), ALU.subtract)
                ins.then_inc(att_ready, 1)

            def rest_o(m):
                dve.wait_ge(o_hi_made, m + 1)
                t = slice(m * NT, m * NT + SEQ)
                nc.vector.tensor_tensor(act_lo[:, t], ps[:, 2 + m % 2, :], act_hi[:, t].bitcast(F32),
                                        ALU.subtract).then_inc(att_ready, 1)

            prep(0, 0, 0, KT[0])
            for m in range(KD):
                split_x(0, m, 0)
            prep(1, 1, 1, KT[1])
            invert(0)
            ffn(0, 1, 1)
            invert(1)
            lru_constants()
            recurrent()
            down(base["wout"], 2, 2, 1.0)
            invert(2)
            ffn(1, 3, 3)
            invert(3)
            key_value()
            ffn(2, 5, 4)
            invert(4)
            attention()
            down(base["wo"], 6, 5, 1.0)
            invert(5)
            ffn(3, None, 6)
            invert(6)
            for m in range(KD):
                nc.vector.scalar_tensor_tensor(x[:, m, :], x[:, m, :], params[:, V_FIN, m:m + 1], rstd[:, :],
                                               ALU.mult, ALU.mult).then_inc(y_out, 1)

        @block.gpsimd
        def _(pool):
            pool.dma_start(ident[:, :], A["ident"]).then_inc(misc_loaded, 16)
            pool.dma_start(sinks[:, :], A["sinks"]).then_inc(misc_loaded, 16)
            pool.dma_start(A["ck_out"], A["cache_k"][:, DEC_SEQ:, :]).then_inc(side_stored, 16)
            pool.dma_start(A["cv_out"], A["cache_v"][:, DEC_SEQ:, :]).then_inc(side_stored, 16)
            pool.dma_start(st_in, A["st_in"]).then_inc(state_loaded, 16)

            for m in range(KD):
                r = m % 2
                pool.wait_ge(dve_evac, evac(base["rec"] + 8 * (m // 2) + r))
                nc.gpsimd.tensor_copy(st_out[:, m, 1:1 + PRE], xe[:, r, SEQ:SEQ + PRE])
                nc.gpsimd.tensor_copy(
                    st_out[:, m, 1 + PRE + DEC_BATCH:].rearrange("p (b k) -> p b k", b=DEC_BATCH),
                    seg(xe[:, r, :], DEC_SEQ, PRE)).then_inc(conv_saved, 1)
                if r == 1:
                    for q in (m - 1, m):
                        pool.wait_ge(act_evac, 2 * q + 2)
                        pool.wait_ge(xc_made, q + 1)
                        nc.gpsimd.tensor_tensor(ii[:, q % 2, :], ii[:, q % 2, :], xc[:, q % 2, :],
                                                ALU.mult).then_inc(ix_made, 1)
                if r == 1 and m >= 3 or m == KD - 1:
                    done = (m - 3, m - 2) if m < KD - 1 else (m - 3, m - 2, m - 1, m)
                    for q in done:
                        pool.wait_ge(h_made, q + 1)
                        last = SEQ + PRE + DEC_SEQ - 1
                        nc.gpsimd.tensor_copy(st_out[:, q, 0:1], hh[:, q % 2, SEQ - 1:SEQ])
                        nc.gpsimd.tensor_copy(
                            st_out[:, q, 1 + PRE:1 + PRE + DEC_BATCH],
                            hh[:, q % 2, last:last + SEG * (DEC_BATCH - 1) + 1:SEG]).then_inc(h_saved, 1)
            pool.wait_ge(h_saved, KD)
            pool.wait_ge(conv_saved, KD)
            pool.dma_start(A["st_out"], st_out).then_inc(side_stored, 16)
            pool.wait_ge(dve_evac, evac(base["kv"] + 1))
            keep = slice(SEQ - WINDOW, NT)
            for g in range(N_KV):
                pool.dma_start(A["k_new"][64 * g:64 * g + 64, :], kdup[64 * g:64 * g + 64, g, keep]).then_inc(side_stored, 16)
            pool.dma_start(A["v_new"], v_t[:, keep]).then_inc(side_stored, 16)
            pool.wait_ge(side_stored, 16 * 6)
            pool.wait_ge(v_turned, 1)
            pool.dma_start(dist, A["dist"]).then_inc(att_loaded, 16)
            pool.dma_start(bias_c, A["bias_c"]).then_inc(att_loaded, 16)
            pool.dma_start(bias_n, A["bias_n"]).then_inc(att_loaded, 16)
            pool.dma_start(kc, A["k_cT"]).then_inc(att_loaded, 16)
            pool.dma_start(vc, A["cache_v"].rearrange("b s n -> s b n")).then_inc(att_loaded, 16)
            for h in range(N_HEADS):
                o = 4 * (h % 2)
                pool.wait_ge(inv_made, h + 1)
                for b in range(NBLK):
                    lo, hi = 256 * b + (0 if b else P), 256 * (b + 1)
                    ins = nc.gpsimd.tensor_scalar(prob[:, lo:hi], prob[:, lo:hi], inv_den[:, o + b:o + b + 1],
                                                  None, ALU.mult)
                ins.then_inc(prob_ready, 1)


def kernel(**inputs):
    import numpy as np
    import concourse.bacc as bacc
    from concourse.bass_utils import run_bass_kernel_spmd

    a = {k: np.asarray(v) for k, v in inputs.items()}
    f32 = np.float32

    def chunks(w, jobs_cols):
        k, n = w.shape
        return w.reshape(k // P, P, n // P, P).transpose(2, 1, 0, 3).reshape(n // P, P, k)

    gu, dn = [], []
    for l in range(2):
        for which in ("ffn1", "ffn2"):
            g = chunks(a[f"{which}_w_gu"][l], None).reshape(2, FT, P, D_MODEL)
            gu.append(g.transpose(1, 0, 2, 3).reshape(2 * FT, P, D_MODEL))
            w = a[f"{which}_w_down"][l]
            for half in range(2):
                dn.append(chunks(w[half * HF * P:(half + 1) * HF * P], None))
    w_in = chunks(a["rg_w_in"][0], None).reshape(2, KD // 2, 2, P, D_MODEL)
    ax = np.stack([a["rg_w_a"][0], a["rg_w_x"][0]])
    ax = ax.reshape(2, 4, 2, P, 2, P).transpose(1, 4, 0, 3, 2, 5).reshape(16, P, 2 * P)

    q, c = np.arange(P)[:, None], np.arange(2 * WINDOW)[None]
    diff = WINDOW + q - c
    dist = np.where((diff >= 0) & (diff < WINDOW), -diff, -1e33).astype(f32)
    head, t = np.arange(P)[:, None] // DEC_SEQ, np.arange(P)[:, None] % DEC_SEQ
    slope = np.exp2(-8.0 * (head + 1) / N_HEADS)
    s = np.arange(WINDOW)[None]
    bias_c = np.where(s > t, -slope * (WINDOW + t - s), -1e30).astype(f32)
    b, tk = np.arange(NS)[None] // DEC_SEQ, np.arange(NS)[None] % DEC_SEQ
    bias_n = np.stack([np.where((b == i) & (tk <= t), -slope * (t - tk), -1e30) for i in range(DEC_BATCH)],
                      axis=1).astype(f32)

    vecs = [a["ffn1_norm"][0], a["ffn1_norm"][1], a["mix_norm"][0], a["mix_norm"][1], a["ffn2_norm"][0],
            a["ffn2_norm"][1], a["kv_norm"], a["final_norm"], *a["rg_conv_w"][0], a["rg_conv_b"][0],
            a["rg_b_a"][0], a["rg_b_x"][0], a["rg_lambda"][0]]
    sinks = a["attn_sinks"][0]
    states = np.concatenate([a["state_rg_h"][0].T, a["state_rg_conv"][0].reshape(-1, D_MODEL).T], axis=1)
    arrays = {
        "xT": np.concatenate([a["x_prompt"][0], a["x_sample"].reshape(NS, D_MODEL)]).T.reshape(KD, P, NT),
        "params": np.stack(vecs).reshape(N_VEC, KD, P).transpose(2, 0, 1),
        "ones": np.ones((P, P), f32),
        "ident": np.eye(P, dtype=f32),
        "eps": np.full((P, 1), EPS, f32),
        "sinks": np.concatenate([np.broadcast_to(sinks, (P, N_HEADS)), np.repeat(sinks, DEC_SEQ)[:, None]], axis=1),
        "st_in": states.reshape(KD, P, -1).transpose(1, 0, 2),
        "w_gu": np.concatenate(gu),
        "w_dn": np.concatenate(dn),
        "w_in": w_in[::-1].transpose(1, 0, 2, 3, 4).reshape(16, P, D_MODEL),
        "w_ax": ax,
        "w_out": chunks(a["rg_w_out"][0], None),
        "w_kv": chunks(a["w_kv"], None),
        "w_q": chunks(a["attn_w_q"][0], None),
        "w_o": chunks(a["attn_w_o"][0], None),
        "cache_k": a["cache_k"].reshape(DEC_BATCH, WINDOW, P),
        "cache_v": a["cache_v"].reshape(DEC_BATCH, WINDOW, P),
        "k_cT": a["cache_k"].reshape(DEC_BATCH, WINDOW, P).transpose(2, 0, 1),
        "dist": dist, "bias_c": bias_c, "bias_n": bias_n,
    }
    outs = {"yT": (KD, P, NT), "st_out": (P, KD, NSTATE), "k_new": (P, WINDOW + NS), "v_new": (P, WINDOW + NS),
            "ck_out": (DEC_BATCH, WINDOW - DEC_SEQ, P), "cv_out": (DEC_BATCH, WINDOW - DEC_SEQ, P)}

    nc = bacc.Bacc("TRN2", target_bir_lowering=False, num_devices=1)
    A = {}
    for name, v in arrays.items():
        arrays[name] = np.ascontiguousarray(v)
        A[name] = nc.dram_tensor(name, v.shape, F32, kind="ExternalInput").ap()
    for name, shape in outs.items():
        A[name] = nc.dram_tensor(name, shape, F32, kind="ExternalOutput").ap()
    build(nc, A)
    r = run_bass_kernel_spmd(nc, [arrays], core_ids=[0]).results[0]

    y = r["yT"].reshape(D_MODEL, NT).T
    st = r["st_out"].transpose(1, 0, 2).reshape(D_MODEL, NSTATE).T
    new = {k: r[f"{k}_new"].T.reshape(WINDOW + NS, N_KV, HEAD_DIM) for k in "kv"}
    cache = {k: r[f"c{k}_out"].reshape(DEC_BATCH, WINDOW - DEC_SEQ, N_KV, HEAD_DIM) for k in "kv"}
    rolled = {k: np.concatenate([cache[k], new[k][WINDOW:].reshape(DEC_BATCH, DEC_SEQ, N_KV, HEAD_DIM)], axis=1)
              for k in "kv"}
    c0, c1, c2 = 1, 1 + PRE, 1 + PRE + DEC_BATCH
    out = (y[None, :SEQ], y[SEQ:].reshape(DEC_BATCH, DEC_SEQ, D_MODEL),
           st[None, 0:c0], st[None, None, c0:c1], new["k"][None, :WINDOW], new["v"][None, :WINDOW],
           st[None, c1:c2], st[c2:].reshape(1, DEC_BATCH, PRE, D_MODEL), rolled["k"], rolled["v"])
    return tuple(np.ascontiguousarray(o) for o in out)
```

```python
from contextlib import ExitStack

import concourse.bass as bass
from concourse import mybir

F32 = mybir.dt.float32
F32R = mybir.dt.float32r
ALU = mybir.AluOpType
ACT = mybir.ActivationFunctionType
AX_X = mybir.AxisListType.X

P = 128
D_MODEL, SEQ, DEC_BATCH, DEC_SEQ = 1024, 512, 8, 8
NS = DEC_BATCH * DEC_SEQ
NT = SEQ + NS
KD = D_MODEL // P
FT = 22
HF = FT // 2
CONV_W = 4
HEAD_DIM, N_HEADS, N_KV = 64, 16, 2
WINDOW = 128
NBLK = SEQ // WINDOW
NKEY = WINDOW + NS
EPS = 1e-6

PRE = CONV_W - 1
SEG = PRE + DEC_SEQ
NE = PRE + SEQ + DEC_BATCH * SEG
NP = NE - PRE
S0 = SEQ + PRE
NSTATE = 1 + PRE + DEC_BATCH * (1 + PRE)

(V_F1A, V_F1B, V_MA, V_MB, V_F2A, V_F2B, V_KV, V_FIN,
 V_CW, V_CB, V_BA, V_BX, V_LAM, N_VEC) = (0, 1, 2, 3, 4, 5, 6, 7, 8, 12, 13, 14, 15, 16)

GU_JOBS, DN_JOBS = 2 * HF, KD
N_FFN = 2 * (GU_JOBS + DN_JOBS)


def plan():
    kt, act, base = [], [], {}

    def ffn(f):
        for half in range(2):
            base["gu", f, half] = len(kt)
            kt.extend([KD] * GU_JOBS)
            base["dn", f, half] = len(kt)
            kt.extend([HF] * DN_JOBS)

    ffn(0)
    def rec(name, *key):
        base[(name, *key)] = len(kt)
        kt.append(KD)

    base["rec"] = len(kt)
    rec("xr", 0)
    rec("xr", 1)
    for n in range(KD // 2):
        if n + 1 < KD // 2:
            rec("xr", 2 * n + 2)
            rec("xr", 2 * n + 3)
        act.append(len(kt))
        rec("ax", n)
        rec("gate", 2 * n)
        rec("gate", 2 * n + 1)
    base["wout"] = len(kt)
    kt.extend([KD] * KD)
    ffn(1)
    base["kv"] = len(kt)
    kt.extend([KD] * 2)
    ffn(2)
    base["q"] = len(kt)
    kt.extend([KD] * KD)
    base["wo"] = len(kt)
    kt.extend([KD] * KD)
    ffn(3)
    return base, kt, act


def build(nc, A):
    base, KT, ACT_JOBS = plan()
    NJ = len(KT)
    act_jobs = set(ACT_JOBS)
    CH = HF * P

    with ExitStack() as ctx:
        def sb(name, shape, dt=F32):
            return ctx.enter_context(nc.sbuf_tensor(name, shape, dt))

        def sem(name):
            return ctx.enter_context(nc.semaphore(name))

        x = sb("x", [P, KD, NT])
        xs_hi = sb("xs_hi", [P, KD, NT], F32R)
        xs_lo = sb("xs_lo", [P, KD, NT], F32R)
        act_hi = sb("act_hi", [P, HF * NT], F32R)
        act_lo = sb("act_lo", [P, HF * NT], F32R)
        raw = sb("raw", [P, 4, CH])
        w_hi = sb("w_hi", [P, 2, CH], F32R)
        w_lo = sb("w_lo", [P, 2, CH], F32R)
        rstd = sb("rstd", [P, NT])
        ssum = sb("ssum", [P, NT])
        sq = sb("sq", [P, 2, NT])
        std = sq[:, 0, :]
        params = sb("params_sb", [P, N_VEC, KD])
        ones = sb("ones_sb", [P, P])
        ident = sb("ident_sb", [P, P])
        eps = sb("eps_sb", [P, 1])
        sinks = sb("sinks_sb", [P, N_HEADS + 1])
        AR = 12700
        arena = sb("arena", [P, AR])
        ps = ctx.enter_context(nc.psum_tensor("ps", [P, 8, 512], F32))

        at = [0]

        def take(n):
            v = arena[:, at[0]:at[0] + n]
            at[0] += n
            assert at[0] <= AR, at[0]
            return v

        gate_t = take(2 * NT).rearrange("p (a n) -> p a n", a=2)
        silu_t = take(2 * NT).rearrange("p (a n) -> p a n", a=2)
        up_t = take(2 * NT).rearrange("p (a n) -> p a n", a=2)
        hid = take(2 * NT).rearrange("p (a n) -> p a n", a=2)
        at[0] = 0
        xe = take(2 * NE).rearrange("p (a n) -> p a n", a=2)
        xc = take(4 * NP).rearrange("p (a n) -> p a n", a=4)
        rr = take(2 * NP).rearrange("p (a n) -> p a n", a=2)
        ii = take(2 * NP).rearrange("p (a n) -> p a n", a=2)
        tt = take(2 * NP).rearrange("p (a n) -> p a n", a=2)
        tmp = take(2 * NP).rearrange("p (a n) -> p a n", a=2)
        hh = take(2 * NP).rearrange("p (a n) -> p a n", a=2)
        gate = take(2 * NT).rearrange("p (a n) -> p a n", a=2)
        st_in = take(KD * DEC_BATCH * (1 + PRE)).rearrange("p (m s) -> p m s", m=KD)
        st_out = take(KD * NSTATE).rearrange("p (m s) -> p m s", m=KD)
        lam = take(8 * KD).rearrange("p (a m) -> p a m", a=8)
        decay = lam[:, 6, :]
        ndecay = lam[:, 7, :]
        at[0] = 8 * NT
        kdup = take(N_KV * NT).rearrange("p (g n) -> p g n", g=N_KV)
        v_tok = take((NBLK + 1) * P).rearrange("p (b n) -> p b n", b=NBLK + 1)
        v_t = take(NT)
        vkeep = at[0]
        at[0] = 0
        q_p = take(KD * SEQ).rearrange("p (m n) -> p m n", m=KD)
        q_s = take(8 * NS).rearrange("p (b n) -> p b n", b=DEC_BATCH)
        assert at[0] <= 8 * NT
        at[0] = vkeep - NT
        dist = take(2 * WINDOW)
        bias_c = take(WINDOW)
        bias_n = take(DEC_BATCH * NS).rearrange("p (b n) -> p b n", b=DEC_BATCH)
        kc = take(DEC_BATCH * WINDOW).rearrange("p (b n) -> p b n", b=DEC_BATCH)
        vc = take(DEC_BATCH * P).rearrange("p (b n) -> p b n", b=DEC_BATCH)
        small = take(64)
        prob = [take(4 * 256), take(4 * 256)]
        pt = [take(7 * P), sq.rearrange("p a n -> p (a n)")[:, 0:7 * P]]
        s_s = q_p[:, 0:3, :].rearrange("p m n -> p (m n)").rearrange("p (b n) -> p b n", b=DEC_BATCH)
        ptc = q_p[:, 3:5, :].rearrange("p m n -> p (m n)").rearrange("p (b n) -> p b n", b=DEC_BATCH)
        ptn = q_p[:, 5:7, :].rearrange("p m n -> p (m n)").rearrange("p (b n) -> p b n", b=DEC_BATCH)
        neg_max, row_sum, sink_exp, inv_den = (small[:, 8 * i:8 * i + 8] for i in range(4))

        x_loaded = [sem(f"x_loaded{m}") for m in range(KD)]
        consts_loaded = sem("consts_loaded")
        misc_loaded = sem("misc_loaded")
        state_loaded = sem("state_loaded")
        att_loaded = sem("att_loaded")
        raw_landed = [sem(f"raw_landed{i}") for i in range(4)]
        stored = sem("stored")
        side_stored = sem("side_stored")
        hi_made = sem("hi_made")
        lo_made = sem("lo_made")
        job_done = sem("job_done")
        dve_evac = sem("dve_evac")
        act_evac = sem("act_evac")
        xs_hi_made = sem("xs_hi_made")
        xs_ready = sem("xs_ready")
        sq_made = sem("sq_made")
        ss_added = sem("ss_added")
        stat_sum = sem("stat_sum")
        std_made = sem("std_made")
        rstd_made = sem("rstd_made")
        silu_made = sem("silu_made")
        hid_made = sem("hid_made")
        hid_hi_made = sem("hid_hi_made")
        hid_ready = sem("hid_ready")
        dve_chain = sem("dve_chain")
        pool_chain = sem("pool_chain")
        lam_exp = sem("lam_exp")
        lam_abs = sem("lam_abs")
        xc_made = sem("xc_made")
        xc_hi_made = sem("xc_hi_made")
        xc_ready = sem("xc_ready")
        conv_saved = sem("conv_saved")
        gate_out = sem("gate_out")
        ix_made = sem("ix_made")
        decay_ready = sem("decay_ready")
        tanh_made = sem("tanh_made")
        a_made = sem("a_made")
        a2_made = sem("a2_made")
        ax_done = sem("ax_done")
        m2_made = sem("m2_made")
        mult_made = sem("mult_made")
        h_made = sem("h_made")
        h_saved = sem("h_saved")
        y_made = sem("y_made")
        y_hi_made = sem("y_hi_made")
        y_ready = sem("y_ready")
        v_turned = sem("v_turned")
        v_tok_made = sem("v_tok_made")
        scores_done = sem("scores_done")
        max_made = sem("max_made")
        exp_made = sem("exp_made")
        prob_ready = sem("prob_ready")
        prob_turned = sem("prob_turned")
        pt_ready = sem("pt_ready")
        pv_done = sem("pv_done")
        o_hi_made = sem("o_hi_made")
        att_ready = sem("att_ready")
        y_out = sem("y_out")

        GAIN = [V_F1A, V_MA, V_F2A, V_KV, V_F1B, V_MB, V_F2B]
        FFN_INPUT = [0, 2, 4, 6]
        dve_done = [0]
        for j in range(NJ):
            dve_done.append(dve_done[-1] + (j not in act_jobs))

        def evac(j):
            return dve_done[j + 1]

        def slot_free(pe, j):
            if j < 2:
                return
            if j - 2 in act_jobs:
                pe.wait_ge(act_evac, 4 * (j - 1 - dve_done[j - 1]))
            else:
                pe.wait_ge(dve_evac, dve_done[j - 1])

        def wv(s, r, k):
            return s[:, r, k * P:(k + 1) * P]

        def act_tile(a, k):
            return a[:, k * NT:(k + 1) * NT]

        def conv_at(m):
            return HF * NT - NP * (2, 1, 4, 3)[m % 4]

        def halves(ap, at_, w):
            return ap[:, at_:at_ + w]

        EVEN = ((0, 288), (288, 288))
        BLOCKS = ((0, 256), (256, 320))
        PADDED = ((0, NP // 2), (NP // 2, NP // 2))

        def ps2(slot, n=288):
            return ps[:, 2 * slot:2 * slot + 2, 0:n]

        def two(ap, n=2):
            return ap.rearrange("p (a n) -> p a n", a=n)

        def seg(ap, first, n):
            return ap[:, S0:S0 + DEC_BATCH * SEG].rearrange(
                "p (b s) -> p b s", b=DEC_BATCH)[:, :, first:first + n]

        def sample_cols(a):
            return a[:, 0:KD * NT].rearrange("p (m n) -> p m n", m=KD)[:, :, SEQ:NT].rearrange(
                "p m (b t) -> p m b t", b=DEC_BATCH)

        sample_o = ps[:, 1, :].rearrange("p (b m t) -> p m b t", b=DEC_BATCH, m=KD)

        block = ctx.enter_context(nc.Block())

        def load(sp, slot, src, kt):
            sp.dma_start(raw[:, slot, 0:kt * P], src).then_inc(raw_landed[slot], 16)

        @block.sync
        def _(sp):
            for m in range(KD):
                sp.dma_start(x[:, m, :], A["xT"][m]).then_inc(x_loaded[m], 16)
                if m == 0:
                    sp.dma_start(params[:, :, :], A["params"]).then_inc(consts_loaded, 16)
                    sp.dma_start(ones[:, :], A["ones"]).then_inc(consts_loaded, 16)
                    sp.dma_start(eps[:, :], A["eps"]).then_inc(consts_loaded, 16)
                    load(sp, 0, A["w_gu"][0], KD)

            def free(c):
                sp.wait_ge(lo_made, c - 3)

            def stream(first, src, n, kt, row0):
                lead = 0
                while first + lead < 4:
                    if first + lead > 0:
                        load(sp, (first + lead) % 4, src[row0 + lead], kt)
                    lead += 1
                turns = (n - lead) // 4
                if turns:
                    with sp.Fori(0, turns) as i:
                        for k in range(4):
                            c = lead + 4 * i + k
                            sp.wait_ge(lo_made, first + c - 3)
                            load(sp, (first + lead + k) % 4,
                                 src[bass.ds(row0 + c, 1)].rearrange("a p n -> p (a n)"), kt)
                for c in range(lead + 4 * turns, n):
                    free(first + c)
                    load(sp, (first + c) % 4, src[row0 + c], kt)

            def ffn(f):
                for half in range(2):
                    stream(base["gu", f, half], A["w_gu"], GU_JOBS, KD, (2 * f + half) * GU_JOBS)
                    stream(base["dn", f, half], A["w_dn"], DN_JOBS, HF, (2 * f + half) * DN_JOBS)

            ffn(0)
            stream(base["rec"], A["w_rec"], base["wout"] - base["rec"], KD, 0)
            stream(base["wout"], A["w_out"], KD, KD, 0)
            ffn(1)
            stream(base["kv"], A["w_kv"], 2, KD, 0)
            ffn(2)
            stream(base["q"], A["w_q"], KD, KD, 0)
            stream(base["wo"], A["w_o"], KD, KD, 0)
            ffn(3)
            for m in range(KD):
                sp.wait_ge(y_out, m + 1)
                sp.dma_start(A["yT"][m], x[:, m, :]).then_inc(stored, 16)
            sp.wait_ge(stored, 16 * KD)
            sp.wait_ge(side_stored, 16 * 6)

        @block.tensor
        def _(pe):
            def mm_k(slot, w, k, hi, lo, cut, first, last, kw=None):
                kw = k if kw is None else kw
                passes = ((w_hi, hi), (w_hi, lo), (w_lo, hi))
                for n, (a, b) in enumerate(passes):
                    for c, (o, width) in enumerate(cut):
                        ins = nc.tensor.matmul(ps[:, 2 * slot + c, 0:width], wv(a, w, kw), halves(b, o, width),
                                               start=first and n == 0, stop=last and n == 2)
                return ins

            def job(j, par, kt, operand, cut=EVEN, ready=None):
                pe.wait_ge(lo_made, j + 1)
                for k in range(kt):
                    if ready:
                        pe.wait_ge(*ready(k))
                    hi, lo = operand(k)
                    ins = mm_k(par, par, k, hi, lo, cut, k == 0, k == kt - 1)
                ins.then_inc(job_done, 1)

            def xs_tile(k):
                return xs_hi[:, k, :], xs_lo[:, k, :]

            def hid_tile(k):
                return act_tile(act_hi, k), act_tile(act_lo, k)

            def stats(s):
                pe.wait_ge(ss_added, (KD - 1) * (s + 1))
                if s == 0:
                    pe.wait_ge(consts_loaded, 48)
                for c, (o, width) in enumerate(EVEN):
                    ins = nc.tensor.matmul(ps[:, 4 + c, 0:width], ones[:, :], ssum[:, o:o + width],
                                           start=True, stop=True)
                ins.then_inc(stat_sum, 1)

            def ffn(f, stat):
                s = FFN_INPUT[f]
                for half in range(2):
                    j0 = base["gu", f, half]
                    for j in (j0, j0 + 1):
                        slot_free(pe, j)
                        job(j, j % 2, KD, xs_tile,
                            ready=(lambda k: (xs_ready, KD * s + k + 1)) if j == j0 and half == 0 else None)
                        if j == j0 and half == 0 and stat is not None:
                            stats(stat)
                    with pe.Fori(0, (GU_JOBS - 2) // 4) as i:
                        for k in range(4):
                            j = 4 * i + (j0 + 2 + k)
                            pe.wait_ge(dve_evac, 4 * i + dve_done[j0 + 1 + k])
                            job(j, (j0 + k) % 2, KD, xs_tile)
                    j0 = base["dn", f, half]
                    u0 = FT * f + HF * half
                    with pe.Fori(0, DN_JOBS // 2) as i:
                        for k in range(2):
                            j = 2 * i + (j0 + k)
                            pe.wait_ge(dve_evac, 2 * i + dve_done[j0 + k - 1])
                            job(j, (j0 + k) % 2, HF, hid_tile,
                                ready=(lambda t: (hid_ready, u0 + t + 1)) if k == 0 else None)

            def recurrent():
                def conv_tile(m):
                    o = conv_at(m)
                    return act_hi[:, o:o + NP], act_lo[:, o:o + NP]

                def conv_input(m):
                    j = base["xr", m]
                    slot_free(pe, j)
                    job(j, j % 2, KD, xs_tile, cut=BLOCKS,
                        ready=(lambda k: (xs_ready, KD + k + 1)) if m == 0 else None)

                conv_input(0)
                stats(1)
                conv_input(1)
                for n in range(KD // 2):
                    if n + 1 < KD // 2:
                        conv_input(2 * n + 2)
                        conv_input(2 * n + 3)
                    j = base["ax", n]
                    slot_free(pe, j)
                    pe.wait_ge(lo_made, j + 1)
                    pe.wait_ge(xc_ready, 2 * n + 2)
                    if n == 0:
                        pe.wait_ge(std_made, 2)
                    else:
                        pe.wait_ge(act_evac, 4 * n)
                    for q in range(4):
                        if q == 3:
                            pe.wait_ge(act_evac, 4 * n + 1)
                        for k in range(2):
                            hi, lo = conv_tile(2 * n + k)
                            ins = mm_k((j % 2, 2, 3, j % 2)[q], j % 2, k, hi, lo, PADDED, k == 0, k == 1,
                                       kw=2 * q + k)
                        if q < 3:
                            ins.then_inc(ax_done, 1)
                    ins.then_inc(job_done, 1)
                    for m in (2 * n, 2 * n + 1):
                        j = base["gate", m]
                        slot_free(pe, j)
                        job(j, j % 2, KD, xs_tile)

            def out_product(j0, ready, first=0):
                for m in range(first, KD):
                    slot_free(pe, j0 + m)
                    job(j0 + m, (j0 + m) % 2, KD, hid_tile, ready=ready if m == 0 else None)

            def key_value():
                j = base["kv"]
                slot_free(pe, j)
                job(j, j % 2, KD, xs_tile, ready=lambda k: (xs_ready, 3 * KD + k + 1))
                stats(3)
                slot_free(pe, j + 1)
                job(j + 1, (j + 1) % 2, KD, xs_tile)

            def turn_values():
                pe.wait_ge(dve_evac, evac(base["kv"] + 1))
                pe.wait_ge(misc_loaded, 32)
                for b in range(NBLK):
                    nc.tensor.transpose(ps[:, 6, b * P:(b + 1) * P], v_t[:, b * P:(b + 1) * P], ident[:, :])
                nc.tensor.transpose(ps[0:NS, 7, 0:P], v_t[:, SEQ:NT], ident[:, :]).then_inc(v_turned, 1)

            def attention():
                j0 = base["q"]
                for m in range(KD):
                    slot_free(pe, j0 + m)
                    job(j0 + m, (j0 + m) % 2, KD, xs_tile, cut=BLOCKS,
                        ready=(lambda k: (xs_ready, 5 * KD + k + 1)) if m == 0 else None)
                    if m == 0:
                        stats(4)

                def scores(h):
                    m, p, g = h // 2, 64 * (h % 2), h // 8
                    b0 = 4 if h % 2 == 0 else 0
                    if h >= 2:
                        pe.wait_ge(exp_made, h - 1)
                    for b in range(NBLK):
                        q = q_p[p:p + 64, m, b * P:(b + 1) * P]
                        lo, hi = (b - 1) * P, (b + 1) * P
                        if b == 0:
                            lo = 0
                        c = (b % 2) * 256 + (0 if b else P)
                        ins = nc.tensor.matmul(ps[:, b0 + b // 2, c:c + hi - lo], q, kdup[p:p + 64, g, lo:hi],
                                               start=True, stop=True)
                    ins.then_inc(scores_done, 1)

                def turn(h):
                    pe.wait_ge(prob_ready, h + 1)
                    if h >= 1:
                        pe.wait_ge(pt_ready, h)
                    for t in range(7):
                        ins = nc.tensor.transpose(ps[:, 6 + t // 4, (t % 4) * P:(t % 4 + 1) * P],
                                                  prob[h % 2][:, (t + 1) * P:(t + 2) * P], ident[:, :])
                    ins.then_inc(prob_turned, 1)

                def values(h):
                    m, p, g = h // 2, 64 * (h % 2), h // 8
                    pe.wait_ge(pt_ready, h + 1)
                    if h % 2 == 0 and m >= 2:
                        pe.wait_ge(att_ready, m - 1)
                    for b in range(NBLK):
                        for t in ([0] if b == 0 else [2 * b - 1, 2 * b]):
                            kb = b if t == 2 * b else b - 1
                            ins = nc.tensor.matmul(ps[p:p + 64, 2 + m % 2, b * P:(b + 1) * P],
                                                   v_tok[:, kb, 64 * g:64 * g + 64],
                                                   pt[h % 2][:, t * P:(t + 1) * P],
                                                   start=t in (0, 2 * b - 1), stop=t == 2 * b)
                    ins.then_inc(pv_done, 1)

                pe.wait_ge(dve_evac, dve_done[j0 + KD])
                pe.wait_ge(std_made, 5)
                pe.wait_ge(v_tok_made, 1)
                scores(0)
                scores(1)
                for h in range(N_HEADS + 1):
                    if h + 2 < N_HEADS:
                        scores(h + 2)
                    if h < N_HEADS:
                        turn(h)
                    if h >= 1:
                        values(h - 1)

                pe.wait_ge(exp_made, N_HEADS)
                pe.wait_ge(pt_ready, N_HEADS)
                pe.wait_ge(att_ready, KD)
                pe.wait_ge(att_loaded, 16 * 5)
                for g in range(N_KV):
                    r = slice(64 * g, 64 * g + 64)
                    for b in range(DEC_BATCH):
                        bank, c = (4 - 4 * g) + b // 2, (b % 2) * NKEY
                        q = q_s[r, b, :]
                        nc.tensor.matmul(ps[r, bank, c:c + WINDOW], q, kc[r, b, :], start=True, stop=True)
                        ins = nc.tensor.matmul(ps[r, bank, c + WINDOW:c + NKEY], q, kdup[r, g, SEQ:NT],
                                               start=True, stop=True)
                ins.then_inc(scores_done, 1)
                pe.wait_ge(prob_ready, N_HEADS + 1)
                for b in range(DEC_BATCH):
                    c = (b % 4) * P
                    nc.tensor.transpose(ps[:, 4 + b // 4, c:c + P], s_s[:, b, 0:WINDOW], ident[:, :])
                    ins = nc.tensor.transpose(ps[0:NS, 6 + b // 4, c:c + P], s_s[:, b, WINDOW:NKEY], ident[:, :])
                ins.then_inc(prob_turned, 1)

                jo = base["wo"]
                for m in range(2):
                    pe.wait_ge(lo_made, jo + m + 1)
                    half_job(jo + m, 0)
                    if m == 0:
                        sample_values()
                pe.wait_ge(att_ready, KD + 1)
                for m in range(2):
                    half_job(jo + m, 1).then_inc(job_done, 1)

            def half_job(j, c):
                for k in range(KD):
                    hi, lo = hid_tile(k)
                    for n, (a, b) in enumerate(((w_hi, hi), (w_hi, lo), (w_lo, hi))):
                        ins = nc.tensor.matmul(ps[:, 2 * (j % 2) + c, 0:288], wv(a, j % 2, k), halves(b, 288 * c, 288),
                                               start=k == n == 0, stop=k == KD - 1 and n == 2)
                return ins

            def sample_values():
                pe.wait_ge(pt_ready, N_HEADS + 1)
                for b in range(DEC_BATCH):
                    for h2 in range(2):
                        for g in range(N_KV):
                            out = ps[64 * h2:64 * h2 + 64, 1, 64 * b + 32 * g:64 * b + 32 * g + 32]
                            rows = lambda a: a[:, b, 64 * g:64 * g + 64].rearrange(
                                "p (m h t) -> p h m t", m=4, h=2)[:, h2]
                            nc.tensor.matmul(out, vc[:, b, 64 * g:64 * g + 64], rows(ptc), start=True, stop=False)
                            ins = nc.tensor.matmul(out, v_tok[0:NS, NBLK, 64 * g:64 * g + 64], rows(ptn[0:NS]),
                                                   start=False, stop=True)
                ins.then_inc(pv_done, 1)

            ffn(0, 0)
            recurrent()
            out_product(base["wout"], lambda k: (y_ready, k + 1))
            ffn(1, 2)
            key_value()
            turn_values()
            ffn(2, None)
            attention()
            out_product(base["wo"], None, first=2)
            ffn(3, 5)
            stats(6)

        @block.scalar
        def _(act):
            def prep(c, slot, par, kt, landed, used=None):
                act.wait_ge(raw_landed[slot], landed)
                if used is not None:
                    act.wait_ge(job_done, used)
                nc.scalar.activation(w_hi[:, par, 0:kt * P], raw[:, slot, 0:kt * P],
                                     ACT.Copy).then_inc(hi_made, 1)

            def prep_next(j):
                c = j + 2
                if c < NJ:
                    prep(c, c % 4, c % 2, KT[c], 16 * (c // 4 + 1), used=j + 1)

            def split_x(s, m, stat, x_job):
                if x_job is None:
                    act.wait_ge(x_loaded[m], 16)
                else:
                    act.wait_ge(dve_evac, evac(x_job))
                if s is not None:
                    nc.scalar.activation(xs_hi[:, m, :], x[:, m, :], ACT.Copy,
                                         scale=params[:, GAIN[s], m:m + 1]).then_inc(xs_hi_made, 1)
                if stat is not None:
                    if m >= 3:
                        act.wait_ge(ss_added, (KD - 1) * stat + m - 2)
                    nc.scalar.activation(ssum[:, :] if m == 0 else sq[:, m % 2, :], x[:, m, :],
                                         ACT.Square).then_inc(sq_made, 1)

            def root(stat):
                act.wait_ge(stat_sum, stat + 1)
                nc.scalar.activation(two(std), ps[:, 4:6, 0:288], ACT.Sqrt, bias=eps[:, 0:1],
                                     scale=1.0 / D_MODEL).then_inc(std_made, 1)

            def down(j0, s, stat):
                for m in range(KD):
                    prep_next(j0 + m)
                    if s is not None or stat is not None:
                        split_x(s, m, stat, j0 + m)

            def ffn(f, s, stat):
                for half in range(2):
                    j0 = base["gu", f, half]
                    u0 = FT * f + HF * half
                    turns = (GU_JOBS - 2) // 4

                    def unit(k, i, prep_a, prep_b):
                        u = 2 * i + (u0 + k)
                        par = k % 2
                        prep_a()
                        act.wait_ge(dve_evac, 4 * i + evac(j0 + 2 * k))
                        nc.scalar.activation(silu_t[:, par, :], gate_t[:, par, :], ACT.Silu).then_inc(silu_made, 1)
                        prep_b()
                        act.wait_ge(hid_made, u + 1)
                        nc.scalar.activation(act_hi[:, bass.ds((2 * i + k) * NT, NT)], hid[:, par, :],
                                             ACT.Copy).then_inc(hid_hi_made, 1)

                    with act.Fori(0, turns) as i:
                        def look(k):
                            c = j0 + k + 2
                            return lambda: prep(4 * i + c, c % 4, c % 2, KD, 64 * 0 + 16 * i + 16 * (c // 4 + 1),
                                                used=4 * i + (j0 + k + 1))
                        for k in range(2):
                            unit(k, i, look(2 * k), look(2 * k + 1))
                    for v in range(2 * turns, HF):
                        unit_static(j0 + 2 * v, u0 + v, v)
                    down(base["dn", f, half], s if half else None, stat if half else None)
                    if f == half == 0:
                        lru_constants()

            def unit_static(j, u, v):
                par = v % 2
                prep_next(j)
                act.wait_ge(dve_evac, evac(j))
                nc.scalar.activation(silu_t[:, par, :], gate_t[:, par, :], ACT.Silu).then_inc(silu_made, 1)
                prep_next(j + 1)
                act.wait_ge(hid_made, u + 1)
                nc.scalar.activation(act_hi[:, v * NT:(v + 1) * NT], hid[:, par, :],
                                     ACT.Copy).then_inc(hid_hi_made, 1)

            def lru_constants():
                act.wait_ge(lam_abs, 1)
                nc.scalar.activation(lam[:, 1, :], lam[:, 0, :], ACT.Exp, scale=-1.0).then_inc(lam_exp, 1)

            def recurrent():

                def round_conv(m):
                    act.wait_ge(xc_made, m + 1)
                    nc.scalar.activation(act_hi[:, conv_at(m):conv_at(m) + NP], xc[:, m % 4, :],
                                         ACT.Copy).then_inc(xc_hi_made, 1)

                def round_y(m):
                    act.wait_ge(y_made, m + 1)
                    nc.scalar.activation(act_tile(act_hi, m), tmp[:, m % 2, 0:NT], ACT.Copy).then_inc(y_hi_made, 1)

                def conv_input(m):
                    prep_next(base["xr", m])
                    round_conv(m)

                conv_input(0)
                conv_input(1)
                for n in range(KD // 2):
                    pair = (2 * n, 2 * n + 1)
                    ahead = n + 1 < KD // 2
                    if ahead:
                        conv_input(2 * n + 2)
                        prep_next(base["xr", 2 * n + 3])
                    j = base["ax", n]
                    if n:
                        act.wait_ge(h_made, 2 * n)
                    for q in range(4):
                        m, (dst, vec) = 2 * n + q // 2, ((rr, V_BA), (ii, V_BX))[q % 2]
                        if q < 3:
                            act.wait_ge(ax_done, 3 * n + q + 1)
                        else:
                            act.wait_ge(job_done, j + 1)
                        nc.scalar.activation(two(dst[:, m % 2, :]), ps2((j % 2, 2, 3, j % 2)[q], NP // 2), ACT.Sigmoid,
                                             bias=params[:, vec, m:m + 1]).then_inc(act_evac, 1)
                    prep_next(j)
                    if ahead:
                        round_conv(2 * n + 3)
                    act.wait_ge(decay_ready, 1)
                    act.wait_ge(act_evac, 4 * n + 4)
                    for m in pair:
                        nc.scalar.activation(tt[:, m % 2, :], rr[:, m % 2, :], ACT.Tanh,
                                             scale=ndecay[:, m:m + 1]).then_inc(tanh_made, 1)
                    act.wait_ge(tanh_made, 2 * n + 2)
                    for m in pair:
                        nc.scalar.activation(rr[:, m % 2, :], rr[:, m % 2, :], ACT.Exp,
                                             scale=decay[:, m:m + 1]).then_inc(a_made, 1)
                    if n:
                        act.wait_ge(y_ready, 2 * n)
                    for m in pair:
                        act.wait_ge(a_made, m + 1)
                        nc.scalar.activation(tmp[:, m % 2, :], rr[:, m % 2, :], ACT.Square).then_inc(a2_made, 1)
                    prep_next(base["gate", 2 * n])
                    for m in pair:
                        act.wait_ge(m2_made, m + 1)
                        nc.scalar.activation(tt[:, m % 2, :], tt[:, m % 2, :], ACT.Sqrt).then_inc(mult_made, 1)
                    for m in pair:
                        act.wait_ge(dve_evac, evac(base["gate", m]))
                        nc.scalar.activation(gate[:, m % 2, :], gate[:, m % 2, :],
                                             ACT.Gelu_apprx_tanh).then_inc(gate_out, 1)
                        if m == 2 * n:
                            prep_next(base["gate", m + 1])
                    round_y(2 * n)
                    round_y(2 * n + 1)

            def attention():
                act.wait_ge(misc_loaded, 32)
                for h in range(N_HEADS + 1):
                    if h < N_HEADS:
                        b0 = 4 if h % 2 == 0 else 0
                        o = 4 * (h % 2)
                        sp_ = ps[:, b0:b0 + 2, :].rearrange("p a n -> p (a n)")
                        act.wait_ge(max_made, h + 1)
                        nc.scalar.activation(sink_exp[:, o:o + 4], neg_max[:, o:o + 4], ACT.Exp,
                                             bias=sinks[:, h:h + 1])
                        if h >= 2:
                            act.wait_ge(prob_turned, h - 1)
                        for b in range(NBLK):
                            lo = 256 * b + (0 if b else P)
                            hi = 256 * (b + 1)
                            ins = nc.scalar.activation(prob[h % 2][:, lo:hi], sp_[:, lo:hi], ACT.Exp,
                                                       bias=neg_max[:, o + b:o + b + 1],
                                                       accum_out=row_sum[:, o + b:o + b + 1])
                        ins.then_inc(exp_made, 1)
                    if h >= 1:
                        q = h - 1
                        act.wait_ge(prob_turned, q + 1)
                        if q >= 2:
                            act.wait_ge(pv_done, q - 1)
                        nc.scalar.activation(pt[q % 2][:, 0:512], ps[:, 6, :], ACT.Copy)
                        nc.scalar.activation(pt[q % 2][:, 512:7 * P], ps[:, 7, 0:3 * P], ACT.Copy).then_inc(pt_ready, 1)
                    if h >= 3 and h % 2 == 1:
                        round_o((h - 3) // 2)
                round_o(KD - 1)
                act.wait_ge(max_made, N_HEADS + 1)
                nc.scalar.activation(sink_exp[:, 0:8], neg_max[:, 0:8], ACT.Exp, bias=sinks[:, N_HEADS:N_HEADS + 1])
                for b in range(DEC_BATCH):
                    ins = nc.scalar.activation(s_s[:, b, :], s_s[:, b, :], ACT.Exp, bias=neg_max[:, b:b + 1],
                                               accum_out=row_sum[:, b:b + 1])
                ins.then_inc(exp_made, 1)
                act.wait_ge(prob_turned, N_HEADS + 1)
                nc.scalar.activation(ptc[:, :, :].rearrange("p (a b) n -> p a (b n)", a=2), ps[:, 4:6, :], ACT.Copy)
                nc.scalar.activation(ptn[0:NS, :, :].rearrange("p (a b) n -> p a (b n)", a=2), ps[0:NS, 6:8, :],
                                     ACT.Copy).then_inc(pt_ready, 1)
                act.wait_ge(pv_done, N_HEADS + 1)
                nc.scalar.activation(sample_cols(act_hi), sample_o, ACT.Copy).then_inc(o_hi_made, 1)

            def round_o(m):
                act.wait_ge(pv_done, 2 * m + 2)
                nc.scalar.activation(act_hi[:, m * NT:m * NT + SEQ], ps[:, 2 + m % 2, :], ACT.Copy).then_inc(o_hi_made, 1)

            prep(0, 0, 0, KT[0], 16)
            act.wait_ge(consts_loaded, 48)
            for m in range(KD):
                split_x(0, m, None, None)
                if m == 3:
                    prep(1, 1, 1, KT[1], 16)
            for m in range(KD):
                split_x(None, m, 0, None)
            root(0)
            ffn(0, 1, 1)
            root(1)
            recurrent()
            down(base["wout"], 2, 2)
            root(2)
            ffn(1, 3, 3)
            root(3)
            j = base["kv"]
            prep_next(j)
            prep_next(j + 1)
            for m in range(KD):
                split_x(4, m, None, j - 1)
            ffn(2, 5, 4)
            root(4)
            for m in range(KD):
                prep_next(base["q"] + m)
            attention()
            down(base["wo"], 6, 5)
            root(5)
            ffn(3, None, 6)
            root(6)

        @block.vector
        def _(dve):
            chain = [0]

            def own(ins):
                chain[0] += 1
                ins.then_inc(dve_chain, 1)
                dve.wait_ge(dve_chain, chain[0])

            def prep(c, slot, par, kt):
                dve.wait_ge(hi_made, c + 1)
                nc.vector.tensor_tensor(w_lo[:, par, 0:kt * P], raw[:, slot, 0:kt * P],
                                        w_hi[:, par, 0:kt * P].bitcast(F32), ALU.subtract).then_inc(lo_made, 1)

            def prep_next(j):
                c = j + 2
                if c < NJ:
                    prep(c, c % 4, c % 2, KT[c])

            def split_x(s, m, stat):
                if s is not None:
                    dve.wait_ge(xs_hi_made, KD * s + m + 1)
                    nc.vector.scalar_tensor_tensor(xs_lo[:, m, :], x[:, m, :], params[:, GAIN[s], m:m + 1],
                                                   xs_hi[:, m, :].bitcast(F32), ALU.mult,
                                                   ALU.subtract).then_inc(xs_ready, 1)
                if stat is not None:
                    dve.wait_ge(sq_made, KD * stat + m + 1)
                    if m >= 2:
                        dve.wait_ge(ss_added, (KD - 1) * stat + m - 1)
                    if m >= 1:
                        nc.vector.tensor_tensor(ssum[:, :], ssum[:, :], sq[:, m % 2, :], ALU.add).then_inc(ss_added, 1)

            def invert(stat):
                dve.wait_ge(std_made, stat + 1)
                nc.vector.reciprocal(rstd[:, :], std).then_inc(rstd_made, 1)
                dve.wait_ge(rstd_made, stat + 1)

            def down(j0, s, stat, factor):
                for m in range(KD):
                    dve.wait_ge(job_done, j0 + m + 1)
                    dve.wait_ge(dve_evac, evac(j0 + m - 1))
                    nc.vector.scalar_tensor_tensor(two(x[:, m, :]), ps2((j0 + m) % 2), factor, two(x[:, m, :]),
                                                   ALU.mult, ALU.add).then_inc(dve_evac, 1)
                    prep_next(j0 + m)
                    split_x(s, m, stat)

            def ffn(f, s, stat):
                for half in range(2):
                    j0 = base["gu", f, half]
                    u0 = FT * f + HF * half
                    turns = (GU_JOBS - 2) // 4

                    def unit(j, u, up_evac, par, slot, tile_at, prep_a, prep_b):
                        dve.wait_ge(job_done, j + 1)
                        nc.vector.tensor_tensor(two(gate_t[:, par, :]), ps2(slot), two(rstd[:, :]),
                                                ALU.mult).then_inc(dve_evac, 1)
                        prep_a()
                        dve.wait_ge(job_done, j + 2)
                        nc.vector.tensor_tensor(two(up_t[:, par, :]), ps2(1 - slot), two(rstd[:, :]),
                                                ALU.mult).then_inc(dve_evac, 1)
                        dve.wait_ge(dve_evac, up_evac)
                        dve.wait_ge(silu_made, u + 1)
                        nc.vector.tensor_tensor(hid[:, par, :], up_t[:, par, :], silu_t[:, par, :],
                                                ALU.mult).then_inc(hid_made, 1)
                        prep_b()
                        dve.wait_ge(hid_hi_made, u + 1)
                        nc.vector.tensor_tensor(act_lo[:, tile_at], hid[:, par, :], act_hi[:, tile_at].bitcast(F32),
                                                ALU.subtract).then_inc(hid_ready, 1)

                    with dve.Fori(0, turns) as i:
                        for k in range(2):
                            ca, cb = j0 + 2 * k + 2, j0 + 2 * k + 3
                            unit(4 * i + (j0 + 2 * k), 2 * i + (u0 + k), 4 * i + evac(j0 + 2 * k + 1), k, j0 % 2,
                                 bass.ds((2 * i + k) * NT, NT),
                                 lambda: prep(4 * i + ca, ca % 4, ca % 2, KD),
                                 lambda: prep(4 * i + cb, cb % 4, cb % 2, KD))
                    for v in range(2 * turns, HF):
                        j = j0 + 2 * v
                        unit(j, u0 + v, evac(j + 1), v % 2, j0 % 2, slice(v * NT, (v + 1) * NT),
                             lambda: prep_next(j), lambda: prep_next(j + 1))
                    down(base["dn", f, half], s if half else None, stat if half else None, 0.5)
                    if f == half == 0:
                        lru_constants()

            def lru_constants():
                v = params[:, V_LAM, :]
                nc.vector.scalar_tensor_tensor(lam[:, 0, :], v, -1.0, v, ALU.mult, ALU.max).then_inc(lam_abs, 1)
                dve.wait_ge(lam_exp, 1)
                own(nc.vector.tensor_scalar(lam[:, 2, :], lam[:, 1, :], 2.0, None, ALU.add))
                own(nc.vector.reciprocal(lam[:, 3, :], lam[:, 2, :]))
                own(nc.vector.tensor_tensor(lam[:, 2, :], lam[:, 1, :], lam[:, 3, :], ALU.mult))
                own(nc.vector.tensor_tensor(lam[:, 3, :], lam[:, 2, :], lam[:, 2, :], ALU.mult))
                own(nc.vector.tensor_scalar(lam[:, 4, :], lam[:, 3, :], 1.0 / 17, None, ALU.mult))
                for k in range(7, 0, -1):
                    own(nc.vector.scalar_tensor_tensor(lam[:, 4, :], lam[:, 4, :], 1.0 / (2 * k + 1), lam[:, 3, :],
                                                       ALU.add, ALU.mult))
                own(nc.vector.scalar_tensor_tensor(lam[:, 5, :], lam[:, 4, :], 1.0, lam[:, 2, :], ALU.add, ALU.mult))
                own(nc.vector.tensor_scalar(lam[:, 4, :], v, -1.0, 0.0, ALU.mult, ALU.max))
                own(nc.vector.scalar_tensor_tensor(lam[:, 3, :], lam[:, 5, :], 2.0, lam[:, 4, :], ALU.mult, ALU.add))
                nc.vector.tensor_scalar(decay, lam[:, 3, :], -8.0, None, ALU.mult)
                nc.vector.tensor_scalar(ndecay, lam[:, 3, :], 8.0, None, ALU.mult).then_inc(decay_ready, 1)

            def recurrent():
                nc.vector.memset(xe[:, :, 0:PRE], 0.0)
                dve.wait_ge(state_loaded, 16)

                def evacuate_x(m, j):
                    r = m % 2
                    dve.wait_ge(job_done, j + 1)
                    if m >= 2:
                        dve.wait_ge(conv_saved, m - 1)
                    nc.vector.tensor_copy(seg(xe[:, r, :], 0, PRE),
                                          st_in[:, m, DEC_BATCH:].rearrange("p (b k) -> p b k", b=DEC_BATCH))
                    nc.vector.tensor_tensor(xe[:, r, PRE:S0].rearrange("p (a n) -> p a n", a=2),
                                            ps2(j % 2, 256), rstd[:, 0:SEQ].rearrange("p (a n) -> p a n", a=2),
                                            ALU.mult)
                    nc.vector.tensor_tensor(seg(xe[:, r, :], PRE, DEC_SEQ),
                                            ps[:, 2 * (j % 2) + 1, 256:256 + NS].rearrange("p (b t) -> p b t", b=DEC_BATCH),
                                            rstd[:, SEQ:NT].rearrange("p (b t) -> p b t", b=DEC_BATCH),
                                            ALU.mult).then_inc(dve_evac, 1)

                def conv(m):
                    r = m % 2
                    dve.wait_ge(dve_evac, evac(base["xr", m]))
                    if m >= 4:
                        dve.wait_ge(ix_made, m - 3)
                    own(nc.vector.tensor_scalar(xc[:, m % 4, :], xe[:, r, 0:NP], params[:, V_CW, m:m + 1],
                                                params[:, V_CB, m:m + 1], ALU.mult, ALU.add))
                    for k in range(1, CONV_W):
                        ins = nc.vector.scalar_tensor_tensor(xc[:, m % 4, :], xe[:, r, k:k + NP],
                                                             params[:, V_CW + k, m:m + 1], xc[:, m % 4, :],
                                                             ALU.mult, ALU.add)
                        if k < CONV_W - 1:
                            own(ins)
                    ins.then_inc(xc_made, 1)

                def rest_conv(m):
                    dve.wait_ge(xc_hi_made, m + 1)
                    t = slice(conv_at(m), conv_at(m) + NP)
                    nc.vector.tensor_tensor(act_lo[:, t], xc[:, m % 4, :], act_hi[:, t].bitcast(F32),
                                            ALU.subtract).then_inc(xc_ready, 1)

                def evacuate_gate(m, j):
                    dve.wait_ge(job_done, j + 1)
                    nc.vector.tensor_tensor(two(gate[:, m % 2, :]), ps2(j % 2), two(rstd[:, :]),
                                            ALU.mult).then_inc(dve_evac, 1)

                def square_of_multiplier(m):
                    r = m % 2
                    dve.wait_ge(tanh_made, m + 1)
                    dve.wait_ge(a2_made, m + 1)
                    nc.vector.scalar_tensor_tensor(tt[:, r, :], tmp[:, r, :], 1.0, tt[:, r, :], ALU.add,
                                                   ALU.mult).then_inc(m2_made, 1)

                def scan(m):
                    r = m % 2
                    dve.wait_ge(mult_made, m + 1)
                    dve.wait_ge(ix_made, m + 1)
                    dve.wait_ge(a_made, m + 1)
                    own(nc.vector.tensor_tensor(ii[:, r, :], ii[:, r, :], tt[:, r, :], ALU.mult))
                    before = slice(S0 - 1, S0 - 1 + SEG * (DEC_BATCH - 1) + 1, SEG)
                    nc.vector.memset(rr[:, r, before], 0.0)
                    own(nc.vector.tensor_copy(ii[:, r, before], st_in[:, m, 0:DEC_BATCH]))
                    if m >= 2:
                        dve.wait_ge(h_saved, m - 1)
                    nc.vector.tensor_tensor_scan(hh[:, r, :], rr[:, r, :], ii[:, r, :], 0.0, ALU.mult,
                                                 ALU.add).then_inc(h_made, 1)

                def gated(m):
                    r = m % 2
                    dve.wait_ge(h_made, m + 1)
                    dve.wait_ge(gate_out, m + 1)
                    nc.vector.tensor_tensor(tmp[:, r, 0:SEQ], hh[:, r, 0:SEQ], gate[:, m % 2, 0:SEQ], ALU.mult)
                    nc.vector.tensor_tensor(tmp[:, r, SEQ:NT].rearrange("p (b t) -> p b t", b=DEC_BATCH),
                                            hseg(hh[:, r, :]),
                                            gate[:, m % 2, SEQ:NT].rearrange("p (b t) -> p b t", b=DEC_BATCH),
                                            ALU.mult).then_inc(y_made, 1)

                def rest_y(m):
                    dve.wait_ge(y_hi_made, m + 1)
                    nc.vector.tensor_tensor(act_tile(act_lo, m), tmp[:, m % 2, 0:NT],
                                            act_tile(act_hi, m).bitcast(F32), ALU.subtract).then_inc(y_ready, 1)

                def conv_input(m):
                    evacuate_x(m, base["xr", m])
                    if m % 2:
                        rest_conv(m - 1)
                    prep_next(base["xr", m])
                    conv(m)

                conv_input(0)
                conv_input(1)
                rest_conv(1)
                for n in range(KD // 2):
                    a, b = 2 * n, 2 * n + 1
                    if n + 1 < KD // 2:
                        conv_input(a + 2)
                        conv_input(b + 2)
                    prep_next(base["ax", n])
                    if n + 1 < KD // 2:
                        rest_conv(b + 2)
                    square_of_multiplier(a)
                    square_of_multiplier(b)
                    evacuate_gate(a, base["gate", a])
                    prep_next(base["gate", a])
                    scan(a)
                    evacuate_gate(b, base["gate", b])
                    prep_next(base["gate", b])
                    gated(a)
                    scan(b)
                    rest_y(a)
                    gated(b)
                    rest_y(b)

            def hseg(v):
                return v[:, S0 - PRE:NP].rearrange("p (b s) -> p b s", b=DEC_BATCH)[:, :, PRE:SEG]

            def key_value():
                j = base["kv"]
                dve.wait_ge(job_done, j + 1)
                for g in range(N_KV):
                    for p in range(2):
                        ins = nc.vector.tensor_tensor(
                            two(kdup[64 * p:64 * p + 64, g, :]), ps[64 * g:64 * g + 64, 2 * (j % 2):2 * (j % 2) + 2, 0:288],
                            two(rstd[64 * p:64 * p + 64, :]), ALU.mult)
                ins.then_inc(dve_evac, 1)
                prep_next(j)
                dve.wait_ge(job_done, j + 2)
                nc.vector.tensor_tensor(two(v_t), ps2((j + 1) % 2), two(rstd[:, :]), ALU.mult).then_inc(dve_evac, 1)
                prep_next(j + 1)
                for m in range(KD):
                    split_x(4, m, None)
                dve.wait_ge(v_turned, 1)
                nc.vector.tensor_copy(v_tok[:, 0:NBLK, :].rearrange("p b n -> p (b n)"), ps[:, 6, :])
                nc.vector.tensor_copy(v_tok[0:NS, NBLK, :], ps[0:NS, 7, 0:P]).then_inc(v_tok_made, 1)

            def attention():
                j0 = base["q"]
                scale = HEAD_DIM ** -0.5
                for m in range(KD):
                    j = j0 + m
                    g = m // 4
                    dve.wait_ge(job_done, j + 1)
                    nc.vector.scalar_tensor_tensor(q_p[:, m, :].rearrange("p (a n) -> p a n", a=2), ps2(j % 2, 256), scale,
                                                   rstd[:, 0:SEQ].rearrange("p (a n) -> p a n", a=2),
                                                   ALU.mult, ALU.mult)
                    for p in range(2):
                        hh_ = (2 * (m % 4) + p) * DEC_SEQ
                        by_seq = lambda v: v.rearrange("p (b t) -> p b t", b=DEC_BATCH)
                        ins = nc.vector.scalar_tensor_tensor(
                            q_s[64 * g:64 * g + 64, :, hh_:hh_ + DEC_SEQ],
                            by_seq(ps[64 * p:64 * p + 64, 2 * (j % 2) + 1, 256:256 + NS]), scale,
                            by_seq(rstd[64 * g:64 * g + 64, SEQ:NT]), ALU.mult, ALU.mult)
                    ins.then_inc(dve_evac, 1)
                    prep_next(j)

                dve.wait_ge(att_loaded, 16 * 5)
                dve.wait_ge(misc_loaded, 32)
                for h in range(N_HEADS + 1):
                    if h < N_HEADS:
                        slope = 2.0 ** (-8.0 * (h + 1) / N_HEADS)
                        o = 4 * (h % 2)
                        b0 = 4 if h % 2 == 0 else 0
                        s0 = ps[:, b0, P:2 * P]
                        s3 = ps[:, b0:b0 + 2, :].rearrange("p a n -> p (a n)")[:, 256:1024].rearrange(
                            "p (b n) -> p b n", b=3)
                        dve.wait_ge(scores_done, h + 1)
                        nc.vector.scalar_tensor_tensor(s0, dist[:, P:2 * P], slope, s0, ALU.mult, ALU.add)
                        own(nc.vector.scalar_tensor_tensor(s3, dist.unsqueeze(1).broadcast_to([P, 3, 256]), slope, s3,
                                                           ALU.mult, ALU.add))
                        nc.vector.tensor_reduce(neg_max[:, o:o + 1], s0, AX_X, ALU.max)
                        own(nc.vector.tensor_reduce(neg_max[:, o + 1:o + 4], s3, AX_X, ALU.max))
                        nc.vector.tensor_scalar(neg_max[:, o:o + 4], neg_max[:, o:o + 4], sinks[:, h:h + 1], -1.0,
                                                ALU.max, ALU.mult).then_inc(max_made, 1)
                    if h >= 1:
                        q = h - 1
                        o = 4 * (q % 2)
                        dve.wait_ge(exp_made, q + 1)
                        own(nc.vector.tensor_tensor(inv_den[:, o:o + 4], row_sum[:, o:o + 4], sink_exp[:, o:o + 4], ALU.add))
                        own(nc.vector.reciprocal(inv_den[:, o:o + 4], inv_den[:, o:o + 4]))
                        for b in range(NBLK):
                            t = slice(256 * b + (0 if b else P), 256 * (b + 1))
                            ins = nc.vector.tensor_scalar(prob[q % 2][:, t], prob[q % 2][:, t],
                                                          inv_den[:, o + b:o + b + 1], None, ALU.mult)
                        ins.then_inc(prob_ready, 1)
                    if h >= 4 and h % 2 == 0:
                        rest_o((h - 4) // 2)
                rest_o(KD - 1)
                dve.wait_ge(scores_done, N_HEADS + 1)
                for g in range(N_KV):
                    r = slice(64 * g, 64 * g + 64)
                    b0 = 4 - 4 * g
                    pairs = lambda v: v.rearrange("p (c a) n -> p c a n", a=2)
                    src = ps[r, b0:b0 + 4, 0:2 * NKEY].rearrange("p c (a n) -> p c a n", a=2)
                    dst = pairs(s_s[r])
                    nc.vector.tensor_tensor(dst[:, :, :, 0:WINDOW], src[:, :, :, 0:WINDOW],
                                            bias_c[r, :].unsqueeze(1).unsqueeze(1).broadcast_to([64, 4, 2, WINDOW]), ALU.add)
                    ins = nc.vector.tensor_tensor(dst[:, :, :, WINDOW:NKEY], src[:, :, :, WINDOW:NKEY],
                                                  pairs(bias_n[r]), ALU.add)
                own(ins)
                own(nc.vector.tensor_reduce(neg_max[:, 0:8], s_s, AX_X, ALU.max))
                nc.vector.tensor_scalar(neg_max[:, 0:8], neg_max[:, 0:8], sinks[:, N_HEADS:N_HEADS + 1], -1.0,
                                        ALU.max, ALU.mult).then_inc(max_made, 1)
                dve.wait_ge(exp_made, N_HEADS + 1)
                own(nc.vector.tensor_tensor(inv_den[:, 0:8], row_sum[:, 0:8], sink_exp[:, 0:8], ALU.add))
                own(nc.vector.reciprocal(inv_den[:, 0:8], inv_den[:, 0:8]))
                nc.vector.tensor_tensor(s_s, s_s, inv_den[:, 0:8].unsqueeze(2).broadcast_to([P, DEC_BATCH, NKEY]),
                                        ALU.mult).then_inc(prob_ready, 1)
                dve.wait_ge(o_hi_made, KD + 1)
                nc.vector.tensor_tensor(sample_cols(act_lo), sample_o, sample_cols(act_hi).bitcast(F32),
                                        ALU.subtract).then_inc(att_ready, 1)

            def rest_o(m):
                dve.wait_ge(o_hi_made, m + 1)
                t = slice(m * NT, m * NT + SEQ)
                nc.vector.tensor_tensor(act_lo[:, t], ps[:, 2 + m % 2, :], act_hi[:, t].bitcast(F32),
                                        ALU.subtract).then_inc(att_ready, 1)

            prep(0, 0, 0, KT[0])
            for m in range(KD):
                split_x(0, m, None)
                if m == 3:
                    prep(1, 1, 1, KT[1])
            for m in range(KD):
                split_x(None, m, 0)
            invert(0)
            ffn(0, 1, 1)
            invert(1)
            recurrent()
            down(base["wout"], 2, 2, 1.0)
            invert(2)
            ffn(1, 3, 3)
            invert(3)
            key_value()
            ffn(2, 5, 4)
            invert(4)
            attention()
            down(base["wo"], 6, 5, 1.0)
            invert(5)
            ffn(3, None, 6)
            invert(6)
            for m in range(KD):
                nc.vector.scalar_tensor_tensor(x[:, m, :], x[:, m, :], params[:, V_FIN, m:m + 1], rstd[:, :],
                                               ALU.mult, ALU.mult).then_inc(y_out, 1)

        @block.gpsimd
        def _(pool):
            pool.dma_start(ident[:, :], A["ident"]).then_inc(misc_loaded, 16)
            pool.dma_start(sinks[:, :], A["sinks"]).then_inc(misc_loaded, 16)
            pool.dma_start(A["ck_out"], A["cache_k"][:, DEC_SEQ:, :]).then_inc(side_stored, 16)
            pool.dma_start(A["cv_out"], A["cache_v"][:, DEC_SEQ:, :]).then_inc(side_stored, 16)
            pool.dma_start(st_in, A["st_in"]).then_inc(state_loaded, 16)

            def save_conv(m):
                r = m % 2
                pool.wait_ge(dve_evac, evac(base["xr", m]))
                nc.gpsimd.tensor_copy(st_out[:, m, 1:1 + PRE], xe[:, r, SEQ:SEQ + PRE])
                nc.gpsimd.tensor_copy(
                    st_out[:, m, 1 + PRE + DEC_BATCH:].rearrange("p (b k) -> p b k", b=DEC_BATCH),
                    seg(xe[:, r, :], DEC_SEQ, PRE)).then_inc(conv_saved, 1)

            def save_h(m):
                pool.wait_ge(h_made, m + 1)
                last = SEQ + PRE + DEC_SEQ - 1
                nc.gpsimd.tensor_copy(st_out[:, m, 0:1], hh[:, m % 2, SEQ - 1:SEQ])
                nc.gpsimd.tensor_copy(
                    st_out[:, m, 1 + PRE:1 + PRE + DEC_BATCH],
                    hh[:, m % 2, last:last + SEG * (DEC_BATCH - 1) + 1:SEG]).then_inc(h_saved, 1)

            save_conv(0)
            save_conv(1)
            for n in range(KD // 2):
                if n + 1 < KD // 2:
                    save_conv(2 * n + 2)
                    save_conv(2 * n + 3)
                for m in (2 * n, 2 * n + 1):
                    pool.wait_ge(act_evac, 2 * m + 2)
                    pool.wait_ge(xc_made, m + 1)
                    nc.gpsimd.tensor_tensor(ii[:, m % 2, :], ii[:, m % 2, :], xc[:, m % 4, :],
                                            ALU.mult).then_inc(ix_made, 1)
                save_h(2 * n)
                save_h(2 * n + 1)
            pool.wait_ge(h_saved, KD)
            pool.wait_ge(conv_saved, KD)
            pool.dma_start(A["st_out"], st_out).then_inc(side_stored, 16)
            pool.wait_ge(dve_evac, evac(base["kv"] + 1))
            keep = slice(SEQ - WINDOW, NT)
            for g in range(N_KV):
                pool.dma_start(A["k_new"][64 * g:64 * g + 64, :], kdup[64 * g:64 * g + 64, g, keep]).then_inc(side_stored, 16)
            pool.dma_start(A["v_new"], v_t[:, keep]).then_inc(side_stored, 16)
            pool.wait_ge(side_stored, 16 * 6)
            pool.wait_ge(v_turned, 1)
            pool.dma_start(dist, A["dist"]).then_inc(att_loaded, 16)
            pool.dma_start(bias_c, A["bias_c"]).then_inc(att_loaded, 16)
            pool.dma_start(bias_n, A["bias_n"]).then_inc(att_loaded, 16)
            pool.dma_start(kc, A["k_cT"]).then_inc(att_loaded, 16)
            pool.dma_start(vc, A["cache_v"].rearrange("b s n -> s b n")).then_inc(att_loaded, 16)


def kernel(**inputs):
    import numpy as np
    import concourse.bacc as bacc
    from concourse.bass_utils import run_bass_kernel_spmd

    a = {k: np.asarray(v) for k, v in inputs.items()}
    f32 = np.float32

    def chunks(w):
        k, n = w.shape
        return w.reshape(k // P, P, n // P, P).transpose(2, 1, 0, 3).reshape(n // P, P, k)

    gu, dn = [], []
    for l in range(2):
        for which in ("ffn1", "ffn2"):
            g = chunks(a[f"{which}_w_gu"][l]).reshape(2, FT, P, D_MODEL)
            gu.append(g.transpose(1, 0, 2, 3).reshape(2 * FT, P, D_MODEL))
            w = a[f"{which}_w_down"][l]
            for half in range(2):
                dn.append(chunks(w[half * HF * P:(half + 1) * HF * P]))
    w_in = chunks(a["rg_w_in"][0])
    ax = np.stack([a["rg_w_a"][0], a["rg_w_x"][0]])
    ax = ax.reshape(2, 4, 2, P, 2, P).transpose(1, 3, 4, 0, 2, 5).reshape(4, P, D_MODEL)
    rec = [w_in[KD:KD + 2]]
    for n in range(KD // 2):
        rec += [w_in[KD + 2 * n + 2:KD + 2 * n + 4], ax[n:n + 1], w_in[2 * n:2 * n + 2]]

    q, c = np.arange(P)[:, None], np.arange(2 * WINDOW)[None]
    diff = WINDOW + q - c
    dist = np.where((diff >= 0) & (diff < WINDOW), -diff, -1e33).astype(f32)
    head, t = np.arange(P)[:, None] // DEC_SEQ, np.arange(P)[:, None] % DEC_SEQ
    slope = np.exp2(-8.0 * (head + 1) / N_HEADS)
    s = np.arange(WINDOW)[None]
    bias_c = np.where(s > t, -slope * (WINDOW + t - s), -1e30).astype(f32)
    b, tk = np.arange(NS)[None] // DEC_SEQ, np.arange(NS)[None] % DEC_SEQ
    bias_n = np.stack([np.where((b == i) & (tk <= t), -slope * (t - tk), -1e30) for i in range(DEC_BATCH)],
                      axis=1).astype(f32)

    vecs = [a["ffn1_norm"][0], a["ffn1_norm"][1], a["mix_norm"][0], a["mix_norm"][1], a["ffn2_norm"][0],
            a["ffn2_norm"][1], a["kv_norm"], a["final_norm"], *a["rg_conv_w"][0], a["rg_conv_b"][0],
            a["rg_b_a"][0], a["rg_b_x"][0], a["rg_lambda"][0]]
    sinks = a["attn_sinks"][0]
    states = np.concatenate([a["state_rg_h"][0].T, a["state_rg_conv"][0].reshape(-1, D_MODEL).T], axis=1)
    arrays = {
        "xT": np.concatenate([a["x_prompt"][0], a["x_sample"].reshape(NS, D_MODEL)]).T.reshape(KD, P, NT),
        "params": np.stack(vecs).reshape(N_VEC, KD, P).transpose(2, 0, 1),
        "ones": np.ones((P, P), f32),
        "ident": np.eye(P, dtype=f32),
        "eps": np.full((P, 1), EPS, f32),
        "sinks": np.concatenate([np.broadcast_to(sinks, (P, N_HEADS)), np.repeat(sinks, DEC_SEQ)[:, None]], axis=1),
        "st_in": states.reshape(KD, P, -1).transpose(1, 0, 2),
        "w_gu": np.concatenate(gu),
        "w_dn": np.concatenate(dn),
        "w_rec": np.concatenate(rec),
        "w_out": chunks(a["rg_w_out"][0]),
        "w_kv": chunks(a["w_kv"]),
        "w_q": chunks(a["attn_w_q"][0]),
        "w_o": chunks(a["attn_w_o"][0]),
        "cache_k": a["cache_k"].reshape(DEC_BATCH, WINDOW, P),
        "cache_v": a["cache_v"].reshape(DEC_BATCH, WINDOW, P),
        "k_cT": a["cache_k"].reshape(DEC_BATCH, WINDOW, P).transpose(2, 0, 1),
        "dist": dist, "bias_c": bias_c, "bias_n": bias_n,
    }
    outs = {"yT": (KD, P, NT), "st_out": (P, KD, NSTATE), "k_new": (P, WINDOW + NS), "v_new": (P, WINDOW + NS),
            "ck_out": (DEC_BATCH, WINDOW - DEC_SEQ, P), "cv_out": (DEC_BATCH, WINDOW - DEC_SEQ, P)}

    nc = bacc.Bacc("TRN2", target_bir_lowering=False, num_devices=1)
    A = {}
    for name, v in arrays.items():
        arrays[name] = np.ascontiguousarray(v)
        A[name] = nc.dram_tensor(name, v.shape, F32, kind="ExternalInput").ap()
    for name, shape in outs.items():
        A[name] = nc.dram_tensor(name, shape, F32, kind="ExternalOutput").ap()
    build(nc, A)
    r = run_bass_kernel_spmd(nc, [arrays], core_ids=[0]).results[0]

    y = r["yT"].reshape(D_MODEL, NT).T
    st = r["st_out"].transpose(1, 0, 2).reshape(D_MODEL, NSTATE).T
    new = {k: r[f"{k}_new"].T.reshape(WINDOW + NS, N_KV, HEAD_DIM) for k in "kv"}
    cache = {k: r[f"c{k}_out"].reshape(DEC_BATCH, WINDOW - DEC_SEQ, N_KV, HEAD_DIM) for k in "kv"}
    rolled = {k: np.concatenate([cache[k], new[k][WINDOW:].reshape(DEC_BATCH, DEC_SEQ, N_KV, HEAD_DIM)], axis=1)
              for k in "kv"}
    c0, c1, c2 = 1, 1 + PRE, 1 + PRE + DEC_BATCH
    out = (y[None, :SEQ], y[SEQ:].reshape(DEC_BATCH, DEC_SEQ, D_MODEL),
           st[None, 0:c0], st[None, None, c0:c1], new["k"][None, :WINDOW], new["v"][None, :WINDOW],
           st[None, c1:c2], st[c2:].reshape(1, DEC_BATCH, PRE, D_MODEL), rolled["k"], rolled["v"])
    return tuple(np.ascontiguousarray(o) for o in out)
```

```python
from contextlib import ExitStack

import concourse.bass as bass
from concourse import mybir

F32 = mybir.dt.float32
F32R = mybir.dt.float32r
ALU = mybir.AluOpType
ACT = mybir.ActivationFunctionType
AX_X = mybir.AxisListType.X

P = 128
D_MODEL, SEQ, DEC_BATCH, DEC_SEQ = 1024, 512, 8, 8
NS = DEC_BATCH * DEC_SEQ
NT = SEQ + NS
HT = NT // 2
KD = D_MODEL // P
FT = 22
HF = FT // 2
CONV_W = 4
HEAD_DIM, N_HEADS, N_KV = 64, 16, 2
WINDOW = 128
NBLK = SEQ // WINDOW
NKEY = WINDOW + NS
EPS = 1e-6

PRE = CONV_W - 1
SEG = PRE + DEC_SEQ
NE = PRE + SEQ + DEC_BATCH * SEG
NP = NE - PRE
S0 = SEQ + PRE
NSTATE = 1 + PRE + DEC_BATCH * (1 + PRE)

FIRST = 2 * P

(V_F1A, V_F1B, V_MA, V_MB, V_F2A, V_F2B, V_KV, V_FIN,
 V_CW, V_CB, V_BA, V_BX, V_LAM, N_VEC) = (0, 1, 2, 3, 4, 5, 6, 7, 8, 12, 13, 14, 15, 16)

GU_JOBS, DN_JOBS = 2 * HF, KD
N_FFN = 2 * (GU_JOBS + DN_JOBS)


def plan():
    kt, act, base = [], [], {}

    def ffn(f):
        for half in range(2):
            base["gu", f, half] = len(kt)
            kt.extend([KD] * GU_JOBS)
            base["dn", f, half] = len(kt)
            kt.extend([HF] * DN_JOBS)

    ffn(0)
    def rec(name, *key):
        base[(name, *key)] = len(kt)
        kt.append(KD)

    base["rec"] = len(kt)
    rec("xr", 0)
    rec("xr", 1)
    for n in range(KD // 2):
        if n + 1 < KD // 2:
            rec("xr", 2 * n + 2)
            rec("xr", 2 * n + 3)
        act.append(len(kt))
        rec("ax", n)
        rec("gate", 2 * n)
        rec("gate", 2 * n + 1)
    base["wout"] = len(kt)
    kt.extend([KD] * KD)
    ffn(1)
    base["kv"] = len(kt)
    kt.extend([KD] * 2)
    ffn(2)
    base["q"] = len(kt)
    kt.extend([KD] * KD)
    base["wo"] = len(kt)
    kt.extend([KD] * KD)
    ffn(3)
    return base, kt, act


def build(nc, A):
    base, KT, ACT_JOBS = plan()
    NJ = len(KT)
    act_jobs = set(ACT_JOBS)
    CH = HF * P

    with ExitStack() as ctx:
        def sb(name, shape, dt=F32):
            return ctx.enter_context(nc.sbuf_tensor(name, shape, dt))

        def sem(name):
            return ctx.enter_context(nc.semaphore(name))

        x = sb("x", [P, KD, NT])
        xs_hi = sb("xs_hi", [P, KD, NT], F32R)
        xs_lo = sb("xs_lo", [P, KD, NT], F32R)
        act_hi = sb("act_hi", [P, HF * NT], F32R)
        act_lo = sb("act_lo", [P, HF * NT], F32R)
        raw = sb("raw", [P, 4, CH])
        w_hi = sb("w_hi", [P, 2, CH], F32R)
        w_lo = sb("w_lo", [P, 2, CH], F32R)
        rstd = sb("rstd", [P, NT])
        ssum = sb("ssum", [P, NT])
        sq = sb("sq", [P, 2, NT])
        std = sq[:, 0, :]
        params = sb("params_sb", [P, N_VEC, KD])
        ones = sb("ones_sb", [P, P])
        ident = sb("ident_sb", [P, P])
        eps = sb("eps_sb", [P, 1])
        sinks = sb("sinks_sb", [P, N_HEADS + 1])
        AR = 12700
        arena = sb("arena", [P, AR])
        ps = ctx.enter_context(nc.psum_tensor("ps", [P, 8, 512], F32))

        at = [0]

        def take(n):
            v = arena[:, at[0]:at[0] + n]
            at[0] += n
            assert at[0] <= AR, at[0]
            return v

        gate_t = take(2 * NT).rearrange("p (a n) -> p a n", a=2)
        silu_t = take(2 * NT).rearrange("p (a n) -> p a n", a=2)
        up_t = take(2 * NT).rearrange("p (a n) -> p a n", a=2)
        hid = take(2 * NT).rearrange("p (a n) -> p a n", a=2)
        first_sq = arena[:, 0:KD * NT].rearrange("p (m n) -> p m n", m=KD)
        at[0] = 0
        xe = take(2 * NE).rearrange("p (a n) -> p a n", a=2)
        xc = take(4 * NP).rearrange("p (a n) -> p a n", a=4)
        rr = take(2 * NP).rearrange("p (a n) -> p a n", a=2)
        ii = take(2 * NP).rearrange("p (a n) -> p a n", a=2)
        tt = take(2 * NP).rearrange("p (a n) -> p a n", a=2)
        tmp = take(2 * NP).rearrange("p (a n) -> p a n", a=2)
        hh = take(2 * NP).rearrange("p (a n) -> p a n", a=2)
        gate = take(2 * NT).rearrange("p (a n) -> p a n", a=2)
        st_in = take(KD * DEC_BATCH * (1 + PRE)).rearrange("p (m s) -> p m s", m=KD)
        st_out = take(KD * NSTATE).rearrange("p (m s) -> p m s", m=KD)
        lam = take(8 * KD).rearrange("p (a m) -> p a m", a=8)
        decay = lam[:, 6, :]
        ndecay = lam[:, 7, :]
        at[0] = 8 * NT
        kdup = take(N_KV * NT).rearrange("p (g n) -> p g n", g=N_KV)
        v_tok = take((NBLK + 1) * P).rearrange("p (b n) -> p b n", b=NBLK + 1)
        v_t = take(NT)
        vkeep = at[0]
        at[0] = 0
        q_p = take(KD * SEQ).rearrange("p (m n) -> p m n", m=KD)
        q_s = take(8 * NS).rearrange("p (b n) -> p b n", b=DEC_BATCH)
        assert at[0] <= 8 * NT
        at[0] = vkeep - NT
        dist = take(2 * WINDOW)
        bias_c = take(WINDOW)
        bias_n = take(DEC_BATCH * NS).rearrange("p (b n) -> p b n", b=DEC_BATCH)
        kc = take(DEC_BATCH * WINDOW).rearrange("p (b n) -> p b n", b=DEC_BATCH)
        vc = take(DEC_BATCH * P).rearrange("p (b n) -> p b n", b=DEC_BATCH)
        small = take(64)
        alibi = ssum[:, 0:512].rearrange("p (a n) -> p a n", a=2)
        prob = [take(4 * 256), take(4 * 256)]
        pt = [take(7 * P), sq.rearrange("p a n -> p (a n)")[:, 0:7 * P]]
        s_s = q_p[:, 0:3, :].rearrange("p m n -> p (m n)").rearrange("p (b n) -> p b n", b=DEC_BATCH)
        ptc = q_p[:, 3:5, :].rearrange("p m n -> p (m n)").rearrange("p (b n) -> p b n", b=DEC_BATCH)
        ptn = q_p[:, 5:7, :].rearrange("p m n -> p (m n)").rearrange("p (b n) -> p b n", b=DEC_BATCH)
        neg_max, row_sum, sink_exp, inv_den = (small[:, 8 * i:8 * i + 8] for i in range(4))

        x_loaded = [sem(f"x_loaded{m}") for m in range(KD)]
        params_loaded = sem("params_loaded")
        consts_loaded = sem("consts_loaded")
        misc_loaded = sem("misc_loaded")
        state_loaded = sem("state_loaded")
        att_loaded = sem("att_loaded")
        raw_landed = [sem(f"raw_landed{i}") for i in range(4)]
        stored = sem("stored")
        side_stored = sem("side_stored")
        first_landed = sem("first_landed")
        first_hi_made = sem("first_hi_made")
        first_lo_made = sem("first_lo_made")
        hi_made = sem("hi_made")
        lo_made = sem("lo_made")
        job_done = sem("job_done")
        dve_evac = sem("dve_evac")
        act_evac = sem("act_evac")
        xs_hi_made = sem("xs_hi_made")
        xs_ready = sem("xs_ready")
        sq_made = sem("sq_made")
        ss_added = sem("ss_added")
        first_sum_012 = sem("first_sum_012")
        first_sq_made = sem("first_sq_made")
        first_added = sem("first_added")
        stat_sum = sem("stat_sum")
        std_made = sem("std_made")
        rstd_made = sem("rstd_made")
        silu_made = sem("silu_made")
        hid_made = sem("hid_made")
        hid_hi_made = sem("hid_hi_made")
        hid_ready = sem("hid_ready")
        dve_chain = sem("dve_chain")
        pool_chain = sem("pool_chain")
        lam_exp = sem("lam_exp")
        lam_abs = sem("lam_abs")
        xc_made = sem("xc_made")
        xc_hi_made = sem("xc_hi_made")
        xc_ready = sem("xc_ready")
        conv_saved = sem("conv_saved")
        gate_out = sem("gate_out")
        ix_made = sem("ix_made")
        decay_ready = sem("decay_ready")
        tanh_made = sem("tanh_made")
        a_made = sem("a_made")
        a2_made = sem("a2_made")
        ax_done = sem("ax_done")
        m2_made = sem("m2_made")
        mult_made = sem("mult_made")
        h_made = sem("h_made")
        h_saved = sem("h_saved")
        y_made = sem("y_made")
        y_hi_made = sem("y_hi_made")
        y_ready = sem("y_ready")
        v_tile_used = sem("v_tile_used")
        k_dup_made = sem("k_dup_made")
        v_turned = sem("v_turned")
        sample_scored = sem("sample_scored")
        bias_added = sem("bias_added")
        sample_max = sem("sample_max")
        sample_exp = sem("sample_exp")
        sample_prob = sem("sample_prob")
        sample_turned = sem("sample_turned")
        sample_pt = sem("sample_pt")
        sample_pv = sem("sample_pv")
        v_tok_made = sem("v_tok_made")
        alibi_made = sem("alibi_made")
        scores_done = sem("scores_done")
        max_made = sem("max_made")
        exp_made = sem("exp_made")
        prob_ready = sem("prob_ready")
        prob_turned = sem("prob_turned")
        pt_ready = sem("pt_ready")
        pv_done = sem("pv_done")
        o_hi_made = sem("o_hi_made")
        att_ready = sem("att_ready")
        y_out = sem("y_out")
        y_out_pool = sem("y_out_pool")
        x_scaled = sem("x_scaled")

        GAIN = [V_F1A, V_MA, V_F2A, V_KV, V_F1B, V_MB, V_F2B]
        FFN_INPUT = [0, 2, 4, 6]
        Y_DVE = 5
        Y_STORES = ((0, 2), (2, Y_DVE), (Y_DVE, KD))
        Y_ORDER = (0, 5, 1, 2, 6, 3, 4, 7)
        dve_done = [0]
        for j in range(NJ):
            dve_done.append(dve_done[-1] + (j not in act_jobs))

        def evac(j):
            return dve_done[j + 1]

        def slot_free(pe, j):
            if j < 2:
                return
            if j - 2 in act_jobs:
                pe.wait_ge(act_evac, 4 * (j - 1 - dve_done[j - 1]))
            else:
                pe.wait_ge(dve_evac, dve_done[j - 1])

        def wv(s, r, k):
            return s[:, r, k * P:(k + 1) * P]

        def act_tile(a, k):
            return a[:, k * NT:(k + 1) * NT]

        def conv_at(m):
            return HF * NT - NP * (2, 1, 4, 3)[m % 4]

        def halves(ap, at_, w):
            return ap[:, at_:at_ + w]

        EVEN = ((0, HT), (HT, HT))
        BLOCKS = ((0, 256), (256, 320))
        PADDED = ((0, NP // 2), (NP // 2, NP // 2))

        def ps2(slot, n=HT):
            return ps[:, 2 * slot:2 * slot + 2, 0:n]

        def two(ap, n=2):
            return ap.rearrange("p (a n) -> p a n", a=n)

        def seg(ap, first, n):
            return ap[:, S0:S0 + DEC_BATCH * SEG].rearrange(
                "p (b s) -> p b s", b=DEC_BATCH)[:, :, first:first + n]

        def sample_cols(a):
            return a[:, 0:KD * NT].rearrange("p (m n) -> p m n", m=KD)[:, :, SEQ:NT].rearrange(
                "p m (b t) -> p m b t", b=DEC_BATCH)

        sample_o = ps[:, 1, :].rearrange("p (b m t) -> p m b t", b=DEC_BATCH, m=KD)

        block = ctx.enter_context(nc.Block())

        def load(sp, slot, src, kt):
            sp.dma_start(raw[:, slot, 0:kt * P], src).then_inc(raw_landed[slot], 16)

        @block.sync
        def _(sp):
            sp.dma_start(raw[:, 0, 0:FIRST], A["w_gu"][0][:, 0:FIRST]).then_inc(first_landed, 16)
            sp.dma_start(x[:, 0, :], A["xT"][0]).then_inc(x_loaded[0], 16)
            sp.dma_start(raw[:, 0, FIRST:D_MODEL], A["w_gu"][0][:, FIRST:]).then_inc(raw_landed[0], 16)
            for m in range(2, KD, 2):
                sp.dma_start(x[:, m, :], A["xT"][m]).then_inc(x_loaded[m], 16)

            def free(c):
                sp.wait_ge(lo_made, c - 3)

            def stream(first, src, n, kt, row0):
                lead = 0
                while first + lead < 4:
                    if first + lead > 0:
                        load(sp, (first + lead) % 4, src[row0 + lead], kt)
                    lead += 1
                turns = (n - lead) // 4
                if turns:
                    with sp.Fori(0, turns) as i:
                        for k in range(4):
                            c = lead + 4 * i + k
                            sp.wait_ge(lo_made, first + c - 3)
                            load(sp, (first + lead + k) % 4,
                                 src[bass.ds(row0 + c, 1)].rearrange("a p n -> p (a n)"), kt)
                for c in range(lead + 4 * turns, n):
                    free(first + c)
                    load(sp, (first + c) % 4, src[row0 + c], kt)

            def ffn(f):
                for half in range(2):
                    stream(base["gu", f, half], A["w_gu"], GU_JOBS, KD, (2 * f + half) * GU_JOBS)
                    stream(base["dn", f, half], A["w_dn"], DN_JOBS, HF, (2 * f + half) * DN_JOBS)

            ffn(0)
            stream(base["rec"], A["w_rec"], base["wout"] - base["rec"], KD, 0)
            stream(base["wout"], A["w_out"], KD, KD, 0)
            ffn(1)
            stream(base["kv"], A["w_kv"], 2, KD, 0)
            ffn(2)
            stream(base["q"], A["w_q"], KD, KD, 0)
            stream(base["wo"], A["w_o"], KD, KD, 0)
            ffn(3)
            for half in range(2):
                t = slice(HT * half, HT * (half + 1))
                for first, last in (Y_STORES, [(m, m + 1) for m in Y_ORDER])[half]:
                    if first < Y_DVE:
                        sp.wait_ge(y_out, Y_DVE * half + last)
                    else:
                        sp.wait_ge(y_out_pool, (KD - Y_DVE) * half + last - Y_DVE)
                    sp.dma_start(A["yT"][first:last, :, t].rearrange("m p n -> p m n"),
                                 x[:, first:last, t]).then_inc(stored, 16)
            sp.wait_ge(stored, 16 * (len(Y_STORES) + KD))
            sp.wait_ge(side_stored, 16 * 6)

        @block.tensor
        def _(pe):
            def mm_k(slot, w, k, hi, lo, cut, first, last, kw=None):
                kw = k if kw is None else kw
                passes = ((w_hi, hi), (w_hi, lo), (w_lo, hi))
                for n, (a, b) in enumerate(passes):
                    for c, (o, width) in enumerate(cut):
                        ins = nc.tensor.matmul(ps[:, 2 * slot + c, 0:width], wv(a, w, kw), halves(b, o, width),
                                               start=first and n == 0, stop=last and n == 2)
                return ins

            def job(j, par, kt, operand, cut=EVEN, ready=None, inside=None, used=None, split_chunk=False):
                if not split_chunk:
                    pe.wait_ge(lo_made, j + 1)
                for k in range(kt):
                    if split_chunk and k == 0:
                        pe.wait_ge(first_lo_made, 1)
                    if split_chunk and k == FIRST // P:
                        pe.wait_ge(lo_made, j + 1)
                    if ready:
                        pe.wait_ge(*ready(k))
                    hi, lo = operand(k)
                    ins = mm_k(par, par, k, hi, lo, cut, k == 0, k == kt - 1)
                    if used is not None and k < kt - 1:
                        ins.then_inc(used, 1)
                    if inside is not None and k == inside[0]:
                        inside[1]()
                ins.then_inc(job_done, 1)

            def xs_tile(k):
                return xs_hi[:, k, :], xs_lo[:, k, :]

            def hid_tile(k):
                return act_tile(act_hi, k), act_tile(act_lo, k)

            def stats(s):
                if s:
                    pe.wait_ge(ss_added, (KD - 1) * s)
                else:
                    pe.wait_ge(first_added, KD - 3)
                    pe.wait_ge(consts_loaded, 32)
                for c, (o, width) in enumerate(EVEN):
                    ins = nc.tensor.matmul(ps[:, 4 + c, 0:width], ones[:, :], ssum[:, o:o + width],
                                           start=True, stop=True)
                ins.then_inc(stat_sum, 1)

            def turn_values():
                pe.wait_ge(dve_evac, evac(base["kv"] + 1))
                pe.wait_ge(misc_loaded, 32)
                for b in range(NBLK):
                    nc.tensor.transpose(ps[:, 6, b * P:(b + 1) * P], v_t[:, b * P:(b + 1) * P], ident[:, :])
                nc.tensor.transpose(ps[0:NS, 7, 0:P], v_t[:, SEQ:NT], ident[:, :]).then_inc(v_turned, 1)

            def ffn(f, stat):
                s = FFN_INPUT[f]
                stat_job = None if stat is None else base["gu", f, 0] + (f == 0)
                for half in range(2):
                    j0 = base["gu", f, half]
                    for j in (j0, j0 + 1):
                        slot_free(pe, j)
                        job(j, j % 2, KD, xs_tile,
                            ready=(lambda k: (xs_ready, KD * s + k + 1)) if j == j0 and half == 0 else None,
                            inside=(5 if f else 3, lambda: stats(stat)) if j == stat_job and half == 0 else None,
                            split_chunk=j == 0)
                        if f == 2 and j == j0 and half == 0:
                            turn_values()
                    with pe.Fori(0, (GU_JOBS - 2) // 4) as i:
                        for k in range(4):
                            j = 4 * i + (j0 + 2 + k)
                            pe.wait_ge(dve_evac, 4 * i + dve_done[j0 + 1 + k])
                            job(j, (j0 + k) % 2, KD, xs_tile)
                    j0 = base["dn", f, half]
                    u0 = FT * f + HF * half
                    with pe.Fori(0, DN_JOBS // 2) as i:
                        for k in range(2):
                            j = 2 * i + (j0 + k)
                            pe.wait_ge(dve_evac, 2 * i + dve_done[j0 + k - 1])
                            job(j, (j0 + k) % 2, HF, hid_tile,
                                ready=(lambda t: (hid_ready, u0 + t + 1)) if k == 0 else None)

            def recurrent():
                def conv_tile(m):
                    o = conv_at(m)
                    return act_hi[:, o:o + NP], act_lo[:, o:o + NP]

                def conv_input(m):
                    j = base["xr", m]
                    slot_free(pe, j)
                    job(j, j % 2, KD, xs_tile, cut=BLOCKS,
                        ready=(lambda k: (xs_ready, KD + k + 1)) if m == 0 else None,
                        inside=(5, lambda: stats(1)) if m == 0 else None)

                conv_input(0)
                conv_input(1)
                for n in range(KD // 2):
                    if n + 1 < KD // 2:
                        conv_input(2 * n + 2)
                        conv_input(2 * n + 3)
                    j = base["ax", n]
                    slot_free(pe, j)
                    pe.wait_ge(lo_made, j + 1)
                    pe.wait_ge(xc_ready, 2 * n + 2)
                    if n == 0:
                        pe.wait_ge(std_made, 2)
                    else:
                        pe.wait_ge(act_evac, 4 * n)
                    for q in range(4):
                        if q == 3:
                            pe.wait_ge(act_evac, 4 * n + 1)
                        for k in range(2):
                            hi, lo = conv_tile(2 * n + k)
                            ins = mm_k((j % 2, 2, 3, j % 2)[q], j % 2, k, hi, lo, PADDED, k == 0, k == 1,
                                       kw=2 * q + k)
                        if q < 3:
                            ins.then_inc(ax_done, 1)
                    ins.then_inc(job_done, 1)
                    for m in (2 * n, 2 * n + 1):
                        j = base["gate", m]
                        slot_free(pe, j)
                        job(j, j % 2, KD, xs_tile)

            def recurrent_out():
                j0 = base["wout"]
                for m, tiles in ((0, range(6)), (1, range(3)), (0, range(6, KD)), (1, range(3, KD))):
                    if tiles[0] == 0:
                        slot_free(pe, j0 + m)
                        pe.wait_ge(lo_made, j0 + m + 1)
                    for k in tiles:
                        if m == 0:
                            pe.wait_ge(y_ready, k + 1)
                        hi, lo = hid_tile(k)
                        ins = mm_k((j0 + m) % 2, (j0 + m) % 2, k, hi, lo, EVEN, k == 0, k == KD - 1)
                    if tiles[-1] == KD - 1:
                        ins.then_inc(job_done, 1)
                out_product(j0, 2)

            def out_product(j0, first):
                for m in range(first, KD):
                    slot_free(pe, j0 + m)
                    job(j0 + m, (j0 + m) % 2, KD, hid_tile)

            def key_value():
                j = base["kv"]
                slot_free(pe, j)
                job(j, j % 2, KD, xs_tile, ready=lambda k: (xs_ready, 3 * KD + k + 1),
                    inside=(2, lambda: stats(3)))
                slot_free(pe, j + 1)
                job(j + 1, (j + 1) % 2, KD, xs_tile, used=v_tile_used)

            def attention():
                def scores(h):
                    m, p, g = h // 2, 64 * (h % 2), h // 8
                    b0 = 4 if h % 2 == 0 else 0
                    if h >= 2:
                        pe.wait_ge(exp_made, h - 1)
                    elif h == 0:
                        pe.wait_ge(std_made, 5)
                        pe.wait_ge(k_dup_made, 1)
                    pe.wait_ge(dve_evac, evac(base["q"] + (m if h != 1 else KD - 2)))
                    for b in range(NBLK):
                        q = q_p[p:p + 64, m, b * P:(b + 1) * P]
                        lo, hi = (b - 1) * P, (b + 1) * P
                        if b == 0:
                            lo = 0
                        c = (b % 2) * 256 + (0 if b else P)
                        ins = nc.tensor.matmul(ps[:, b0 + b // 2, c:c + hi - lo], q, kdup[p:p + 64, g, lo:hi],
                                               start=True, stop=True)
                    ins.then_inc(scores_done, 1)

                def turn(h):
                    pe.wait_ge(prob_ready, h + 1)
                    if h >= 1:
                        pe.wait_ge(pt_ready, h)
                    for t in range(7):
                        ins = nc.tensor.transpose(ps[:, 6 + t // 4, (t % 4) * P:(t % 4 + 1) * P],
                                                  prob[h % 2][:, (t + 1) * P:(t + 2) * P], ident[:, :])
                    ins.then_inc(prob_turned, 1)

                def values(h):
                    m, p, g = h // 2, 64 * (h % 2), h // 8
                    pe.wait_ge(pt_ready, h + 1)
                    if h == 0:
                        pe.wait_ge(dve_evac, evac(base["q"] + KD - 1))
                    if h % 2 == 0 and m >= 2:
                        pe.wait_ge(att_ready, m - 1)
                    for b in range(NBLK):
                        for t in ([0] if b == 0 else [2 * b - 1, 2 * b]):
                            kb = b if t == 2 * b else b - 1
                            ins = nc.tensor.matmul(ps[p:p + 64, 2 + m % 2, b * P:(b + 1) * P],
                                                   v_tok[:, kb, 64 * g:64 * g + 64],
                                                   pt[h % 2][:, t * P:(t + 1) * P],
                                                   start=t in (0, 2 * b - 1), stop=t == 2 * b)
                    ins.then_inc(pv_done, 1)

                j0 = base["q"]
                for m in range(KD):
                    slot_free(pe, j0 + m)
                    job(j0 + m, (j0 + m) % 2, KD, xs_tile, cut=BLOCKS,
                        ready=(lambda k: (xs_ready, 5 * KD + k + 1)) if m == 0 else None,
                        inside={0: (5, lambda: stats(4)), KD - 1: (1, lambda: scores(1))}.get(m))
                    if m == 4:
                        scores(0)
                    if m == 6:
                        pe.wait_ge(v_tok_made, 1)
                        turn(0)
                for h in range(N_HEADS + 1):
                    if h + 2 < N_HEADS:
                        scores(h + 2)
                    if 0 < h < N_HEADS:
                        turn(h)
                    if h == N_HEADS - 1:
                        sample_scores(0)
                    if h >= 1:
                        values(h - 1)

                sample_scores(1)
                jo = base["wo"]
                pe.wait_ge(bias_added, 1)
                pe.wait_ge(att_ready, KD)
                pe.wait_ge(lo_made, jo + 1)
                half_job(jo, 0)
                turn_sample(0)
                pe.wait_ge(bias_added, 2)
                pe.wait_ge(lo_made, jo + 2)
                half_job(jo + 1, 0, range(5))
                turn_sample(1)
                sample_values(0)
                sample_values(1)
                half_job(jo + 1, 0, range(5, KD))
                pe.wait_ge(att_ready, KD + 1)
                for m in range(2):
                    half_job(jo + m, 1).then_inc(job_done, 1)

            def sample_scores(s):
                for g in range(N_KV):
                    if s == 0:
                        pe.wait_ge(exp_made, N_HEADS - 1 + g)
                    elif g == 0:
                        pe.wait_ge(pt_ready, N_HEADS)
                    else:
                        pe.wait_ge(att_ready, KD)
                    if s == g == 0:
                        pe.wait_ge(att_loaded, 16 * 5)
                    r = slice(64 * g, 64 * g + 64)
                    for b in range(4 * s, 4 * s + 4):
                        bank, c = (4, 0)[g] + b // 2, (b % 2) * NKEY
                        q = q_s[r, b, :]
                        nc.tensor.matmul(ps[r, bank, c:c + WINDOW], q, kc[r, b, :], start=True, stop=True)
                        ins = nc.tensor.matmul(ps[r, bank, c + WINDOW:c + NKEY], q, kdup[r, g, SEQ:NT],
                                               start=True, stop=True)
                    ins.then_inc(sample_scored, 1)

            def turn_sample(s):
                pe.wait_ge(sample_prob, s + 1)
                for b in range(4 * s, 4 * s + 4):
                    c = (b % 4) * P
                    nc.tensor.transpose(ps[:, 4 + 2 * s, c:c + P], s_s[:, b, 0:WINDOW], ident[:, :])
                    ins = nc.tensor.transpose(ps[0:NS, 5 + 2 * s, c:c + P], s_s[:, b, WINDOW:NKEY], ident[:, :])
                ins.then_inc(sample_turned, 1)

            def half_job(j, c, tiles=range(KD)):
                for k in tiles:
                    hi, lo = hid_tile(k)
                    for n, (a, b) in enumerate(((w_hi, hi), (w_hi, lo), (w_lo, hi))):
                        ins = nc.tensor.matmul(ps[:, 2 * (j % 2) + c, 0:HT], wv(a, j % 2, k), halves(b, HT * c, HT),
                                               start=k == n == 0, stop=k == KD - 1 and n == 2)
                return ins

            def sample_values(s):
                pe.wait_ge(sample_pt, s + 1)
                for b in range(4 * s, 4 * s + 4):
                    for h2 in range(2):
                        for g in range(N_KV):
                            out = ps[64 * h2:64 * h2 + 64, 1, 64 * b + 32 * g:64 * b + 32 * g + 32]
                            rows = lambda a: a[:, b, 64 * g:64 * g + 64].rearrange(
                                "p (m h t) -> p h m t", m=4, h=2)[:, h2]
                            nc.tensor.matmul(out, vc[:, b, 64 * g:64 * g + 64], rows(ptc), start=True, stop=False)
                            ins = nc.tensor.matmul(out, v_tok[0:NS, NBLK, 64 * g:64 * g + 64], rows(ptn[0:NS]),
                                                   start=False, stop=True)
                ins.then_inc(sample_pv, 1)

            ffn(0, 0)
            recurrent()
            recurrent_out()
            ffn(1, 2)
            key_value()
            ffn(2, None)
            attention()
            out_product(base["wo"], 2)
            ffn(3, 5)
            pe.wait_ge(ss_added, (KD - 1) * 6 - 1)
            for c, (o, width) in enumerate(EVEN):
                nc.tensor.matmul(ps[:, 4 + c, 0:width], ones[:, :], ssum[:, o:o + width], start=True, stop=False)
            pe.wait_ge(sq_made, KD * 6)
            for c, (o, width) in enumerate(EVEN):
                ins = nc.tensor.matmul(ps[:, 4 + c, 0:width], ones[:, :], sq[:, (KD - 1) % 2, o:o + width],
                                       start=False, stop=True)
            ins.then_inc(stat_sum, 1)

        @block.scalar
        def _(act):
            def prep(c, slot, par, kt, landed, used=None):
                act.wait_ge(raw_landed[slot], landed)
                if used is not None:
                    act.wait_ge(job_done, used)
                nc.scalar.activation(w_hi[:, par, 0:kt * P], raw[:, slot, 0:kt * P],
                                     ACT.Copy).then_inc(hi_made, 1)

            def prep_next(j):
                c = j + 2
                if c < NJ:
                    prep(c, c % 4, c % 2, KT[c], 16 * (c // 4 + 1), used=j + 1)

            def split_x(s, m, stat, x_job):
                if x_job is None:
                    act.wait_ge(x_loaded[m], 16)
                else:
                    act.wait_ge(dve_evac, evac(x_job))
                if s is not None:
                    nc.scalar.activation(xs_hi[:, m, :], x[:, m, :], ACT.Copy,
                                         scale=params[:, GAIN[s], m:m + 1]).then_inc(xs_hi_made, 1)
                if stat is not None:
                    if m >= 3:
                        act.wait_ge(ss_added, (KD - 1) * (stat - 1) + m - 2)
                    nc.scalar.activation(ssum[:, :] if m == 0 else sq[:, m % 2, :], x[:, m, :],
                                         ACT.Square).then_inc(sq_made, 1)

            def root(stat):
                act.wait_ge(stat_sum, stat + 1)
                nc.scalar.activation(two(std), ps[:, 4:6, 0:HT], ACT.Sqrt, bias=eps[:, 0:1],
                                     scale=1.0 / D_MODEL).then_inc(std_made, 1)

            def down(j0, s, stat):
                for m in range(KD):
                    prep_next(j0 + m)
                    if s is not None or stat is not None:
                        split_x(s, m, stat, j0 + m)

            def ffn(f, s, stat):
                for half in range(2):
                    j0 = base["gu", f, half]
                    u0 = FT * f + HF * half
                    turns = (GU_JOBS - 2) // 4

                    def unit(k, i, prep_a, prep_b):
                        u = 2 * i + (u0 + k)
                        par = k % 2
                        prep_a()
                        act.wait_ge(dve_evac, 4 * i + evac(j0 + 2 * k))
                        nc.scalar.activation(silu_t[:, par, :], gate_t[:, par, :], ACT.Silu).then_inc(silu_made, 1)
                        prep_b()
                        act.wait_ge(hid_made, u + 1)
                        nc.scalar.activation(act_hi[:, bass.ds((2 * i + k) * NT, NT)], hid[:, par, :],
                                             ACT.Copy).then_inc(hid_hi_made, 1)

                    peeled = int(f == half == 0)
                    for v in range(2 * peeled):
                        unit_static(j0 + 2 * v, u0 + v, v)
                    with act.Fori(peeled, turns) as i:
                        def look(k):
                            c = j0 + k + 2
                            return lambda: prep(4 * i + c, c % 4, c % 2, KD, 16 * i + 16 * (c // 4 + 1),
                                                used=4 * i + (j0 + k + 1))
                        for k in range(2):
                            unit(k, i, look(2 * k), look(2 * k + 1))
                    for v in range(2 * turns, HF):
                        unit_static(j0 + 2 * v, u0 + v, v)
                    down(base["dn", f, half], s if half else None, stat if half else None)
                    if f == half == 0:
                        lru_constants()

            def unit_static(j, u, v):
                par = v % 2
                if j > 0:
                    prep_next(j)
                act.wait_ge(dve_evac, evac(j))
                nc.scalar.activation(silu_t[:, par, :], gate_t[:, par, :], ACT.Silu).then_inc(silu_made, 1)
                prep_next(j + 1)
                act.wait_ge(hid_made, u + 1)
                nc.scalar.activation(act_hi[:, v * NT:(v + 1) * NT], hid[:, par, :],
                                     ACT.Copy).then_inc(hid_hi_made, 1)

            def lru_constants():
                act.wait_ge(lam_abs, 1)
                nc.scalar.activation(lam[:, 1, :], lam[:, 0, :], ACT.Exp, scale=-1.0).then_inc(lam_exp, 1)

            def recurrent():

                def round_conv(m):
                    act.wait_ge(xc_made, m + 1)
                    nc.scalar.activation(act_hi[:, conv_at(m):conv_at(m) + NP], xc[:, m % 4, :],
                                         ACT.Copy).then_inc(xc_hi_made, 1)

                def round_y(m):
                    act.wait_ge(y_made, m + 1)
                    nc.scalar.activation(act_tile(act_hi, m), tmp[:, m % 2, 0:NT], ACT.Copy).then_inc(y_hi_made, 1)

                def conv_input(m):
                    prep_next(base["xr", m])
                    round_conv(m)

                conv_input(0)
                conv_input(1)
                for n in range(KD // 2):
                    pair = (2 * n, 2 * n + 1)
                    ahead = n + 1 < KD // 2
                    if ahead:
                        conv_input(2 * n + 2)
                        prep_next(base["xr", 2 * n + 3])
                    j = base["ax", n]
                    if n:
                        act.wait_ge(h_made, 2 * n)
                    for q in range(4):
                        m, (dst, vec) = 2 * n + q // 2, ((rr, V_BA), (ii, V_BX))[q % 2]
                        if q < 3:
                            act.wait_ge(ax_done, 3 * n + q + 1)
                        else:
                            act.wait_ge(job_done, j + 1)
                        nc.scalar.activation(two(dst[:, m % 2, :]), ps2((j % 2, 2, 3, j % 2)[q], NP // 2), ACT.Sigmoid,
                                             bias=params[:, vec, m:m + 1]).then_inc(act_evac, 1)
                    prep_next(j)
                    if n:
                        round_y(2 * n - 2)
                        round_y(2 * n - 1)
                    if ahead:
                        round_conv(2 * n + 3)
                    act.wait_ge(decay_ready, 1)
                    act.wait_ge(act_evac, 4 * n + 4)
                    for m in pair:
                        nc.scalar.activation(tt[:, m % 2, :], rr[:, m % 2, :], ACT.Tanh,
                                             scale=ndecay[:, m:m + 1]).then_inc(tanh_made, 1)
                    act.wait_ge(tanh_made, 2 * n + 2)
                    for m in pair:
                        nc.scalar.activation(rr[:, m % 2, :], rr[:, m % 2, :], ACT.Exp,
                                             scale=decay[:, m:m + 1]).then_inc(a_made, 1)
                    if n:
                        act.wait_ge(y_ready, 2 * n)
                    for m in pair:
                        act.wait_ge(a_made, m + 1)
                        nc.scalar.activation(tmp[:, m % 2, :], rr[:, m % 2, :], ACT.Square).then_inc(a2_made, 1)
                    prep_next(base["gate", 2 * n])
                    for m in pair:
                        act.wait_ge(m2_made, m + 1)
                        nc.scalar.activation(tt[:, m % 2, :], tt[:, m % 2, :], ACT.Sqrt).then_inc(mult_made, 1)
                    for m in pair:
                        act.wait_ge(dve_evac, evac(base["gate", m]))
                        nc.scalar.activation(gate[:, m % 2, :], gate[:, m % 2, :],
                                             ACT.Gelu_apprx_tanh).then_inc(gate_out, 1)
                        if m == 2 * n:
                            prep_next(base["gate", m + 1])
                round_y(KD - 2)
                round_y(KD - 1)

            def attention():
                act.wait_ge(misc_loaded, 32)
                for m in range(KD - 1):
                    prep_next(base["q"] + m)
                    if m == 4:
                        exponentials(0)
                for h in range(1, N_HEADS + 1):
                    if h < N_HEADS:
                        exponentials(h)
                    q = h - 1
                    act.wait_ge(prob_turned, q + 1)
                    if q >= 2:
                        act.wait_ge(pv_done, q - 1)
                    nc.scalar.activation(pt[q % 2][:, 0:512], ps[:, 6, :], ACT.Copy)
                    nc.scalar.activation(pt[q % 2][:, 512:7 * P], ps[:, 7, 0:3 * P], ACT.Copy).then_inc(pt_ready, 1)
                    if h == 1:
                        prep_next(base["q"] + KD - 1)
                    if h >= 3 and h % 2 == 1:
                        round_o((h - 3) // 2)
                round_o(KD - 1)
                sample_exponentials(0)
                sample_exponentials(1)
                copy_turned(0)
                copy_turned(1)
                act.wait_ge(sample_pv, 2)
                nc.scalar.activation(sample_cols(act_hi), sample_o, ACT.Copy).then_inc(o_hi_made, 1)

            def exponentials(h):
                b0 = 4 if h % 2 == 0 else 0
                o = 4 * (h % 2)
                two_banks = ps[:, b0:b0 + 2, :].rearrange("p a n -> p (a n)")
                act.wait_ge(max_made, h + 1)
                nc.scalar.activation(sink_exp[:, o:o + 4], neg_max[:, o:o + 4], ACT.Exp, bias=sinks[:, h:h + 1])
                if h >= 2:
                    act.wait_ge(prob_turned, h - 1)
                for b in range(NBLK):
                    t = slice(256 * b + (0 if b else P), 256 * (b + 1))
                    ins = nc.scalar.activation(prob[h % 2][:, t], two_banks[:, t], ACT.Exp,
                                               bias=neg_max[:, o + b:o + b + 1],
                                               accum_out=row_sum[:, o + b:o + b + 1])
                ins.then_inc(exp_made, 1)

            def sample_exponentials(s):
                o = slice(4 * s, 4 * s + 4)
                act.wait_ge(sample_max, s + 1)
                nc.scalar.activation(sink_exp[:, o], neg_max[:, o], ACT.Exp, bias=sinks[:, N_HEADS:N_HEADS + 1])
                for b in range(4 * s, 4 * s + 4):
                    ins = nc.scalar.activation(s_s[:, b, :], s_s[:, b, :], ACT.Exp, bias=neg_max[:, b:b + 1],
                                               accum_out=row_sum[:, b:b + 1])
                ins.then_inc(sample_exp, 1)

            def copy_turned(s):
                act.wait_ge(sample_turned, s + 1)
                b = slice(4 * s, 4 * s + 4)
                nc.scalar.activation(ptc[:, b, :].rearrange("p b n -> p (b n)"), ps[:, 4 + 2 * s, :], ACT.Copy)
                nc.scalar.activation(ptn[0:NS, b, :].rearrange("p b n -> p (b n)"), ps[0:NS, 5 + 2 * s, :],
                                     ACT.Copy).then_inc(sample_pt, 1)

            def round_o(m):
                act.wait_ge(pv_done, 2 * m + 2)
                nc.scalar.activation(act_hi[:, m * NT:m * NT + SEQ], ps[:, 2 + m % 2, :], ACT.Copy).then_inc(o_hi_made, 1)

            act.dma_start(params[:, :, :], A["params"]).then_inc(params_loaded, 16)
            for m in range(1, KD, 2):
                act.dma_start(x[:, m, :], A["xT"][m]).then_inc(x_loaded[m], 16)
            act.dma_start(ones[:, :], A["ones"]).then_inc(consts_loaded, 16)
            act.dma_start(eps[:, :], A["eps"]).then_inc(consts_loaded, 16)
            act.wait_ge(first_landed, 16)
            nc.scalar.activation(w_hi[:, 0, 0:FIRST], raw[:, 0, 0:FIRST], ACT.Copy).then_inc(first_hi_made, 1)
            act.wait_ge(params_loaded, 16)
            for m in range(KD):
                split_x(0, m, None, None)
                if m == 0:
                    act.wait_ge(raw_landed[0], 16)
                    nc.scalar.activation(w_hi[:, 0, FIRST:D_MODEL], raw[:, 0, FIRST:D_MODEL],
                                         ACT.Copy).then_inc(hi_made, 1)
            for m in range(3, KD):
                nc.scalar.activation(first_sq[:, m, :], x[:, m, :], ACT.Square).then_inc(first_sq_made, 1)
                if m == 3:
                    prep(1, 1, 1, KT[1], 16)
            act.wait_ge(consts_loaded, 32)
            prep_next(0)
            root(0)
            ffn(0, 1, 1)
            root(1)
            recurrent()
            down(base["wout"], 2, 2)
            root(2)
            ffn(1, 3, 3)
            root(3)
            j = base["kv"]
            prep_next(j)
            for m in range(KD):
                if m < KD - 1:
                    act.wait_ge(v_tile_used, m + 1)
                else:
                    act.wait_ge(job_done, j + 2)
                split_x(4, m, None, j - 1)
            prep_next(j + 1)
            ffn(2, 5, 4)
            root(4)
            attention()
            down(base["wo"], 6, 5)
            root(5)
            ffn(3, None, 6)
            root(6)
            for m in range(Y_DVE, KD):
                nc.scalar.activation(x[:, m, :], x[:, m, :], ACT.Copy,
                                     scale=params[:, V_FIN, m:m + 1]).then_inc(x_scaled, 1)

        @block.vector
        def _(dve):
            chain = [0]

            def own(ins):
                chain[0] += 1
                ins.then_inc(dve_chain, 1)
                dve.wait_ge(dve_chain, chain[0])

            def prep(c, slot, par, kt):
                dve.wait_ge(hi_made, c + 1)
                nc.vector.tensor_tensor(w_lo[:, par, 0:kt * P], raw[:, slot, 0:kt * P],
                                        w_hi[:, par, 0:kt * P].bitcast(F32), ALU.subtract).then_inc(lo_made, 1)

            def prep_next(j):
                c = j + 2
                if c < NJ:
                    prep(c, c % 4, c % 2, KT[c])

            def split_x(s, m, stat):
                if s is not None:
                    dve.wait_ge(xs_hi_made, KD * s + m + 1)
                    nc.vector.scalar_tensor_tensor(xs_lo[:, m, :], x[:, m, :], params[:, GAIN[s], m:m + 1],
                                                   xs_hi[:, m, :].bitcast(F32), ALU.mult,
                                                   ALU.subtract).then_inc(xs_ready, 1)
                if stat is not None:
                    dve.wait_ge(sq_made, KD * (stat - 1) + m + 1)
                    if m >= 2:
                        dve.wait_ge(ss_added, (KD - 1) * (stat - 1) + m - 1)
                    if m >= 1 and (stat, m) != (6, KD - 1):
                        nc.vector.tensor_tensor(ssum[:, :], ssum[:, :], sq[:, m % 2, :], ALU.add).then_inc(ss_added, 1)

            def invert(stat):
                dve.wait_ge(std_made, stat + 1)
                nc.vector.reciprocal(rstd[:, :], std).then_inc(rstd_made, 1)
                dve.wait_ge(rstd_made, stat + 1)

            def down(j0, s, stat, factor):
                for m in range(KD):
                    dve.wait_ge(job_done, j0 + m + 1)
                    dve.wait_ge(dve_evac, evac(j0 + m - 1))
                    nc.vector.scalar_tensor_tensor(two(x[:, m, :]), ps2((j0 + m) % 2), factor, two(x[:, m, :]),
                                                   ALU.mult, ALU.add).then_inc(dve_evac, 1)
                    prep_next(j0 + m)
                    split_x(s, m, stat)

            def ffn(f, s, stat):
                for half in range(2):
                    j0 = base["gu", f, half]
                    u0 = FT * f + HF * half
                    turns = (GU_JOBS - 2) // 4

                    def unit(j, u, up_evac, par, slot, tile_at, prep_a, prep_b):
                        dve.wait_ge(job_done, j + 1)
                        nc.vector.tensor_tensor(two(gate_t[:, par, :]), ps2(slot), two(rstd[:, :]),
                                                ALU.mult).then_inc(dve_evac, 1)
                        prep_a()
                        dve.wait_ge(job_done, j + 2)
                        nc.vector.tensor_tensor(two(up_t[:, par, :]), ps2(1 - slot), two(rstd[:, :]),
                                                ALU.mult).then_inc(dve_evac, 1)
                        dve.wait_ge(dve_evac, up_evac)
                        dve.wait_ge(silu_made, u + 1)
                        nc.vector.tensor_tensor(hid[:, par, :], up_t[:, par, :], silu_t[:, par, :],
                                                ALU.mult).then_inc(hid_made, 1)
                        prep_b()
                        dve.wait_ge(hid_hi_made, u + 1)
                        nc.vector.tensor_tensor(act_lo[:, tile_at], hid[:, par, :], act_hi[:, tile_at].bitcast(F32),
                                                ALU.subtract).then_inc(hid_ready, 1)

                    def static(v):
                        j = j0 + 2 * v
                        unit(j, u0 + v, evac(j + 1), v % 2, j0 % 2, slice(v * NT, (v + 1) * NT),
                             lambda: prep_next(j) if j else None, lambda: prep_next(j + 1))

                    peeled = int(f == half == 0)
                    for v in range(2 * peeled):
                        static(v)
                    with dve.Fori(peeled, turns) as i:
                        for k in range(2):
                            ca, cb = j0 + 2 * k + 2, j0 + 2 * k + 3
                            unit(4 * i + (j0 + 2 * k), 2 * i + (u0 + k), 4 * i + evac(j0 + 2 * k + 1), k, j0 % 2,
                                 bass.ds((2 * i + k) * NT, NT),
                                 lambda: prep(4 * i + ca, ca % 4, ca % 2, KD),
                                 lambda: prep(4 * i + cb, cb % 4, cb % 2, KD))
                    for v in range(2 * turns, HF):
                        static(v)
                    down(base["dn", f, half], s if half else None, stat if half else None, 0.5)
                    if f == half == 0:
                        lru_constants()

            def lru_constants():
                v = params[:, V_LAM, :]
                nc.vector.scalar_tensor_tensor(lam[:, 0, :], v, -1.0, v, ALU.mult, ALU.max).then_inc(lam_abs, 1)
                dve.wait_ge(lam_exp, 1)
                own(nc.vector.tensor_scalar(lam[:, 2, :], lam[:, 1, :], 2.0, None, ALU.add))
                own(nc.vector.reciprocal(lam[:, 3, :], lam[:, 2, :]))
                own(nc.vector.tensor_tensor(lam[:, 2, :], lam[:, 1, :], lam[:, 3, :], ALU.mult))
                own(nc.vector.tensor_tensor(lam[:, 3, :], lam[:, 2, :], lam[:, 2, :], ALU.mult))
                own(nc.vector.tensor_scalar(lam[:, 4, :], lam[:, 3, :], 1.0 / 17, None, ALU.mult))
                for k in range(7, 0, -1):
                    own(nc.vector.scalar_tensor_tensor(lam[:, 4, :], lam[:, 4, :], 1.0 / (2 * k + 1), lam[:, 3, :],
                                                       ALU.add, ALU.mult))
                own(nc.vector.scalar_tensor_tensor(lam[:, 5, :], lam[:, 4, :], 1.0, lam[:, 2, :], ALU.add, ALU.mult))
                own(nc.vector.tensor_scalar(lam[:, 4, :], v, -1.0, 0.0, ALU.mult, ALU.max))
                own(nc.vector.scalar_tensor_tensor(lam[:, 3, :], lam[:, 5, :], 2.0, lam[:, 4, :], ALU.mult, ALU.add))
                nc.vector.tensor_scalar(decay, lam[:, 3, :], -8.0, None, ALU.mult)
                nc.vector.tensor_scalar(ndecay, lam[:, 3, :], 8.0, None, ALU.mult).then_inc(decay_ready, 1)

            def recurrent():
                nc.vector.memset(xe[:, :, 0:PRE], 0.0)
                dve.wait_ge(state_loaded, 16)

                def evacuate_x(m, j):
                    r = m % 2
                    dve.wait_ge(job_done, j + 1)
                    if m >= 2:
                        dve.wait_ge(conv_saved, m - 1)
                    nc.vector.tensor_copy(seg(xe[:, r, :], 0, PRE),
                                          st_in[:, m, DEC_BATCH:].rearrange("p (b k) -> p b k", b=DEC_BATCH))
                    nc.vector.tensor_tensor(xe[:, r, PRE:S0].rearrange("p (a n) -> p a n", a=2),
                                            ps2(j % 2, 256), rstd[:, 0:SEQ].rearrange("p (a n) -> p a n", a=2),
                                            ALU.mult)
                    nc.vector.tensor_tensor(seg(xe[:, r, :], PRE, DEC_SEQ),
                                            ps[:, 2 * (j % 2) + 1, 256:256 + NS].rearrange("p (b t) -> p b t", b=DEC_BATCH),
                                            rstd[:, SEQ:NT].rearrange("p (b t) -> p b t", b=DEC_BATCH),
                                            ALU.mult).then_inc(dve_evac, 1)

                def conv(m):
                    r = m % 2
                    dve.wait_ge(dve_evac, evac(base["xr", m]))
                    if m >= 4:
                        dve.wait_ge(ix_made, m - 3)
                    own(nc.vector.tensor_scalar(xc[:, m % 4, :], xe[:, r, 0:NP], params[:, V_CW, m:m + 1],
                                                params[:, V_CB, m:m + 1], ALU.mult, ALU.add))
                    for k in range(1, CONV_W):
                        ins = nc.vector.scalar_tensor_tensor(xc[:, m % 4, :], xe[:, r, k:k + NP],
                                                             params[:, V_CW + k, m:m + 1], xc[:, m % 4, :],
                                                             ALU.mult, ALU.add)
                        if k < CONV_W - 1:
                            own(ins)
                    ins.then_inc(xc_made, 1)

                def rest_conv(m):
                    dve.wait_ge(xc_hi_made, m + 1)
                    t = slice(conv_at(m), conv_at(m) + NP)
                    nc.vector.tensor_tensor(act_lo[:, t], xc[:, m % 4, :], act_hi[:, t].bitcast(F32),
                                            ALU.subtract).then_inc(xc_ready, 1)

                def evacuate_gate(m, j):
                    dve.wait_ge(job_done, j + 1)
                    nc.vector.tensor_tensor(two(gate[:, m % 2, :]), ps2(j % 2), two(rstd[:, :]),
                                            ALU.mult).then_inc(dve_evac, 1)

                def square_of_multiplier(m):
                    r = m % 2
                    dve.wait_ge(tanh_made, m + 1)
                    dve.wait_ge(a2_made, m + 1)
                    nc.vector.scalar_tensor_tensor(tt[:, r, :], tmp[:, r, :], 1.0, tt[:, r, :], ALU.add,
                                                   ALU.mult).then_inc(m2_made, 1)

                def scan(m):
                    r = m % 2
                    dve.wait_ge(mult_made, m + 1)
                    dve.wait_ge(ix_made, m + 1)
                    dve.wait_ge(a_made, m + 1)
                    own(nc.vector.tensor_tensor(ii[:, r, :], ii[:, r, :], tt[:, r, :], ALU.mult))
                    before = slice(S0 - 1, S0 - 1 + SEG * (DEC_BATCH - 1) + 1, SEG)
                    nc.vector.memset(rr[:, r, before], 0.0)
                    own(nc.vector.tensor_copy(ii[:, r, before], st_in[:, m, 0:DEC_BATCH]))
                    if m >= 2:
                        dve.wait_ge(h_saved, m - 1)
                    nc.vector.tensor_tensor_scan(hh[:, r, :], rr[:, r, :], ii[:, r, :], 0.0, ALU.mult,
                                                 ALU.add).then_inc(h_made, 1)

                def gated(m):
                    r = m % 2
                    dve.wait_ge(h_made, m + 1)
                    dve.wait_ge(gate_out, m + 1)
                    nc.vector.tensor_tensor(tmp[:, r, 0:SEQ], hh[:, r, 0:SEQ], gate[:, m % 2, 0:SEQ], ALU.mult)
                    nc.vector.tensor_tensor(tmp[:, r, SEQ:NT].rearrange("p (b t) -> p b t", b=DEC_BATCH),
                                            hseg(hh[:, r, :]),
                                            gate[:, m % 2, SEQ:NT].rearrange("p (b t) -> p b t", b=DEC_BATCH),
                                            ALU.mult).then_inc(y_made, 1)

                def rest_y(m):
                    dve.wait_ge(y_hi_made, m + 1)
                    nc.vector.tensor_tensor(act_tile(act_lo, m), tmp[:, m % 2, 0:NT],
                                            act_tile(act_hi, m).bitcast(F32), ALU.subtract).then_inc(y_ready, 1)

                def conv_input(m):
                    evacuate_x(m, base["xr", m])
                    if m % 2:
                        rest_conv(m - 1)
                    prep_next(base["xr", m])
                    conv(m)

                conv_input(0)
                conv_input(1)
                rest_conv(1)
                for n in range(KD // 2):
                    a, b = 2 * n, 2 * n + 1
                    if n + 1 < KD // 2:
                        conv_input(a + 2)
                        conv_input(b + 2)
                    prep_next(base["ax", n])
                    if n:
                        rest_y(a - 2)
                        rest_y(b - 2)
                    if n + 1 < KD // 2:
                        rest_conv(b + 2)
                    square_of_multiplier(a)
                    square_of_multiplier(b)
                    evacuate_gate(a, base["gate", a])
                    prep_next(base["gate", a])
                    scan(a)
                    scan(b)
                    evacuate_gate(b, base["gate", b])
                    prep_next(base["gate", b])
                    gated(a)
                    gated(b)
                rest_y(KD - 2)
                rest_y(KD - 1)

            def hseg(v):
                return v[:, S0 - PRE:NP].rearrange("p (b s) -> p b s", b=DEC_BATCH)[:, :, PRE:SEG]

            def key_value():
                j = base["kv"]
                invert(3)
                dve.wait_ge(job_done, j + 1)
                for g in range(N_KV):
                    r = slice(64 * g, 64 * g + 64)
                    ins = nc.vector.tensor_tensor(two(kdup[r, g, :]), ps[r, 2 * (j % 2):2 * (j % 2) + 2, 0:HT],
                                                  two(rstd[r, :]), ALU.mult)
                ins.then_inc(dve_evac, 1)
                prep_next(j)
                for m in range(KD):
                    split_x(4, m, None)
                dve.wait_ge(job_done, j + 2)
                nc.vector.tensor_tensor(two(v_t), ps2((j + 1) % 2), two(rstd[:, :]), ALU.mult).then_inc(dve_evac, 1)
                prep_next(j + 1)
                dve.wait_ge(v_turned, 1)
                nc.vector.tensor_copy(v_tok[:, 0:NBLK, :].rearrange("p b n -> p (b n)"), ps[:, 6, :])
                nc.vector.tensor_copy(v_tok[0:NS, NBLK, :], ps[0:NS, 7, 0:P]).then_inc(v_tok_made, 1)

            def attention():
                j0 = base["q"]
                scale = HEAD_DIM ** -0.5
                by_seq = lambda v: v.rearrange("p (b t) -> p b t", b=DEC_BATCH)
                dve.wait_ge(att_loaded, 16 * 5)
                dve.wait_ge(misc_loaded, 32)
                for m in range(KD):
                    j = j0 + m
                    g = m // 4
                    dve.wait_ge(job_done, j + 1)
                    nc.vector.scalar_tensor_tensor(q_p[:, m, :].rearrange("p (a n) -> p a n", a=2), ps2(j % 2, 256), scale,
                                                   rstd[:, 0:SEQ].rearrange("p (a n) -> p a n", a=2),
                                                   ALU.mult, ALU.mult)
                    for p in range(2):
                        t = (2 * (m % 4) + p) * DEC_SEQ
                        ins = nc.vector.scalar_tensor_tensor(
                            q_s[64 * g:64 * g + 64, :, t:t + DEC_SEQ],
                            by_seq(ps[64 * p:64 * p + 64, 2 * (j % 2) + 1, 256:256 + NS]), scale,
                            by_seq(rstd[64 * g:64 * g + 64, SEQ:NT]), ALU.mult, ALU.mult)
                    ins.then_inc(dve_evac, 1)
                    if m < KD - 1:
                        prep_next(j)
                    if m == 4:
                        maximum(0)
                    if m == 5:
                        normalise(0)
                    if m == 6:
                        maximum(1)
                normalise(1)
                for h in range(2, N_HEADS + 1):
                    if h < N_HEADS:
                        maximum(h)
                    if h > 2:
                        normalise(h - 1)
                    if h == 5:
                        prep_next(j0 + KD - 1)
                    if h >= 4 and h % 2 == 0:
                        rest_o((h - 4) // 2)
                sample_maximum(0)
                rest_o(KD - 1)
                sample_maximum(1)
                sample_normalise(0)
                sample_normalise(1)
                dve.wait_ge(o_hi_made, KD + 1)
                nc.vector.tensor_tensor(sample_cols(act_lo), sample_o, sample_cols(act_hi).bitcast(F32),
                                        ALU.subtract).then_inc(att_ready, 1)

            def maximum(h):
                o = 4 * (h % 2)
                two_banks = ps[:, 4 - 4 * (h % 2):6 - 4 * (h % 2), :].rearrange("p a n -> p (a n)")
                dve.wait_ge(scores_done, h + 1)
                dve.wait_ge(alibi_made, h + 1)
                for b in range(NBLK):
                    c = 0 if b else P
                    v = two_banks[:, 256 * b + c:256 * (b + 1)]
                    ins = nc.vector.tensor_tensor_reduce(v, v, alibi[:, h % 2, c:], 1.0, sinks[:, h:h + 1], ALU.add,
                                                         ALU.max, neg_max[:, o + b:o + b + 1])
                own(ins)
                nc.vector.tensor_scalar(neg_max[:, o:o + 4], neg_max[:, o:o + 4], -1.0, None,
                                        ALU.mult).then_inc(max_made, 1)

            def normalise(h):
                o = 4 * (h % 2)
                dve.wait_ge(exp_made, h + 1)
                own(nc.vector.tensor_tensor(inv_den[:, o:o + 4], row_sum[:, o:o + 4], sink_exp[:, o:o + 4], ALU.add))
                own(nc.vector.reciprocal(inv_den[:, o:o + 4], inv_den[:, o:o + 4]))
                for b in range(NBLK):
                    t = slice(256 * b + (0 if b else P), 256 * (b + 1))
                    ins = nc.vector.tensor_scalar(prob[h % 2][:, t], prob[h % 2][:, t],
                                                  inv_den[:, o + b:o + b + 1], None, ALU.mult)
                ins.then_inc(prob_ready, 1)

            def sample_maximum(s):
                seqs = slice(4 * s, 4 * s + 4)
                pairs = lambda v: v.rearrange("p (c a) n -> p c a n", a=2)
                for g in range(N_KV):
                    r = slice(64 * g, 64 * g + 64)
                    b0 = (4, 0)[g] + 2 * s
                    dve.wait_ge(sample_scored, 2 * s + g + 1)
                    src = ps[r, b0:b0 + 2, 0:2 * NKEY].rearrange("p c (a n) -> p c a n", a=2)
                    dst = pairs(s_s[r, seqs, :])
                    nc.vector.tensor_tensor(dst[:, :, :, 0:WINDOW], src[:, :, :, 0:WINDOW],
                                            bias_c[r, :].unsqueeze(1).unsqueeze(1).broadcast_to([64, 2, 2, WINDOW]), ALU.add)
                    ins = nc.vector.tensor_tensor(dst[:, :, :, WINDOW:NKEY], src[:, :, :, WINDOW:NKEY],
                                                  pairs(bias_n[r, seqs, :]), ALU.add)
                ins.then_inc(bias_added, 1)
                dve.wait_ge(bias_added, s + 1)
                own(nc.vector.tensor_reduce(neg_max[:, seqs], s_s[:, seqs, :], AX_X, ALU.max))
                nc.vector.tensor_scalar(neg_max[:, seqs], neg_max[:, seqs], sinks[:, N_HEADS:N_HEADS + 1], -1.0,
                                        ALU.max, ALU.mult).then_inc(sample_max, 1)

            def sample_normalise(s):
                seqs = slice(4 * s, 4 * s + 4)
                dve.wait_ge(sample_exp, s + 1)
                own(nc.vector.tensor_tensor(inv_den[:, seqs], row_sum[:, seqs], sink_exp[:, seqs], ALU.add))
                own(nc.vector.reciprocal(inv_den[:, seqs], inv_den[:, seqs]))
                nc.vector.tensor_tensor(s_s[:, seqs, :], s_s[:, seqs, :],
                                        inv_den[:, seqs].unsqueeze(2).broadcast_to([P, 4, NKEY]),
                                        ALU.mult).then_inc(sample_prob, 1)

            def rest_o(m):
                dve.wait_ge(o_hi_made, m + 1)
                t = slice(m * NT, m * NT + SEQ)
                nc.vector.tensor_tensor(act_lo[:, t], ps[:, 2 + m % 2, :], act_hi[:, t].bitcast(F32),
                                        ALU.subtract).then_inc(att_ready, 1)

            dve.wait_ge(first_hi_made, 1)
            nc.vector.tensor_tensor(w_lo[:, 0, 0:FIRST], raw[:, 0, 0:FIRST], w_hi[:, 0, 0:FIRST].bitcast(F32),
                                    ALU.subtract).then_inc(first_lo_made, 1)
            for m in range(KD):
                split_x(0, m, None)
                if m == 0:
                    dve.wait_ge(hi_made, 1)
                    nc.vector.tensor_tensor(w_lo[:, 0, FIRST:D_MODEL], raw[:, 0, FIRST:D_MODEL],
                                            w_hi[:, 0, FIRST:D_MODEL].bitcast(F32), ALU.subtract).then_inc(lo_made, 1)
            dve.wait_ge(first_sum_012, 1)
            for m in range(3, KD):
                dve.wait_ge(first_sq_made, m - 2)
                if m > 3:
                    dve.wait_ge(first_added, m - 3)
                nc.vector.tensor_tensor(ssum[:, :], first_sq[:, 0, :] if m == 3 else ssum[:, :], first_sq[:, m, :],
                                        ALU.add).then_inc(first_added, 1)
                if m == 3:
                    prep(1, 1, 1, KT[1])
            prep_next(0)
            invert(0)
            ffn(0, 1, 1)
            invert(1)
            recurrent()
            down(base["wout"], 2, 2, 1.0)
            invert(2)
            ffn(1, 3, 3)
            key_value()
            ffn(2, 5, 4)
            invert(4)
            attention()
            down(base["wo"], 6, 5, 1.0)
            invert(5)
            ffn(3, None, 6)
            dve.wait_ge(std_made, 7)
            for half in range(2):
                t = slice(HT * half, HT * (half + 1))
                nc.vector.reciprocal(rstd[:, t], std[:, t]).then_inc(rstd_made, 1)
                dve.wait_ge(rstd_made, 7 + half)
                for m in range(Y_DVE):
                    nc.vector.scalar_tensor_tensor(x[:, m, t], x[:, m, t], params[:, V_FIN, m:m + 1], rstd[:, t],
                                                   ALU.mult, ALU.mult).then_inc(y_out, 1)

        @block.gpsimd
        def _(pool):
            pool.dma_start(ident[:, :], A["ident"]).then_inc(misc_loaded, 16)
            pool.dma_start(sinks[:, :], A["sinks"]).then_inc(misc_loaded, 16)
            pool.dma_start(A["ck_out"], A["cache_k"][:, DEC_SEQ:, :]).then_inc(side_stored, 16)
            pool.dma_start(A["cv_out"], A["cache_v"][:, DEC_SEQ:, :]).then_inc(side_stored, 16)
            pool.dma_start(st_in, A["st_in"]).then_inc(state_loaded, 16)

            for m in range(3):
                pool.wait_ge(x_loaded[m], 16)
                nc.gpsimd.tensor_tensor(first_sq[:, m, :], x[:, m, :], x[:, m, :], ALU.mult).then_inc(pool_chain, 1)
            for m in (1, 2):
                pool.wait_ge(pool_chain, m + 2)
                nc.gpsimd.tensor_tensor(first_sq[:, 0, :], first_sq[:, 0, :], first_sq[:, m, :],
                                        ALU.add).then_inc(pool_chain if m == 1 else first_sum_012, 1)

            def save_conv(m):
                r = m % 2
                pool.wait_ge(dve_evac, evac(base["xr", m]))
                nc.gpsimd.tensor_copy(st_out[:, m, 1:1 + PRE], xe[:, r, SEQ:SEQ + PRE])
                nc.gpsimd.tensor_copy(
                    st_out[:, m, 1 + PRE + DEC_BATCH:].rearrange("p (b k) -> p b k", b=DEC_BATCH),
                    seg(xe[:, r, :], DEC_SEQ, PRE)).then_inc(conv_saved, 1)

            def save_h(m):
                pool.wait_ge(h_made, m + 1)
                last = SEQ + PRE + DEC_SEQ - 1
                nc.gpsimd.tensor_copy(st_out[:, m, 0:1], hh[:, m % 2, SEQ - 1:SEQ])
                nc.gpsimd.tensor_copy(
                    st_out[:, m, 1 + PRE:1 + PRE + DEC_BATCH],
                    hh[:, m % 2, last:last + SEG * (DEC_BATCH - 1) + 1:SEG]).then_inc(h_saved, 1)

            save_conv(0)
            save_conv(1)
            for n in range(KD // 2):
                if n + 1 < KD // 2:
                    save_conv(2 * n + 2)
                    save_conv(2 * n + 3)
                for m in (2 * n, 2 * n + 1):
                    pool.wait_ge(act_evac, 2 * m + 2)
                    pool.wait_ge(xc_made, m + 1)
                    nc.gpsimd.tensor_tensor(ii[:, m % 2, :], ii[:, m % 2, :], xc[:, m % 4, :],
                                            ALU.mult).then_inc(ix_made, 1)
                save_h(2 * n)
                save_h(2 * n + 1)
            pool.wait_ge(h_saved, KD)
            pool.wait_ge(conv_saved, KD)
            pool.dma_start(A["st_out"], st_out).then_inc(side_stored, 16)
            pool.wait_ge(dve_evac, evac(base["kv"]))
            for g in range(N_KV):
                ins = nc.gpsimd.tensor_copy(kdup[64 * (1 - g):64 * (1 - g) + 64, g, :], kdup[64 * g:64 * g + 64, g, :])
            ins.then_inc(k_dup_made, 1)
            pool.wait_ge(dve_evac, evac(base["kv"] + 1))
            keep = slice(SEQ - WINDOW, NT)
            for g in range(N_KV):
                pool.dma_start(A["k_new"][64 * g:64 * g + 64, :], kdup[64 * g:64 * g + 64, g, keep]).then_inc(side_stored, 16)
            pool.dma_start(A["v_new"], v_t[:, keep]).then_inc(side_stored, 16)
            pool.wait_ge(side_stored, 16 * 6)
            pool.wait_ge(v_turned, 1)
            pool.dma_start(dist, A["dist"]).then_inc(att_loaded, 16)
            pool.dma_start(bias_c, A["bias_c"]).then_inc(att_loaded, 16)
            pool.dma_start(bias_n, A["bias_n"]).then_inc(att_loaded, 16)
            pool.dma_start(kc, A["k_cT"]).then_inc(att_loaded, 16)
            pool.dma_start(vc, A["cache_v"].rearrange("b s n -> s b n")).then_inc(att_loaded, 16)

            pool.wait_ge(att_loaded, 16 * 5)
            pool.wait_ge(stat_sum, 5)
            pool.wait_ge(k_dup_made, 1)
            for h in range(N_HEADS):
                if h >= 2:
                    pool.wait_ge(max_made, h - 1)
                nc.gpsimd.tensor_scalar(alibi[:, h % 2, :], dist, 2.0 ** (-8.0 * (h + 1) / N_HEADS), None,
                                        ALU.mult).then_inc(alibi_made, 1)

            pool.wait_ge(x_scaled, KD - Y_DVE)
            for half in range(2):
                pool.wait_ge(rstd_made, 7 + half)
                t = slice(HT * half, HT * (half + 1))
                for m in range(Y_DVE, KD):
                    nc.gpsimd.tensor_tensor(x[:, m, t], x[:, m, t], rstd[:, t], ALU.mult).then_inc(y_out_pool, 1)


def kernel(**inputs):
    import numpy as np
    import concourse.bacc as bacc
    from concourse.bass_utils import run_bass_kernel_spmd

    a = {k: np.asarray(v) for k, v in inputs.items()}
    f32 = np.float32

    def chunks(w):
        k, n = w.shape
        return w.reshape(k // P, P, n // P, P).transpose(2, 1, 0, 3).reshape(n // P, P, k)

    gu, dn = [], []
    for l in range(2):
        for which in ("ffn1", "ffn2"):
            g = chunks(a[f"{which}_w_gu"][l]).reshape(2, FT, P, D_MODEL)
            gu.append(g.transpose(1, 0, 2, 3).reshape(2 * FT, P, D_MODEL))
            w = a[f"{which}_w_down"][l]
            for half in range(2):
                dn.append(chunks(w[half * HF * P:(half + 1) * HF * P]))
    w_in = chunks(a["rg_w_in"][0])
    ax = np.stack([a["rg_w_a"][0], a["rg_w_x"][0]])
    ax = ax.reshape(2, 4, 2, P, 2, P).transpose(1, 3, 4, 0, 2, 5).reshape(4, P, D_MODEL)
    rec = [w_in[KD:KD + 2]]
    for n in range(KD // 2):
        rec += [w_in[KD + 2 * n + 2:KD + 2 * n + 4], ax[n:n + 1], w_in[2 * n:2 * n + 2]]

    q, c = np.arange(P)[:, None], np.arange(2 * WINDOW)[None]
    diff = WINDOW + q - c
    dist = np.where((diff >= 0) & (diff < WINDOW), -diff, -1e33).astype(f32)
    head, t = np.arange(P)[:, None] // DEC_SEQ, np.arange(P)[:, None] % DEC_SEQ
    slope = np.exp2(-8.0 * (head + 1) / N_HEADS)
    s = np.arange(WINDOW)[None]
    bias_c = np.where(s > t, -slope * (WINDOW + t - s), -1e30).astype(f32)
    b, tk = np.arange(NS)[None] // DEC_SEQ, np.arange(NS)[None] % DEC_SEQ
    bias_n = np.stack([np.where((b == i) & (tk <= t), -slope * (t - tk), -1e30) for i in range(DEC_BATCH)],
                      axis=1).astype(f32)

    vecs = [a["ffn1_norm"][0], a["ffn1_norm"][1], a["mix_norm"][0], a["mix_norm"][1], a["ffn2_norm"][0],
            a["ffn2_norm"][1], a["kv_norm"], a["final_norm"], *a["rg_conv_w"][0], a["rg_conv_b"][0],
            a["rg_b_a"][0], a["rg_b_x"][0], a["rg_lambda"][0]]
    sinks = a["attn_sinks"][0]
    states = np.concatenate([a["state_rg_h"][0].T, a["state_rg_conv"][0].reshape(-1, D_MODEL).T], axis=1)
    arrays = {
        "xT": np.concatenate([a["x_prompt"][0], a["x_sample"].reshape(NS, D_MODEL)]).T.reshape(KD, P, NT),
        "params": np.stack(vecs).reshape(N_VEC, KD, P).transpose(2, 0, 1),
        "ones": np.ones((P, P), f32),
        "ident": np.eye(P, dtype=f32),
        "eps": np.full((P, 1), EPS, f32),
        "sinks": np.concatenate([np.broadcast_to(sinks, (P, N_HEADS)), np.repeat(sinks, DEC_SEQ)[:, None]], axis=1),
        "st_in": states.reshape(KD, P, -1).transpose(1, 0, 2),
        "w_gu": np.concatenate(gu),
        "w_dn": np.concatenate(dn),
        "w_rec": np.concatenate(rec),
        "w_out": chunks(a["rg_w_out"][0]),
        "w_kv": chunks(a["w_kv"]),
        "w_q": chunks(a["attn_w_q"][0]),
        "w_o": chunks(a["attn_w_o"][0]),
        "cache_k": a["cache_k"].reshape(DEC_BATCH, WINDOW, P),
        "cache_v": a["cache_v"].reshape(DEC_BATCH, WINDOW, P),
        "k_cT": a["cache_k"].reshape(DEC_BATCH, WINDOW, P).transpose(2, 0, 1),
        "dist": dist, "bias_c": bias_c, "bias_n": bias_n,
    }
    outs = {"yT": (KD, P, NT), "st_out": (P, KD, NSTATE), "k_new": (P, WINDOW + NS), "v_new": (P, WINDOW + NS),
            "ck_out": (DEC_BATCH, WINDOW - DEC_SEQ, P), "cv_out": (DEC_BATCH, WINDOW - DEC_SEQ, P)}

    nc = bacc.Bacc("TRN2", target_bir_lowering=False, num_devices=1)
    A = {}
    for name, v in arrays.items():
        arrays[name] = np.ascontiguousarray(v)
        A[name] = nc.dram_tensor(name, v.shape, F32, kind="ExternalInput").ap()
    for name, shape in outs.items():
        A[name] = nc.dram_tensor(name, shape, F32, kind="ExternalOutput").ap()
    build(nc, A)
    r = run_bass_kernel_spmd(nc, [arrays], core_ids=[0]).results[0]

    y = r["yT"].reshape(D_MODEL, NT).T
    st = r["st_out"].transpose(1, 0, 2).reshape(D_MODEL, NSTATE).T
    new = {k: r[f"{k}_new"].T.reshape(WINDOW + NS, N_KV, HEAD_DIM) for k in "kv"}
    cache = {k: r[f"c{k}_out"].reshape(DEC_BATCH, WINDOW - DEC_SEQ, N_KV, HEAD_DIM) for k in "kv"}
    rolled = {k: np.concatenate([cache[k], new[k][WINDOW:].reshape(DEC_BATCH, DEC_SEQ, N_KV, HEAD_DIM)], axis=1)
              for k in "kv"}
    c0, c1, c2 = 1, 1 + PRE, 1 + PRE + DEC_BATCH
    out = (y[None, :SEQ], y[SEQ:].reshape(DEC_BATCH, DEC_SEQ, D_MODEL),
           st[None, 0:c0], st[None, None, c0:c1], new["k"][None, :WINDOW], new["v"][None, :WINDOW],
           st[None, c1:c2], st[c2:].reshape(1, DEC_BATCH, PRE, D_MODEL), rolled["k"], rolled["v"])
    return tuple(np.ascontiguousarray(o) for o in out)
```
